# Optimizing a Trainium2 kernel written in Bass

```python
import math
import jax, jax.numpy as jnp
from jax import lax
import numpy as np

D_MODEL = 1024
BATCH = 1
SEQ = 256
DEPTH = 2
DEC_BATCH = 8
DEC_SEQ = 16
PAST_LEN = 512

CHUNK = 64
N_A_LAYERS = DEPTH // 2
N_B_LAYERS = DEPTH - N_A_LAYERS
RWKV_HEAD = 64
RWKV_HEADS = D_MODEL // RWKV_HEAD
DECAY_LORA = 64
AAA_LORA = 64
GATE_LORA = 128
GN_EPS = 64e-5
DIFF_HEADS = 8
DIFF_DH = D_MODEL // (2 * DIFF_HEADS)
ROT_DIM = DIFF_DH // 4
ROPE_THETA = 500000.0
Q_BLOCK = 128
SUBLN_EPS = 1e-5
PEER_HEADS = 8
PEER_KEYS = 128
PEER_EXPERTS = PEER_KEYS * PEER_KEYS
PEER_DKEY = 256
PEER_DHALF = PEER_DKEY // 2
PEER_TOPK = 16
PEER_ROWS = 64
DN_ALPHA = (2.0 * DEPTH) ** 0.25
DN_BETA = (8.0 * DEPTH) ** -0.25
LN_EPS = 1e-5

kernel_name = "yoco_rwkv7_diffattn_peer_stream_step"

F32 = jnp.float32

def layer_norm(x, g, b):
    xf = x.astype(F32)
    mu = jnp.mean(xf, -1, keepdims=True)
    var = jnp.mean(jnp.square(xf - mu), -1, keepdims=True)
    return ((xf - mu) * lax.rsqrt(var + LN_EPS) * g.astype(F32) + b.astype(F32)).astype(x.dtype)

def rwkv7_time_mix(x, shift_prev, wkv_prev, mu, w_rkv, w0, w1, w2, a0, a1, a2, g1, g2,
                   k_k, k_a, r_k, lnx_g, lnx_b, w_out):
    B, T, D = x.shape
    H, N = RWKV_HEADS, RWKV_HEAD
    x_prev = jnp.concatenate([shift_prev.astype(x.dtype), x[:, :-1]], axis=1)
    xx = x_prev - x
    xr, xk, xv, xw, xa, xg = (x + xx * mu[i] for i in range(6))
    r = xr @ w_rkv[0]
    k = xk @ w_rkv[1]
    v = xv @ w_rkv[2]
    logw = -jax.nn.softplus(-(w0 + jnp.tanh(xw @ w1) @ w2)) - 0.5
    a = jax.nn.sigmoid(a0 + (xa @ a1) @ a2)
    g = jax.nn.sigmoid(xg @ g1) @ g2
    hd = lambda t: t.reshape(B, T, H, N).astype(F32)
    kk = hd(k * k_k)
    kk = kk / jnp.maximum(jnp.sqrt(jnp.sum(kk * kk, -1, keepdims=True)), 1e-12)
    k = k * (1.0 + (a - 1.0) * k_a)
    rf, kf, vf, af = hd(r), hd(k), hd(v), hd(a)
    decay = jnp.exp(-jnp.exp(hd(logw)))

    def step(S, inp):
        r_t, d_t, k_t, v_t, kk_t, a_t = inp
        Skk = jnp.einsum('bhvk,bhk->bhv', S, kk_t)
        S = (S * d_t[:, :, None, :]
             - Skk[..., None] * (kk_t * a_t)[:, :, None, :]
             + v_t[..., None] * k_t[:, :, None, :])
        y_t = jnp.einsum('bhvk,bhk->bhv', S, r_t)
        return S, y_t

    seq = tuple(jnp.moveaxis(t, 1, 0) for t in (rf, decay, kf, vf, kk, af))
    S_final, y = lax.scan(step, wkv_prev.astype(F32), seq)
    y = jnp.moveaxis(y, 0, 1)
    ym = jnp.mean(y, -1, keepdims=True)
    yv = jnp.mean(jnp.square(y - ym), -1, keepdims=True)
    y = ((y - ym) * lax.rsqrt(yv + GN_EPS)).reshape(B, T, D) * lnx_g.astype(F32) + lnx_b.astype(F32)
    bonus = jnp.sum(rf * kf * r_k.astype(F32), -1, keepdims=True) * vf
    y = y + bonus.reshape(B, T, D)
    out = (y * g.astype(F32)).astype(x.dtype) @ w_out
    return out, x[:, -1:], S_final.astype(x.dtype)

def rope_partial(t, pos):
    half = ROT_DIM // 2
    inv = jnp.power(ROPE_THETA, -jnp.arange(half, dtype=F32) * 2.0 / ROT_DIM)
    ang = pos.astype(F32)[:, None] * inv[None, :]
    cos = jnp.cos(ang)[None, :, None, None, :]
    sin = jnp.sin(ang)[None, :, None, None, :]
    tr = t[..., :ROT_DIM].astype(F32)
    t1, t2 = tr[..., :half], tr[..., half:]
    rot = jnp.concatenate([t1 * cos - t2 * sin, t1 * sin + t2 * cos], -1)
    return jnp.concatenate([rot.astype(t.dtype), t[..., ROT_DIM:]], -1)

def shared_kv(x, w_kv, pos):
    B, T, _ = x.shape
    kv = x @ w_kv
    k = kv[..., :D_MODEL].reshape(B, T, DIFF_HEADS, 2, DIFF_DH)
    v = kv[..., D_MODEL:].reshape(B, T, DIFF_HEADS, 2 * DIFF_DH)
    return rope_partial(k, pos), v

def diff_core(q, kf, vf, lam, mask):
    s = jnp.einsum('bqhcd,bkhcd->bhcqk', q.astype(F32), kf) * (DIFF_DH ** -0.5)
    if mask is not None:
        s = jnp.where(mask[None, None, None], s, -jnp.inf)
    p = jax.nn.softmax(s, axis=-1)
    attn = p[:, :, 0] - lam * p[:, :, 1]
    return jnp.einsum('bhqk,bkhe->bqhe', attn, vf)

def diff_attention(x, k_all, v_all, pos, w_q, lam_params, subln_g, w_o, layer_idx, prompt_mode):
    B, T, _ = x.shape
    q = rope_partial((x @ w_q).reshape(B, T, DIFF_HEADS, 2, DIFF_DH), pos)
    lam_init = 0.8 - 0.6 * math.exp(-0.3 * layer_idx)
    lp = lam_params.astype(F32)
    lam = jnp.exp(jnp.sum(lp[0] * lp[1])) - jnp.exp(jnp.sum(lp[2] * lp[3])) + lam_init
    kf, vf = k_all.astype(F32), v_all.astype(F32)
    if prompt_mode:
        nb = T // Q_BLOCK
        qb = q.reshape(B, nb, Q_BLOCK, DIFF_HEADS, 2, DIFF_DH).transpose(1, 0, 2, 3, 4, 5)
        k_chunk = jnp.arange(kf.shape[1]) // CHUNK

        def block(args):
            qi, bi = args
            q_chunk = (bi * Q_BLOCK + jnp.arange(Q_BLOCK)) // CHUNK
            mask = k_chunk[None, :] <= q_chunk[:, None]
            return diff_core(qi, kf, vf, lam, mask)

        o = lax.map(block, (qb, jnp.arange(nb)))
        o = o.transpose(1, 0, 2, 3, 4).reshape(B, T, DIFF_HEADS, 2 * DIFF_DH)
    else:
        o = diff_core(q, kf, vf, lam, None)
    o = o * lax.rsqrt(jnp.mean(o * o, -1, keepdims=True) + SUBLN_EPS) * subln_g.astype(F32)
    o = o * (1.0 - lam_init)
    return o.reshape(B, T, D_MODEL).astype(x.dtype) @ w_o

def peer_rows(xr, w_query, sub_keys, expert_u, expert_v):
    n = xr.shape[0]
    q = (xr @ w_query).reshape(n, PEER_HEADS, 2, PEER_DHALF).astype(F32)
    s = jnp.einsum('nhcd,ckd->nhck', q, sub_keys.astype(F32))
    s1, i1 = lax.top_k(s[:, :, 0], PEER_TOPK)
    s2, i2 = lax.top_k(s[:, :, 1], PEER_TOPK)
    cand_s = (s1[..., :, None] + s2[..., None, :]).reshape(n, PEER_HEADS, PEER_TOPK * PEER_TOPK)
    cand_i = (i1[..., :, None] * PEER_KEYS + i2[..., None, :]).reshape(n, PEER_HEADS, PEER_TOPK * PEER_TOPK)
    top_s, top_pos = lax.top_k(cand_s, PEER_TOPK)
    eidx = jnp.take_along_axis(cand_i, top_pos, axis=-1)
    gate = jax.nn.softmax(top_s, axis=-1)
    u = expert_u[eidx].astype(F32)
    h = jax.nn.gelu(jnp.einsum('nhkd,nd->nhk', u, xr.astype(F32)), approximate=False)
    out = jnp.einsum('nhk,nhkd->nd', gate * h, expert_v[eidx].astype(F32))
    return out.astype(xr.dtype)

def peer_ffn(x, w_query, sub_keys, expert_u, expert_v):
    B, T, D = x.shape
    n = B * T
    nb = -(-n // PEER_ROWS)
    rows = jnp.pad(x.reshape(n, D), ((0, nb * PEER_ROWS - n), (0, 0)))
    out = lax.map(lambda r: peer_rows(r, w_query, sub_keys, expert_u, expert_v),
                  rows.reshape(nb, PEER_ROWS, D))
    return out.reshape(nb * PEER_ROWS, D)[:n].reshape(B, T, D)

def _trunk(x, pos, shift_prev, wkv_prev, past_k, past_v, W):
    new_shift, new_wkv = [], []
    k_all = v_all = k_new = v_new = None
    for l in range(DEPTH):
        if l < N_A_LAYERS:
            mix, sh, st = rwkv7_time_mix(
                x, shift_prev[l], wkv_prev[l], W['rwkv_mu'][l], W['rwkv_w_rkv'][l],
                W['rwkv_w0'][l], W['rwkv_w1'][l], W['rwkv_w2'][l],
                W['rwkv_a0'][l], W['rwkv_a1'][l], W['rwkv_a2'][l],
                W['rwkv_g1'][l], W['rwkv_g2'][l], W['rwkv_k_k'][l], W['rwkv_k_a'][l],
                W['rwkv_r_k'][l], W['rwkv_lnx_g'][l], W['rwkv_lnx_b'][l], W['rwkv_w_out'][l])
            new_shift.append(sh)
            new_wkv.append(st)
        else:
            if l == N_A_LAYERS:
                k_new, v_new = shared_kv(x, W['w_kv'], pos)
                if past_k is None:
                    k_all, v_all = k_new, v_new
                else:
                    k_all = jnp.concatenate([past_k.astype(k_new.dtype), k_new], axis=1)
                    v_all = jnp.concatenate([past_v.astype(v_new.dtype), v_new], axis=1)
            j = l - N_A_LAYERS
            mix = diff_attention(x, k_all, v_all, pos, W['diff_w_q'][j], W['diff_lambda'][j],
                                 W['diff_subln_g'][j], W['diff_w_o'][j], l, past_k is None)
        x = layer_norm(DN_ALPHA * x + mix, W['ln_mix_g'][l], W['ln_mix_b'][l])
        ffn = peer_ffn(x, W['peer_w_query'][l], W['peer_sub_keys'][l], W['peer_u'][l], W['peer_v'][l])
        x = layer_norm(DN_ALPHA * x + ffn, W['ln_ffn_g'][l], W['ln_ffn_b'][l])
    return x, jnp.stack(new_shift), jnp.stack(new_wkv), k_new, v_new

def setup_inputs(seed: int = 0) -> dict:
    key = jax.random.key(seed)
    ks = iter(jax.random.split(key, 64))
    D, H, N = D_MODEL, RWKV_HEADS, RWKV_HEAD
    A, Bn = N_A_LAYERS, N_B_LAYERS

    def nrm(shape, scale):
        return jax.random.normal(next(ks), shape, F32) * scale

    def uni(shape, lo, hi):
        return jax.random.uniform(next(ks), shape, F32, minval=lo, maxval=hi)

    return {
        'x_prompt': nrm((BATCH, SEQ, D), 1.0),
        'x_sample': nrm((DEC_BATCH, DEC_SEQ, D), 1.0),
        'state_wkv': nrm((A, DEC_BATCH, H, N, N), 0.1),
        'state_shift': nrm((A, DEC_BATCH, 1, D), 1.0),
        'cache_k': nrm((DEC_BATCH, PAST_LEN, DIFF_HEADS, 2, DIFF_DH), 1.0),
        'cache_v': nrm((DEC_BATCH, PAST_LEN, DIFF_HEADS, 2 * DIFF_DH), 1.0),
        'rwkv_mu': uni((A, 6, D), 0.0, 1.0),
        'rwkv_w_rkv': nrm((A, 3, D, D), D ** -0.5),
        'rwkv_w0': uni((A, D), -4.0, 1.0),
        'rwkv_w1': nrm((A, D, DECAY_LORA), D ** -0.5),
        'rwkv_w2': nrm((A, DECAY_LORA, D), 0.1 * DECAY_LORA ** -0.5),
        'rwkv_a0': nrm((A, D), 0.1),
        'rwkv_a1': nrm((A, D, AAA_LORA), D ** -0.5),
        'rwkv_a2': nrm((A, AAA_LORA, D), AAA_LORA ** -0.5),
        'rwkv_g1': nrm((A, D, GATE_LORA), D ** -0.5),
        'rwkv_g2': nrm((A, GATE_LORA, D), GATE_LORA ** -0.5),
        'rwkv_k_k': 0.85 + nrm((A, D), 0.05),
        'rwkv_k_a': 1.0 + nrm((A, D), 0.05),
        'rwkv_r_k': nrm((A, H, N), 0.1),
        'rwkv_lnx_g': 1.0 + nrm((A, D), 0.05),
        'rwkv_lnx_b': nrm((A, D), 0.02),
        'rwkv_w_out': nrm((A, D, D), D ** -0.5 * DN_BETA),
        'w_kv': nrm((D, 2 * D), D ** -0.5),
        'diff_w_q': nrm((Bn, D, D), D ** -0.5),
        'diff_lambda': nrm((Bn, 4, DIFF_DH), 0.1),
        'diff_subln_g': 1.0 + nrm((Bn, 2 * DIFF_DH), 0.05),
        'diff_w_o': nrm((Bn, D, D), D ** -0.5 * DN_BETA),
        'ln_mix_g': 1.0 + nrm((DEPTH, D), 0.05),
        'ln_mix_b': nrm((DEPTH, D), 0.02),
        'ln_ffn_g': 1.0 + nrm((DEPTH, D), 0.05),
        'ln_ffn_b': nrm((DEPTH, D), 0.02),
        'peer_w_query': nrm((DEPTH, D, PEER_HEADS * PEER_DKEY), D ** -0.5),
        'peer_sub_keys': nrm((DEPTH, 2, PEER_KEYS, PEER_DHALF), PEER_DHALF ** -0.5),
        'peer_u': nrm((DEPTH, PEER_EXPERTS, D), D ** -0.5),
        'peer_v': nrm((DEPTH, PEER_EXPERTS, D), DN_BETA * PEER_HEADS ** -0.5),
    }

def reference(x_prompt, x_sample, state_wkv, state_shift, cache_k, cache_v,
              rwkv_mu, rwkv_w_rkv, rwkv_w0, rwkv_w1, rwkv_w2, rwkv_a0, rwkv_a1, rwkv_a2,
              rwkv_g1, rwkv_g2, rwkv_k_k, rwkv_k_a, rwkv_r_k, rwkv_lnx_g, rwkv_lnx_b, rwkv_w_out,
              w_kv, diff_w_q, diff_lambda, diff_subln_g, diff_w_o,
              ln_mix_g, ln_mix_b, ln_ffn_g, ln_ffn_b,
              peer_w_query, peer_sub_keys, peer_u, peer_v):
    W = dict(rwkv_mu=rwkv_mu, rwkv_w_rkv=rwkv_w_rkv, rwkv_w0=rwkv_w0, rwkv_w1=rwkv_w1,
             rwkv_w2=rwkv_w2, rwkv_a0=rwkv_a0, rwkv_a1=rwkv_a1, rwkv_a2=rwkv_a2,
             rwkv_g1=rwkv_g1, rwkv_g2=rwkv_g2, rwkv_k_k=rwkv_k_k, rwkv_k_a=rwkv_k_a,
             rwkv_r_k=rwkv_r_k, rwkv_lnx_g=rwkv_lnx_g, rwkv_lnx_b=rwkv_lnx_b,
             rwkv_w_out=rwkv_w_out, w_kv=w_kv, diff_w_q=diff_w_q, diff_lambda=diff_lambda,
             diff_subln_g=diff_subln_g, diff_w_o=diff_w_o, ln_mix_g=ln_mix_g,
             ln_mix_b=ln_mix_b, ln_ffn_g=ln_ffn_g, ln_ffn_b=ln_ffn_b,
             peer_w_query=peer_w_query, peer_sub_keys=peer_sub_keys,
             peer_u=peer_u, peer_v=peer_v)
    Bp, Tp, D = x_prompt.shape
    _, Ts, _ = x_sample.shape
    pos_p = jnp.arange(Tp, dtype=jnp.int32)
    shift0 = jnp.zeros((N_A_LAYERS, Bp, 1, D), x_prompt.dtype)
    wkv0 = jnp.zeros((N_A_LAYERS, Bp, RWKV_HEADS, RWKV_HEAD, RWKV_HEAD), x_prompt.dtype)
    y_prompt, state_shift_prompt, state_wkv_prompt, cache_k_prompt, cache_v_prompt = _trunk(
        x_prompt, pos_p, shift0, wkv0, None, None, W)
    pos_s = PAST_LEN + jnp.arange(Ts, dtype=jnp.int32)
    y_sample, state_shift_sample, state_wkv_sample, cache_k_sample, cache_v_sample = _trunk(
        x_sample, pos_s, state_shift, state_wkv, cache_k, cache_v, W)
    return (y_prompt, y_sample, state_wkv_prompt, state_shift_prompt, cache_k_prompt, cache_v_prompt,
            state_wkv_sample, state_shift_sample, cache_k_sample, cache_v_sample)


_drawn_inputs = setup_inputs


def setup_inputs(seed=0):
    import zlib

    import numpy as np

    out = dict(_drawn_inputs(seed))
    spreads = {}
    factors = {'rwkv_w1': 7.277,
     'rwkv_w2': 6.628,
     'rwkv_lnx_g': 4.203,
     'rwkv_lnx_b': 6.274,
     'diff_subln_g': 4.469}
    for name, (base, spread) in spreads.items():
        noise = np.random.default_rng([zlib.crc32(name.encode()), seed]).standard_normal(out[name].shape)
        drawn = base * np.exp(spread * noise) if base else spread * noise
        out[name] = __import__('jax').numpy.asarray(drawn.astype(out[name].dtype))
    for name, factor in factors.items():
        out[name] = (out[name] * factor).astype(out[name].dtype)
    return out
```

```python
import math
from contextlib import ExitStack, contextmanager

import numpy as np

import concourse.bass as bass
from concourse import mybir

F32 = mybir.dt.float32
U32 = mybir.dt.uint32
I32 = mybir.dt.int32
ALU = mybir.AluOpType
ACT = mybir.ActivationFunctionType
AX = mybir.AxisListType

P = 128
D = 1024
KD = D // P
HALF = 512
SEQ = 256
DEC_BATCH, DEC_SEQ, PAST = 8, 16, 512
TILES = 3
TOK = TILES * P
L = 16
NCH = P // L
H, N = 16, 64
DH, DD = 8, 64
ROT = DD // 4
PH, PK, PTOP = 8, 128, 16
EXPERTS = PK * PK
SLOTS = PH * PTOP
ALPHA = (2.0 * 2) ** 0.25
LN_EPS, GN_EPS, SUBLN_EPS = 1e-5, 64e-5, 1e-5
DECAY_SCALE = -math.exp(-0.5)
LAM_INIT = 0.8 - 0.6 * math.exp(-0.3 * 1)
FAR = -1e30


def constant_layout():
    widths = [("ident", P), ("strict_incl", 2 * P), ("lower", P), ("block", P), ("chunk", NCH), ("first", NCH),
              ("causal", 3 * P), ("own_stream", 240), ("iota", PTOP), ("cos", TILES * ROT // 2),
              ("sin", TILES * ROT // 2)]
    at, where = 0, {}
    for name, w in widths:
        where[name] = (at, at + w)
        at += w
    return where, at


def shape_constants():
    where, width = constant_layout()
    c = np.zeros((P, width), np.float32)
    row, col = np.arange(P)[:, None], np.arange(P)[None, :]
    same = row // L == col // L

    def put(name, value):
        c[:, where[name][0]:where[name][1]] = value

    put("ident", row == col)
    put("strict_incl", np.concatenate([same & (row < col), same & (row <= col)], 1))
    put("lower", same & (col < row))
    put("block", same)
    put("chunk", row // L == np.arange(NCH)[None, :])
    put("first", row == L * np.arange(NCH)[None, :])
    causal = np.where((row < 64) & (col >= 64), FAR, 0.0)
    put("causal", np.concatenate([causal, np.zeros((P, P)), causal], 1))
    strip = np.full((P, 240), FAR)
    strip[:, 112:128] = 0.0
    put("own_stream", strip)
    put("iota", np.broadcast_to(np.arange(PTOP), (P, PTOP)))
    half = ROT // 2
    inv = np.power(np.float32(500000.0), -np.arange(half, dtype=np.float32) * np.float32(2.0) / np.float32(ROT))
    pos = np.stack([np.arange(P), P + np.arange(P), PAST + np.arange(P) % DEC_SEQ]).astype(np.float32)
    ang = (pos[:, :, None] * inv.astype(np.float32)).astype(np.float32)
    put("cos", np.cos(ang).astype(np.float32).transpose(1, 0, 2).reshape(P, -1))
    put("sin", np.sin(ang).astype(np.float32).transpose(1, 0, 2).reshape(P, -1))
    return c


class Signal:

    def __init__(self, ctx, nc, name):
        self.sem = ctx.enter_context(nc.semaphore(name))
        self.base = 0
        self.made = 0

    def by(self, n=1):
        self.made += n
        return self.sem, n

    def at(self, n):
        return self.sem, self.base + n

    def last(self):
        return self.sem, self.base + self.made

    def new_stage(self):
        self.base += self.made
        self.made = 0


class Core:

    def __init__(self, nc, ctx):
        self.nc, self.ctx = nc, ctx
        self.signals = {}

    def sig(self, name):
        if name not in self.signals:
            self.signals[name] = Signal(self.ctx, self.nc, name)
        return self.signals[name]

    def end_stage(self):
        for s in self.signals.values():
            s.new_stage()

    def const(self, name):
        a, b = self.where[name]
        return self.constants[:, a:b]


@contextmanager
def turns(i, times, counted=(), own=None, per=0):
    before = [s.made for s in counted]
    if own is not None:
        base, made = own.base, own.made
        own.base, own.made = base + made + i * per, 0
    yield
    if own is not None:
        assert own.made == per, own.made
        own.base, own.made = base, made + per * times
    for s, n in zip(counted, before):
        s.made = n + (s.made - n) * times


def in_order(eng, steps):

    def own(ins):
        ins.then_inc(*steps.by())
        eng.wait_ge(*steps.last())

    return own


def row_tile(x_prompt, x_sample, t):
    if t < 2:
        return x_prompt[0, t * P:(t + 1) * P, :]
    return x_sample.rearrange("b s d -> (b s) d")


def by_chunk(w):
    return w.rearrange("(k p) n -> p k n", p=P)


def rwkv_projections(core, io, buf):
    nc = core.nc
    ident = core.const("ident")
    with ExitStack() as ctx:
        def sb(name, shape, dt=F32):
            return ctx.enter_context(nc.sbuf_tensor(name, shape, dt))

        x_tok = sb("x_rows", [P, TILES, D])
        shift_rows = sb("shift_rows", [DEC_BATCH, D])
        mu_rows = sb("mu_rows", [6 * KD, P])
        mu_cols = sb("mu_cols", [P, 6 * KD])
        xT = sb("xT", [P, KD, TOK + DEC_BATCH])
        dxT = sb("dxT", [P, KD, TOK])
        mixed = sb("mixed", [P, 2, KD, TOK])
        RING = 7
        w_ring = sb("w_ring", [P, RING, D])
        lora_in = {"w": sb("w1_sb", [P, KD, 64]), "a": sb("a1_sb", [P, KD, 64]), "g": sb("g1_sb", [P, KD, P])}
        lora_out = {"w": sb("w2_sb", [64, D]), "a": sb("a2_sb", [64, D]), "g": sb("g2_sb", [P, D])}
        lora_bias = {"w": sb("w0_sb", [P, D]), "a": sb("a0_sb", [P, D])}
        hidden = sb("hidden", [P, TOK])
        acc = ctx.enter_context(nc.psum_tensor("acc", [P, 6, HALF], F32))
        aux = ctx.enter_context(nc.psum_tensor("aux", [P, 2, HALF], F32))

        rows_in, xT_psum, xT_done = core.sig("rows_in"), core.sig("rows_psum"), core.sig("rows_copied")
        mu_psum, mu_done = core.sig("mu_psum"), core.sig("mu_done")
        mixed_done, mixed_used = core.sig("mixed_done"), core.sig("mixed_used")
        w_in = [core.sig(f"loaded{i}") for i in range(RING)]
        w_used, acc_full = core.sig("w_used"), core.sig("acc_full")
        free_by = {m: core.sig("acc_free_dve" if m in "wa" else "acc_free_act") for m in "rkvwag"}
        lora_w_in, hid_psum, hid_done = core.sig("lora_w_in"), core.sig("hid_psum"), core.sig("hid_done")
        dve_steps, act_steps = core.sig("dve_steps"), core.sig("act_steps")
        shift_out, spilled = core.sig("shift_out"), core.sig("spilled")

        PLAN = [("r", 0), ("k", 1), ("v", 2), ("w", 3), ("a", 4), ("g", 5)]
        into = {"r": buf["r"], "k": buf["k"], "v": buf["v"], "w": buf["z"], "a": buf["a"], "g": buf["g"]}

        def bank_free(eng, j, b):
            if j > 0:
                m = PLAN[j - 1][0]
                before = sum(free_by[q] is free_by[m] for q, _ in PLAN[:j - 1])
                eng.wait_ge(*free_by[m].at(6 * before + b + 1))

        with nc.Block() as block:
            @block.sync
            def _(sp):
                sp.dma_start(core.constants[:], io["constants"]).then_inc(*rows_in.by(16))
                for t in range(TILES):
                    sp.dma_start(x_tok[:, t, :], row_tile(io["x_prompt"], io["x_sample"], t)).then_inc(*rows_in.by(16))
                sp.dma_start(shift_rows[:], io["state_shift"].rearrange("a b c d -> (a b c) d")).then_inc(*rows_in.by(16))
                sp.dma_start(mu_rows[:], io["rwkv_mu"].rearrange("a i (k p) -> (a i k) p", p=P)).then_inc(*rows_in.by(16))
                n = 0
                for i in range(3):
                    for k in range(KD):
                        if n >= RING:
                            sp.wait_ge(*w_used.at(n - RING + 1))
                        sp.dma_start(w_ring[:, n % RING, :], io["rwkv_w_rkv"][0, i, k * P:(k + 1) * P, :]).then_inc(*w_in[n % RING].by(16))
                        n += 1

            @block.gpsimd
            def _(pool):
                for m, (w1, w2) in {"w": ("rwkv_w1", "rwkv_w2"), "a": ("rwkv_a1", "rwkv_a2"), "g": ("rwkv_g1", "rwkv_g2")}.items():
                    pool.dma_start(lora_in[m][:], by_chunk(io[w1][0])).then_inc(*lora_w_in.by(16))
                    pool.dma_start(lora_out[m][:], io[w2][0]).then_inc(*lora_w_in.by(16))
                for m, w0 in {"w": "rwkv_w0", "a": "rwkv_a0"}.items():
                    pool.dma_start(lora_bias[m][:], io[w0].broadcast_to([P, D])).then_inc(*lora_w_in.by(16))
                pool.dma_start(io["shift_p"].rearrange("a b c d -> (a b c) d"), io["x_prompt"][0, SEQ - 1:SEQ, :]).then_inc(*shift_out.by(16))
                pool.dma_start(io["shift_s"].rearrange("a b c d -> (a b c) d"), io["x_sample"][:, DEC_SEQ - 1, :]).then_inc(*shift_out.by(16))
                for j, (m, _) in enumerate(PLAN):
                    before = sum(free_by[q] is free_by[m] for q, _ in PLAN[:j])
                    pool.wait_ge(*free_by[m].at(6 * (before + 1)))
                    pool.dma_start(core.spill[m].rearrange("t p d -> p t d"), into[m][:]).then_inc(*spilled.by(16))
                pool.wait_ge(*spilled.at(16 * 6))
                pool.wait_ge(*shift_out.at(32))

            @block.tensor
            def _(pe):
                pe.wait_ge(*rows_in.at(96))
                pe.transpose(acc[:, 0, 0:6 * KD], mu_rows[:], ident[0:6 * KD, 0:6 * KD]).then_inc(*mu_psum.by())
                for k in range(KD):
                    if k >= 2:
                        pe.wait_ge(*xT_done.at(k - 1))
                    for t in range(TILES):
                        pe.transpose(aux[:, k % 2, t * P:(t + 1) * P], x_tok[:, t, k * P:(k + 1) * P], ident)
                    pe.transpose(aux[:, k % 2, TOK:TOK + DEC_BATCH], shift_rows[:, k * P:(k + 1) * P],
                                 ident[0:DEC_BATCH, 0:DEC_BATCH]).then_inc(*xT_psum.by())
                n = 0
                pe.wait_ge(*mu_done.at(1))
                for j, (m, _) in enumerate(PLAN):
                    pe.wait_ge(*mixed_done.at(j + 1))
                    xm = mixed[:, j % 2]
                    if j < 3:
                        for k in range(KD):
                            pe.wait_ge(*w_in[n % RING].at(16 * (n // RING + 1)))
                            for t in range(TILES):
                                for h in range(2):
                                    if k == 0:
                                        bank_free(pe, j, 2 * t + h)
                                    mm = pe.matmul(acc[:, 2 * t + h, :], xm[:, k, t * P:(t + 1) * P],
                                                   w_ring[:, n % RING, h * HALF:(h + 1) * HALF],
                                                   start=(k == 0), stop=(k == KD - 1))
                                    if k == KD - 1 and (t, h) != (TILES - 1, 1):
                                        mm.then_inc(*acc_full.by())
                            mm.then_inc(*(w_used.by() if k < KD - 1 else acc_full.by()))
                            n += 1
                        pe.wait_ge(*acc_full.at(6 * (j + 1)))
                        pe.sem_inc(*w_used.by())
                        pe.sem_inc(*mixed_used.by())
                    else:
                        if j == 3:
                            pe.wait_ge(*lora_w_in.at(16 * 8))
                        r = 64 if m != "g" else P
                        for k in range(KD):
                            mm = pe.matmul(aux[0:r, j % 2, 0:TOK], lora_in[m][:, k, :], xm[:, k, :],
                                           start=(k == 0), stop=(k == KD - 1))
                        mm.then_inc(*hid_psum.by())
                        pe.wait_ge(*hid_done.at(j - 2))
                        pe.sem_inc(*mixed_used.by())
                        for t in range(TILES):
                            for h in range(2):
                                bank_free(pe, j, 2 * t + h)
                                pe.matmul(acc[:, 2 * t + h, :], hidden[0:r, t * P:(t + 1) * P],
                                          lora_out[m][:, h * HALF:(h + 1) * HALF]).then_inc(*acc_full.by())

            @block.scalar
            def _(act):
                for k in range(KD):
                    act.wait_ge(*xT_psum.at(k + 1))
                    act.copy(xT[:, k, :], aux[:, k % 2, 0:TOK + DEC_BATCH]).then_inc(*xT_done.by())
                for j, (m, _) in enumerate(PLAN):
                    if j >= 3:
                        r = 64 if m != "g" else P
                        act.wait_ge(*hid_psum.at(j - 2))
                        if j > 3:
                            act.wait_ge(*acc_full.at(6 * j))
                        act.activation(hidden[0:r, :], aux[0:r, j % 2, 0:TOK],
                                       {"w": ACT.Tanh, "a": ACT.Copy, "g": ACT.Sigmoid}[m]).then_inc(*hid_done.by())
                    if m in "rkvg":
                        for b in range(6):
                            act.wait_ge(*acc_full.at(6 * j + b + 1))
                            act.copy(into[m][:, b // 2, (b % 2) * HALF:(b % 2 + 1) * HALF],
                                     acc[:, b, :]).then_inc(*free_by[m].by())

            @block.vector
            def _(dve):
                own = in_order(dve, dve_steps)
                dve.wait_ge(*mu_psum.at(1))
                own(dve.tensor_copy(mu_cols[:], acc[:, 0, 0:6 * KD]))
                dve.sem_inc(*mu_done.by())
                dve.wait_ge(*xT_done.at(KD))
                s_cur = xT[:, :, SEQ:TOK].rearrange("p k (b s) -> p k b s", s=DEC_SEQ)
                s_dx = dxT[:, :, SEQ:TOK].rearrange("p k (b s) -> p k b s", s=DEC_SEQ)
                dve.tensor_tensor(dxT[:, :, 1:SEQ], xT[:, :, 0:SEQ - 1], xT[:, :, 1:SEQ], ALU.subtract)
                dve.tensor_scalar(dxT[:, :, 0:1], xT[:, :, 0:1], -1.0, None, ALU.mult)
                for b in range(DEC_BATCH):
                    dve.tensor_tensor(s_dx[:, :, b, 1:], s_cur[:, :, b, :DEC_SEQ - 1], s_cur[:, :, b, 1:], ALU.subtract)
                own(dve.tensor_tensor(s_dx[:, :, :, 0], xT[:, :, TOK:], s_cur[:, :, :, 0], ALU.subtract))
                for j, (m, i) in enumerate(PLAN):
                    if j >= 2:
                        dve.wait_ge(*mixed_used.at(j - 1))
                    for k in range(KD):
                        ins = dve.scalar_tensor_tensor(mixed[:, j % 2, k, :], dxT[:, k, :],
                                                       mu_cols[:, i * KD + k:i * KD + k + 1],
                                                       xT[:, k, 0:TOK], ALU.mult, ALU.add)
                    ins.then_inc(*mixed_done.by())
                    if j >= 1 and PLAN[j - 1][0] in "wa":
                        if j == 4:
                            dve.wait_ge(*lora_w_in.at(16 * 8))
                        for b in range(6):
                            dve.wait_ge(*acc_full.at(6 * (j - 1) + b + 1))
                            q = PLAN[j - 1][0]
                            dve.tensor_tensor(into[q][:, b // 2, (b % 2) * HALF:(b % 2 + 1) * HALF], acc[:, b, :],
                                              lora_bias[q][:, (b % 2) * HALF:(b % 2 + 1) * HALF],
                                              ALU.add).then_inc(*free_by[q].by())

        core.end_stage()


def wkv_operands(core, io, buf, w, t):
    nc = core.nc
    r, k, v, z, a = (buf[n][:] for n in "rkvza")
    heads = lambda x: x.rearrange("p (h n) -> p h n", n=N)
    with ExitStack() as ctx:
        def sb(name, shape, dt=F32):
            return ctx.enter_context(nc.sbuf_tensor(f"{name}_{t}", shape, dt))

        kk, kka, tmp = sb("kk", [P, D]), sb("kka", [P, D]), sb("tmp", [P, D])
        e_incl, e_neg, e_excl = sb("e_incl", [P, D]), sb("e_neg", [P, D]), sb("e_excl", [P, D])
        norm2, rnorm, bonus_dot = sb("norm2", [P, H]), sb("rnorm", [P, H]), sb("bonus_dot", [P, H])
        run = ctx.enter_context(nc.psum_tensor(f"run_{t}", [P, D], F32))
        end = ctx.enter_context(nc.psum_tensor(f"end_{t}", [P, D], F32))
        vec = {n: sb(n, [P, D]) for n in ("k_k", "k_a", "r_k")}
        loaded = "zakrvg"
        proj_in = [core.sig(f"loaded{i}") for i in range(6)]
        vec_in, gates, logd = core.sig("vectors_in"), core.sig("gates"), core.sig("logd")
        sums, norms, rnorms = core.sig("sums"), core.sig("norms"), core.sig("rnorms")
        excl_arg, exps, dve_steps = core.sig("excl_arg"), core.sig("exps"), core.sig("dve_steps")

        with nc.Block() as block:
            @block.sync
            def _(sp):
                for i, n in enumerate(loaded):
                    sp.dma_start(buf[n][:], core.spill["w" if n == "z" else n][t]).then_inc(*proj_in[i].by(16))
                for name in ("k_k", "k_a"):
                    sp.dma_start(vec[name][:], io["rwkv_" + name].broadcast_to([P, D])).then_inc(*vec_in.by(16))
                sp.dma_start(vec["r_k"][:], io["rwkv_r_k"].rearrange("a h n -> a (h n)").broadcast_to([P, D])).then_inc(*vec_in.by(16))
                sp.wait_ge(*proj_in[loaded.index("g")].at(16))

            @block.scalar
            def _(act):
                act.wait_ge(*proj_in[0].at(16))
                act.activation(z, z, ACT.Sigmoid).then_inc(*gates.by())
                act.wait_ge(*proj_in[1].at(16))
                act.activation(a, a, ACT.Sigmoid).then_inc(*gates.by())
                act.wait_ge(*norms.at(1))
                act.activation(rnorm[:], norm2[:], ACT.Sqrt).then_inc(*rnorms.by())
                act.wait_ge(*sums.at(2))
                act.activation(e_incl[:], run[:], ACT.Exp).then_inc(*exps.by())
                act.activation(e_neg[:], run[:], ACT.Exp, scale=-1.0).then_inc(*exps.by())
                act.activation(w["e_end"][:], end[:], ACT.Exp).then_inc(*exps.by())
                act.wait_ge(*excl_arg.at(1))
                act.activation(e_excl[:], e_excl[:], ACT.Exp).then_inc(*exps.by())

            @block.tensor
            def _(pe):
                pe.wait_ge(*logd.at(1))
                _, incl = core.const("strict_incl")[:, 0:P], core.const("strict_incl")[:, P:]
                for out, ones in ((run, incl), (end, core.const("block"))):
                    for h in range(2):
                        mm = pe.matmul(out[:, h * HALF:(h + 1) * HALF], ones, z[:, h * HALF:(h + 1) * HALF])
                    mm.then_inc(*sums.by())

            @block.vector
            def _(dve):
                own = in_order(dve, dve_steps)
                dve.wait_ge(*gates.at(1))
                own(dve.tensor_scalar(z, z, DECAY_SCALE, None, ALU.mult))
                dve.sem_inc(*logd.by())
                dve.wait_ge(*vec_in.at(48))
                dve.wait_ge(*proj_in[2].at(16))
                own(dve.tensor_tensor(kk[:], k, vec["k_k"][:], ALU.mult))
                own(dve.tensor_tensor(tmp[:], kk[:], kk[:], ALU.mult))
                own(dve.tensor_reduce(norm2[:], heads(tmp[:]), AX.X, ALU.add))
                own(dve.tensor_scalar(norm2[:], norm2[:], 1e-24, None, ALU.max))
                own(dve.reciprocal(norm2[:], norm2[:]))
                dve.sem_inc(*norms.by())
                dve.wait_ge(*gates.at(2))
                own(dve.scalar_tensor_tensor(tmp[:], a, -1.0, vec["k_a"][:], ALU.add, ALU.mult))
                own(dve.scalar_tensor_tensor(k, tmp[:], 1.0, k, ALU.add, ALU.mult))
                dve.wait_ge(*proj_in[3].at(16))
                own(dve.tensor_tensor(tmp[:], r, k, ALU.mult))
                own(dve.tensor_tensor(tmp[:], tmp[:], vec["r_k"][:], ALU.mult))
                own(dve.tensor_reduce(bonus_dot[:], heads(tmp[:]), AX.X, ALU.add))
                dve.wait_ge(*proj_in[4].at(16))
                dve.tensor_tensor(heads(w["bonus"][:]), heads(v), bonus_dot[:].unsqueeze(2).broadcast_to([P, H, N]), ALU.mult)
                dve.wait_ge(*rnorms.at(1))
                own(dve.tensor_tensor(heads(kk[:]), heads(kk[:]), rnorm[:].unsqueeze(2).broadcast_to([P, H, N]), ALU.mult))
                own(dve.tensor_tensor(kka[:], kk[:], a, ALU.mult))
                dve.wait_ge(*exps.at(2))
                own(dve.tensor_tensor(e_excl[:], run[:], z, ALU.subtract))
                dve.sem_inc(*excl_arg.by())
                dve.wait_ge(*exps.at(3))
                dve.tensor_tensor(r, r, e_incl[:], ALU.mult)
                own(dve.scalar_tensor_tensor(w["B"][:], kka[:], -1.0, e_neg[:], ALU.mult, ALU.mult))
                own(dve.tensor_tensor(k, k, e_neg[:], ALU.mult))
                dve.tensor_tensor(w["B_end"][:], w["B"][:], w["e_end"][:], ALU.mult)
                dve.tensor_tensor(w["K_end"][:], k, w["e_end"][:], ALU.mult)
                dve.wait_ge(*exps.at(4))
                own(dve.tensor_tensor(a, kk[:], e_excl[:], ALU.mult))
        core.end_stage()


def wkv_chunks(core, buf, w, t):
    nc = core.nc
    GH = 4
    ident = core.const("ident")
    token = {"A": buf["a"], "R": buf["r"], "B": w["B"], "K": buf["k"]}
    v = buf["v"]
    with ExitStack() as ctx:
        def sb(name, shape, dt=F32):
            return ctx.enter_context(nc.sbuf_tensor(f"{name}_{t}", shape, dt))

        feat = sb("feat", [N, GH, 4, P])
        by_b = sb("by_b", [P, GH, 2 * P])
        by_k = sb("by_k", [P, GH, 2 * P])
        m1 = sb("m1", [P, GH, P])
        m2, m2t, m4, m4t, m8t = (sb(n, [P, GH, P]) for n in ("m2", "m2t", "m4", "m4t", "m8t"))
        x = sb("x", [P, 2, GH, 2 * N])
        B_by_chunk, K_by_chunk = sb("B_by_chunk", [P, GH, NCH, N]), sb("K_by_chunk", [P, GH, NCH, N])
        p_end = sb("p_end", [N, GH, NCH])
        decay_diag = sb("decay_diag", [N, GH, NCH, N])
        bank = [ctx.enter_context(nc.psum_tensor(f"bank{i}_{t}", [P, HALF], F32)) for i in range(8)]

        tp, feat_done = core.sig("tp"), core.sig("feat_done")
        gram, gram_done = core.sig("gram"), core.sig("gram_done")
        nv, x_done, pw, pw_done = core.sig("nv"), core.sig("x_done"), core.sig("pw"), core.sig("pw_done")
        xp, q1, q1_done, y2, y2_done = core.sig("xp"), core.sig("q1"), core.sig("q1_done"), core.sig("y2"), core.sig("y2_done")
        pend_done, diag_done, exp_done = core.sig("pend_done"), core.sig("diag_done"), core.sig("exp_done")
        fp, fp_done, gp, gp_done = core.sig("fp"), core.sig("fp_done"), core.sig("gp"), core.sig("gp_done")
        a_copied = core.sig("a_copied")
        NG = H // GH
        quad = lambda b, n: b[:, 0:GH * n].rearrange("p (h n) -> p h n", h=GH)

        with nc.Block() as block:
            @block.tensor
            def _(pe):
                for g in range(NG):
                    for h in range(GH):
                        hc = slice((g * GH + h) * N, (g * GH + h + 1) * N)
                        if g > 0:
                            if h == 0:
                                pe.wait_ge(*gp_done.at(GH * g))
                                pe.wait_ge(*fp_done.at(GH * g))
                                pe.wait_ge(*q1_done.at(g))
                                pe.wait_ge(*x_done.at(5 * g))
                        for i, n in enumerate("ARBK"):
                            mm = pe.transpose(bank[h][0:N, i * P:(i + 1) * P], token[n][:, hc], ident)
                        mm.then_inc(*tp.by())
                    for h in range(GH):
                        pe.wait_ge(*feat_done.at(GH * g + h + 1))
                        if g > 0 and h == 0:
                            pe.wait_ge(*y2_done.at(g))
                        ar = feat[:, h, 0:2, :].rearrange("k i t -> k (i t)")
                        pe.matmul(bank[4 + h // 2][:, (h % 2) * 2 * P:(h % 2 + 1) * 2 * P], feat[:, h, 2, :], ar)
                        mm = pe.matmul(bank[6 + h // 2][:, (h % 2) * 2 * P:(h % 2 + 1) * 2 * P], feat[:, h, 3, :], ar)
                        if h % 2:
                            mm.then_inc(*gram.by())
                    for h in range(GH):
                        mm = pe.matmul(bank[0][:, h * P:(h + 1) * P], feat[:, h, 0, :], feat[:, h, 2, :])
                    mm.then_inc(*gram.by())
                    pe.wait_ge(*gram_done.at(5 * g + 5))
                    for h in range(GH):
                        hc = slice((g * GH + h) * N, (g * GH + h + 1) * N)
                        pe.matmul(bank[1][:, h * N:(h + 1) * N], by_k[:, h, 0:P], v[:, hc])
                        mm = pe.matmul(bank[1][0:N, GH * N + h * NCH:GH * N + (h + 1) * NCH], w["e_end"][:, hc], core.const("first"))
                    mm.then_inc(*nv.by())
                    for h in range(GH):
                        mm = pe.matmul(bank[2][:, h * P:(h + 1) * P], m1[:, h, :], by_b[:, h, 0:P])
                    mm.then_inc(*pw.by())
                    for h in range(GH):
                        mm = pe.matmul(bank[3][:, h * P:(h + 1) * P], by_b[:, h, 0:P], m1[:, h, :])
                    mm.then_inc(*pw.by())
                    pe.wait_ge(*x_done.at(5 * g + 1))
                    for h in range(GH):
                        mm = pe.matmul(bank[4][:, h * P:(h + 1) * P], by_b[:, h, 0:P], x[:, 0, h, :])
                    mm.then_inc(*xp.by())
                    pe.wait_ge(*pw_done.at(5 * g + 2))
                    for h in range(GH):
                        mm = pe.matmul(bank[5][:, h * P:(h + 1) * P], m2[:, h, :], m2t[:, h, :])
                    mm.then_inc(*pw.by())
                    for h in range(GH):
                        mm = pe.matmul(bank[6][:, h * P:(h + 1) * P], m2t[:, h, :], m2[:, h, :])
                    mm.then_inc(*pw.by())
                    pe.wait_ge(*x_done.at(5 * g + 2))
                    for h in range(GH):
                        mm = pe.matmul(bank[7][:, h * P:(h + 1) * P], m2t[:, h, :], x[:, 1, h, :])
                    mm.then_inc(*xp.by())
                    pe.wait_ge(*pw_done.at(5 * g + 4))
                    for h in range(GH):
                        mm = pe.matmul(bank[0][:, h * P:(h + 1) * P], m4[:, h, :], m4t[:, h, :])
                    mm.then_inc(*pw.by())
                    pe.wait_ge(*x_done.at(5 * g + 3))
                    for h in range(GH):
                        mm = pe.matmul(bank[1][:, h * P:(h + 1) * P], m4t[:, h, :], x[:, 0, h, :])
                    mm.then_inc(*xp.by())
                    pe.wait_ge(*pw_done.at(5 * g + 5))
                    pe.wait_ge(*x_done.at(5 * g + 4))
                    for h in range(GH):
                        mm = pe.matmul(bank[2][:, h * P:(h + 1) * P], m8t[:, h, :], x[:, 1, h, :])
                    mm.then_inc(*xp.by())
                    pe.wait_ge(*x_done.at(5 * g + 5))
                    for h in range(GH):
                        mm = pe.matmul(bank[3][0:N, h * P:(h + 1) * P], x[:, 0, h, 0:N], by_b[:, h, P:])
                    mm.then_inc(*q1.by())
                    for h in range(GH):
                        hc = slice((g * GH + h) * N, (g * GH + h + 1) * N)
                        pe.matmul(bank[4][0:N, h * P:(h + 1) * P], x[:, 0, h, N:], by_b[:, h, P:], start=True, stop=False)
                        mm = pe.matmul(bank[4][0:N, h * P:(h + 1) * P], v[:, hc], by_k[:, h, P:], start=False, stop=True)
                    mm.then_inc(*y2.by())
                    pe.wait_ge(*exp_done.at(2 * GH * (g + 1)))
                    pe.wait_ge(*diag_done.at(g + 1))
                    for h in range(GH):
                        hc = slice((g * GH + h) * N, (g * GH + h + 1) * N)
                        f, gg = bank[(5, 7)[h % 2]], bank[(6, 0)[h % 2]]
                        if h >= 2:
                            pe.wait_ge(*fp_done.at(GH * g + h - 1))
                            pe.wait_ge(*gp_done.at(GH * g + h - 1))
                        pe.matmul(f[0:N, :], x[:, 0, h, 0:N], B_by_chunk[:, h].rearrange("p c n -> p (c n)"), start=True, stop=False)
                        pe.matmul(f[0:N, :], ident[0:N, 0:N], decay_diag[:, h].rearrange("p c n -> p (c n)"), start=False, stop=True).then_inc(*fp.by())
                        for c in range(NCH):
                            pe.matmul(gg[0:N, c * N:(c + 1) * N], B_by_chunk[:, h, c, :], x[:, 0, h, N:], start=True, stop=False)
                            mm = pe.matmul(gg[0:N, c * N:(c + 1) * N], K_by_chunk[:, h, c, :], v[:, hc], start=False, stop=True)
                        mm.then_inc(*gp.by())

            @block.scalar
            def _(act):
                for g in range(NG):
                    for h in range(GH):
                        act.wait_ge(*tp.at(GH * g + h + 1))
                        if g > 0 and h == 0:
                            act.wait_ge(*q1_done.at(g))
                        act.copy(feat[:, h].rearrange("k i t -> k (i t)"), bank[h][0:N, :]).then_inc(*feat_done.by())
                    for i, (dst, b) in enumerate(((m2t, 2), (m2, 3), (m4t, 5), (m4, 6), (m8t, 0))):
                        act.wait_ge(*pw.at(5 * g + i + 1))
                        act.copy(dst[:], quad(bank[b], P)).then_inc(*pw_done.by())
                    act.wait_ge(*y2.at(g + 1))
                    act.copy(w["Y2t"][:, g * GH:(g + 1) * GH, :], quad(bank[4], P)[0:N]).then_inc(*y2_done.by())
                    for h in range(GH):
                        act.wait_ge(*fp.at(GH * g + h + 1))
                        act.copy(w["Ft"][:, :, g * GH + h, :], bank[(5, 7)[h % 2]][0:N, :].rearrange("k (c n) -> k c n", n=N)).then_inc(*fp_done.by())

            @block.vector
            def _(dve):
                both = core.const("strict_incl").unsqueeze(1).broadcast_to([P, 2, 2 * P])
                for g in range(NG):
                    for i in range(2):
                        dve.wait_ge(*gram.at(3 * g + i + 1))
                        if g > 0 and i == 0:
                            dve.wait_ge(*y2.at(g))
                        dve.tensor_tensor(by_b[:, 2 * i:2 * i + 2, :], bank[4 + i].rearrange("p (h s) -> p h s", h=2), both, ALU.mult).then_inc(*gram_done.by())
                        dve.tensor_tensor(by_k[:, 2 * i:2 * i + 2, :], bank[6 + i].rearrange("p (h s) -> p h s", h=2), both, ALU.mult).then_inc(*gram_done.by())
                    dve.wait_ge(*gram.at(3 * g + 3))
                    dve.tensor_tensor(m1[:], quad(bank[0], P), core.const("lower").unsqueeze(1).broadcast_to([P, GH, P]), ALU.mult).then_inc(*gram_done.by())
                    dve.wait_ge(*a_copied.at(g + 1))
                    dve.wait_ge(*nv.at(g + 1))
                    dve.tensor_copy(x[:, 0, :, N:], quad(bank[1], N)).then_inc(*x_done.by())
                    if g > 0:
                        dve.wait_ge(*diag_done.at(g))
                    dve.tensor_copy(p_end[:].rearrange("k h c -> k (h c)"), bank[1][0:N, GH * N:GH * (N + NCH)]).then_inc(*pend_done.by())
                    for i, b in enumerate((4, 7, 1, 2)):
                        dve.wait_ge(*xp.at(4 * g + i + 1))
                        dve.wait_ge(*x_done.at(5 * g + i + 1))
                        dve.tensor_tensor(x[:, (i + 1) % 2], quad(bank[b], P), x[:, i % 2], ALU.add).then_inc(*x_done.by())
                    dve.wait_ge(*q1.at(g + 1))
                    dve.tensor_tensor(w["Q1t"][:, g * GH:(g + 1) * GH, :], quad(bank[3], P)[0:N], feat[:, :, 1, :], ALU.add).then_inc(*q1_done.by())
                    for h in range(GH):
                        dve.wait_ge(*gp.at(GH * g + h + 1))
                        dve.tensor_copy(w["G"][:, 1:, g * GH + h, :], bank[(6, 0)[h % 2]][0:N, :].rearrange("k (c n) -> k c n", n=N)).then_inc(*gp_done.by())

            @block.gpsimd
            def _(pool):
                spread = core.const("chunk").unsqueeze(2).broadcast_to([P, NCH, N])
                for g in range(NG):
                    gc = slice(g * GH * N, (g + 1) * GH * N)
                    if g > 0:
                        pool.wait_ge(*gp.at(GH * g))
                    pool.tensor_copy(x[:, 0, :, 0:N], token["A"][:, gc].rearrange("p (h n) -> p h n", n=N)).then_inc(*a_copied.by())
                    for h in range(GH):
                        hc = slice((g * GH + h) * N, (g * GH + h + 1) * N)
                        for dst, src in ((B_by_chunk, w["B_end"]), (K_by_chunk, w["K_end"])):
                            pool.tensor_tensor(dst[:, h], src[:, hc].unsqueeze(1).broadcast_to([P, NCH, N]), spread, ALU.mult).then_inc(*exp_done.by())
                    pool.wait_ge(*pend_done.at(g + 1))
                    for h in range(GH):
                        ins = pool.tensor_tensor(decay_diag[:, h], ident[0:N, 0:N].unsqueeze(1).broadcast_to([N, NCH, N]),
                                                 p_end[:, h, :].unsqueeze(2).broadcast_to([N, NCH, N]), ALU.mult)
                    ins.then_inc(*diag_done.by())
        core.end_stage()


def wkv_states(core, io, buf, w, t):
    nc = core.nc
    ident = core.const("ident")
    G, Ft, carry = w["G"], w["Ft"], w["carry"]
    sample = t == 2
    St = w["start"] if sample else G
    pairs = lambda s: s.rearrange("(q r) v k -> (r v) q k", r=2)
    with ExitStack() as ctx:
        def sb(name, shape, dt=F32):
            return ctx.enter_context(nc.sbuf_tensor(f"{name}_{t}", shape, dt))

        natural = sb("natural", [P, 2 if not sample else DEC_BATCH, H // 2, N])
        Yt = sb("Yt", [N, H, P])
        bank = [ctx.enter_context(nc.psum_tensor(f"sbank{i}_{t}", [P, HALF], F32)) for i in range(8)]
        state_in, s_psum, s_done = core.sig("vectors_in"), core.sig("s_psum"), core.sig("s_done")
        step_psum, step_done = core.sig("step_psum"), core.sig("step_done")
        y_psum, y_sum, y_tok, y_tok_done = core.sig("rows_psum"), core.sig("rows_copied"), core.sig("y_tok"), core.sig("y_tok_done")
        fin_psum, fin_done, fin_out = core.sig("fin_psum"), core.sig("fin_done"), core.sig("fin_out")
        first = core.sig("first_state")

        with nc.Block() as block:
            if sample:
                @block.sync
                def _(sp):
                    for b in range(DEC_BATCH):
                        sp.dma_start(natural[:, b], pairs(io["state_wkv"][0, b])).then_inc(*state_in.by(16))
                    for b in range(DEC_BATCH):
                        sp.wait_ge(*fin_done.at(b + 1))
                        sp.dma_start(pairs(io["wkv_s"][0, b]), natural[:, b]).then_inc(*fin_out.by(16))
                    sp.wait_ge(*fin_out.at(16 * DEC_BATCH))
            elif t == 1:
                @block.sync
                def _(sp):
                    sp.wait_ge(*fin_done.at(1))
                    sp.dma_start(pairs(io["wkv_p"][0, 0]), natural[:, 0]).then_inc(*fin_out.by(16))
                    sp.wait_ge(*fin_out.at(16))

            @block.tensor
            def _(pe):
                def step(c, n):
                    for half in range(2):
                        for h in range(8 * half, 8 * half + 8):
                            mm = pe.matmul(bank[2 * (n % 2) + half][0:N, (h % 8) * N:(h % 8 + 1) * N], Ft[:, c, h, :], St[:, c, h, :])
                        mm.then_inc(*step_psum.by())

                if sample:
                    pe.wait_ge(*state_in.at(16 * DEC_BATCH))
                    for b in range(DEC_BATCH):
                        for half in range(2):
                            n = 2 * b + half
                            if n >= 4:
                                pe.wait_ge(*s_done.at(n - 3))
                            for q in range(4):
                                mm = pe.transpose(bank[4 + n % 4][0:N, q * P:(q + 1) * P], natural[:, b, 4 * half + q, :], ident)
                            mm.then_inc(*s_psum.by())
                    pe.wait_ge(*s_done.at(2 * DEC_BATCH))
                    for c in range(NCH):
                        if c >= 2:
                            pe.wait_ge(*step_done.at(2 * c - 2))
                        step(c, c)
                else:
                    pe.wait_ge(*first.at(1))
                    for c in range(NCH):
                        if c > 0:
                            pe.wait_ge(*step_done.at(2 * c))
                        step(c, c)
                pe.wait_ge(*step_done.at(2 * NCH))
                for q in range(4):
                    for h in range(4 * q, 4 * q + 4):
                        for c in range(NCH):
                            mm = pe.matmul(bank[q][0:N, (h % 4) * P + c * L:(h % 4) * P + (c + 1) * L], St[:, c, h, :], w["Q1t"][:, h, c * L:(c + 1) * L])
                    mm.then_inc(*y_psum.by())
                for half in range(2):
                    pe.wait_ge(*y_sum.at(2 * half + 2))
                    for h in range(8 * half, 8 * half + 8):
                        mm = pe.transpose(bank[4 + half][:, (h % 8) * N:(h % 8 + 1) * N], Yt[:, h, :], ident[0:N, 0:N])
                    mm.then_inc(*y_tok.by())
                if t >= 1:
                    for b in range(DEC_BATCH if sample else 1):
                        if b >= 2:
                            pe.wait_ge(*fin_done.at(b - 1))
                        src = G[:, b + 1] if sample else G[:, NCH]
                        for q in range(H // 2):
                            mm = pe.transpose(bank[6 + b % 2][:, q * N:(q + 1) * N], src[:, 2 * q:2 * q + 2, :].rearrange("k h v -> k (h v)"), ident[0:N, 0:N])
                        mm.then_inc(*fin_psum.by())

            @block.vector
            def _(dve):
                if t == 0:
                    dve.memset(St[:, 0], 0.0).then_inc(*first.by())
                elif t == 1:
                    dve.tensor_copy(St[:, 0], carry[:]).then_inc(*first.by())
                for c in range(NCH):
                    for half in range(2):
                        hs = slice(8 * half, 8 * half + 8)
                        dve.wait_ge(*step_psum.at(2 * c + half + 1))
                        dst = G[:, c + 1, hs, :]
                        dve.tensor_tensor(dst, bank[2 * (c % 2) + half][0:N, :].rearrange("k (h v) -> k h v", v=N), dst, ALU.add).then_inc(*step_done.by())
                if t == 0:
                    dve.wait_ge(*step_done.at(2 * NCH))
                    dve.tensor_copy(carry[:], G[:, NCH])
                for q in range(4):
                    dve.wait_ge(*y_psum.at(q + 1))
                    dve.tensor_tensor(Yt[:, 4 * q:4 * q + 4, :], bank[q][0:N, :].rearrange("k (h t) -> k h t", t=P), w["Y2t"][:, 4 * q:4 * q + 4, :], ALU.add).then_inc(*y_sum.by())

            @block.scalar
            def _(act):
                if sample:
                    for n in range(2 * DEC_BATCH):
                        act.wait_ge(*s_psum.at(n + 1))
                        act.copy(St[:, n // 2, 8 * (n % 2):8 * (n % 2) + 8, :], bank[4 + n % 4][0:N, :].rearrange("k (h v) -> k h v", v=N)).then_inc(*s_done.by())
                for half in range(2):
                    act.wait_ge(*y_tok.at(half + 1))
                    act.copy(w["y"][:, half * HALF:(half + 1) * HALF], bank[4 + half][:]).then_inc(*y_tok_done.by())
                if t >= 1:
                    for b in range(DEC_BATCH if sample else 1):
                        act.wait_ge(*fin_psum.at(b + 1))
                        act.copy(natural[:, b].rearrange("p q k -> p (q k)"), bank[6 + b % 2][:]).then_inc(*fin_done.by())
        core.end_stage()


def wkv_states_and_outputs(core, io, buf, w, t):
    with ExitStack() as ctx:
        if t == 2:
            w["start"] = ctx.enter_context(core.nc.sbuf_tensor("wkv_start", [N, NCH, H, N], F32))
        wkv_states(core, io, buf, w, t)
    wkv_outputs(core, io, buf, w, t)


def load_rows(core, io, gated):
    rows_back = core.sig("rows_back")
    with core.nc.Block() as block:
        @block.sync
        def _(sp):
            for t in range(TILES):
                sp.dma_start(core.x_tok[:, t, :], row_tile(io["x_prompt"], io["x_sample"], t)).then_inc(*rows_back.by(16))
            sp.dma_start(gated[:], core.spill["g"].rearrange("t p d -> p t d")).then_inc(*rows_back.by(16))
            sp.wait_ge(*rows_back.at(16 * (TILES + 1)))
    core.end_stage()


def wkv_outputs(core, io, buf, w, t):
    nc = core.nc
    y, gate = w["y"], buf["g"][:]
    heads = lambda x: x.rearrange("p (h n) -> p h n", n=N)
    wide = lambda x: x[:].unsqueeze(2).broadcast_to([P, H, N])
    with ExitStack() as ctx:
        def sb(name, shape, dt=F32):
            return ctx.enter_context(nc.sbuf_tensor(f"{name}_{t}", shape, dt))

        sq, mean, var, rstd = sb("sq", [P, D]), sb("mean", [P, H]), sb("var", [P, H]), sb("rstd", [P, H])
        lnx_g, lnx_b = sb("lnx_g", [P, D]), sb("lnx_b", [P, D])
        gated, gated_out = core.sig("gated"), core.sig("gated_out")
        lnx_in, var_done, rstd_done, dve_steps = core.sig("vectors_in"), core.sig("var_done"), core.sig("rstd_done"), core.sig("dve_steps")
        with nc.Block() as block:
            @block.sync
            def _(sp):
                sp.dma_start(lnx_g[:], io["rwkv_lnx_g"].broadcast_to([P, D])).then_inc(*lnx_in.by(16))
                sp.dma_start(lnx_b[:], io["rwkv_lnx_b"].broadcast_to([P, D])).then_inc(*lnx_in.by(16))
                sp.wait_ge(*gated.at(1))
                sp.dma_start(core.spill["g"][t], gate).then_inc(*gated_out.by(16))
                sp.wait_ge(*gated_out.at(16))

            @block.scalar
            def _(act):
                act.wait_ge(*var_done.at(1))
                act.activation(rstd[:], var[:], ACT.Sqrt).then_inc(*rstd_done.by())

            @block.vector
            def _(dve):
                own = in_order(dve, dve_steps)
                own(dve.tensor_reduce(mean[:], heads(y[:]), AX.X, ALU.add))
                own(dve.tensor_scalar(mean[:], mean[:], 1.0 / N, None, ALU.mult))
                own(dve.tensor_tensor(heads(y[:]), heads(y[:]), wide(mean), ALU.subtract))
                own(dve.tensor_tensor(sq[:], y[:], y[:], ALU.mult))
                own(dve.tensor_reduce(var[:], heads(sq[:]), AX.X, ALU.add))
                own(dve.tensor_scalar(var[:], var[:], 1.0 / N, GN_EPS, ALU.mult, ALU.add))
                own(dve.reciprocal(var[:], var[:]))
                dve.sem_inc(*var_done.by())
                dve.wait_ge(*lnx_in.at(32))
                dve.wait_ge(*rstd_done.at(1))
                own(dve.tensor_tensor(heads(y[:]), heads(y[:]), wide(rstd), ALU.mult))
                own(dve.tensor_tensor(y[:], y[:], lnx_g[:], ALU.mult))
                own(dve.tensor_tensor(y[:], y[:], lnx_b[:], ALU.add))
                own(dve.tensor_tensor(y[:], y[:], w["bonus"][:], ALU.add))
                dve.tensor_tensor(gate, y[:], gate, ALU.mult).then_inc(*gated.by())
        core.end_stage()


def to_features(core, src, dst, name):
    nc = core.nc
    with ExitStack() as ctx:
        bank = [ctx.enter_context(nc.psum_tensor(f"tf{i}_{name}", [P, TOK], F32)) for i in range(4)]
        tf_psum, tf_act, tf_dve = core.sig("rows_psum"), core.sig("copied_act"), core.sig("copied_dve")
        with nc.Block() as block:
            @block.tensor
            def _(pe):
                for k in range(KD):
                    if k >= 4:
                        pe.wait_ge(*(tf_act, tf_dve)[k % 2].at((k - 4) // 2 + 1))
                    for t in range(TILES):
                        mm = pe.transpose(bank[k % 4][:, t * P:(t + 1) * P], src[:, t, k * P:(k + 1) * P], core.const("ident"))
                    mm.then_inc(*tf_psum.by())

            @block.scalar
            def _(act):
                for k in range(0, KD, 2):
                    act.wait_ge(*tf_psum.at(k + 1))
                    act.copy(dst[:, k, :], bank[k % 4][:]).then_inc(*tf_act.by())

            @block.vector
            def _(dve):
                for k in range(1, KD, 2):
                    dve.wait_ge(*tf_psum.at(k + 1))
                    dve.tensor_copy(dst[:, k, :], bank[k % 4][:]).then_inc(*tf_dve.by())
        core.end_stage()


def layer_norm_steps(core, dve, own, res, out, g, b, stats, mv, rstd, n):
    for half in range(2):
        ins = dve.bn_stats(stats[:, half, :], res[:, half * HALF:(half + 1) * HALF])
    own(ins)
    own(dve.bn_aggr(mv[:], stats[:].rearrange("p a s -> p (a s)")))
    own(dve.tensor_scalar(mv[:, 1:2], mv[:, 1:2], LN_EPS, None, ALU.add))
    own(dve.reciprocal(mv[:, 1:2], mv[:, 1:2]))
    dve.sem_inc(*core.sig("ln_var").by())
    dve.wait_ge(*core.sig("ln_rstd").at(n))
    own(dve.tensor_scalar(res, res, mv[:, 0:1], rstd[:], ALU.subtract, ALU.mult))
    own(dve.tensor_tensor(res, res, g, ALU.mult))
    own(dve.tensor_tensor(out, res, b, ALU.add))


def layer_norm_roots(core, act, mv, rstd):
    for t in range(TILES):
        act.wait_ge(*core.sig("ln_var").at(t + 1))
        act.activation(rstd[:], mv[:, 1:2], ACT.Sqrt).then_inc(*core.sig("ln_rstd").by())


def project_and_norm(core, io, actT, weight, layer, name):
    nc = core.nc
    with ExitStack() as ctx:
        def sb(name_, shape, dt=F32):
            return ctx.enter_context(nc.sbuf_tensor(f"{name_}_{name}", shape, dt))

        wt = sb("pn_w", [P, KD, D])
        g, b = sb("pn_g", [P, D]), sb("pn_b", [P, D])
        res = sb("pn_res", [P, 2, D])
        stats, mv, rstd = sb("pn_stats", [P, 2, 6]), sb("pn_mv", [P, 2]), sb("pn_rstd", [P, 1])
        acc = ctx.enter_context(nc.psum_tensor(f"pn_acc_{name}", [P, TILES, D], F32))
        pn_w = [core.sig(f"loaded{k}") for k in range(KD)]
        pn_vec, pn_psum, dve_steps = core.sig("vectors_in"), core.sig("rows_psum"), core.sig("dve_steps")
        core.sig("ln_var"), core.sig("ln_rstd")
        with nc.Block() as block:
            @block.sync
            def _(sp):
                for k in range(KD):
                    sp.dma_start(wt[:, k, :], weight[k * P:(k + 1) * P, :]).then_inc(*pn_w[k].by(16))
                sp.dma_start(g[:], io["ln_mix_g"][layer:layer + 1, :].broadcast_to([P, D])).then_inc(*pn_vec.by(16))
                sp.dma_start(b[:], io["ln_mix_b"][layer:layer + 1, :].broadcast_to([P, D])).then_inc(*pn_vec.by(16))

            @block.tensor
            def _(pe):
                for t in range(TILES):
                    for k in range(KD):
                        if t == 0:
                            pe.wait_ge(*pn_w[k].at(16))
                        for h in range(2):
                            mm = pe.matmul(acc[:, t, h * HALF:(h + 1) * HALF], actT[:, k, t * P:(t + 1) * P],
                                           wt[:, k, h * HALF:(h + 1) * HALF], start=(k == 0), stop=(k == KD - 1))
                    mm.then_inc(*pn_psum.by())

            @block.scalar
            def _(act):
                layer_norm_roots(core, act, mv, rstd)

            @block.vector
            def _(dve):
                own = in_order(dve, dve_steps)
                dve.wait_ge(*pn_vec.at(32))
                for t in range(TILES):
                    dve.wait_ge(*pn_psum.at(t + 1))
                    x = core.x_tok[:, t, :]
                    own(dve.scalar_tensor_tensor(res[:, t % 2], x, ALPHA, acc[:, t, :], ALU.mult, ALU.add))
                    layer_norm_steps(core, dve, own, res[:, t % 2], x, g[:], b[:], stats, mv, rstd, t + 1)
        core.end_stage()


def peer_scores(core, io, xT, scores, layer):
    nc = core.nc
    HC = 2 * PH
    with ExitStack() as ctx:
        def sb(name, shape, dt=F32):
            return ctx.enter_context(nc.sbuf_tensor(f"{name}_{layer}", shape, dt))

        RING, PAIR = 4, 2 * P
        wq = sb("wq", [P, RING, KD, PAIR])
        keys, keysT = sb("keys", [P, 2, P]), sb("keysT", [P, 2, P])
        qT = sb("qT", [P, HC, TOK])
        bank = [ctx.enter_context(nc.psum_tensor(f"pbank{i}_{layer}", [P, HALF], F32)) for i in range(8)]
        wq_in = [core.sig(f"loaded{i}") for i in range(RING)]
        keys_in, keys_psum, keys_done = core.sig("vectors_in"), core.sig("keysT_psum"), core.sig("keys_done")
        q_psum, q_done, s_psum, s_done = core.sig("rows_psum"), core.sig("rows_copied"), core.sig("s_psum"), core.sig("ps_done")

        with nc.Block() as block:
            @block.sync
            def _(sp):
                sp.dma_start(keys[:], io["peer_sub_keys"][layer].rearrange("c k d -> k c d")).then_inc(*keys_in.by(16))
                for i in range(PH):
                    if i >= RING:
                        sp.wait_ge(*q_psum.at(2 * (i - RING) + 2))
                    sp.dma_start(wq[:, i % RING], by_chunk(io["peer_w_query"][layer][:, i * PAIR:(i + 1) * PAIR])).then_inc(*wq_in[i % RING].by(16))

            @block.tensor
            def _(pe):
                pe.wait_ge(*keys_in.at(16))
                for c in range(2):
                    mm = pe.transpose(bank[7][:, c * P:(c + 1) * P], keys[:, c, :], core.const("ident"))
                mm.then_inc(*keys_psum.by())
                for m in range(HC):
                    if m % 2 == 0:
                        pe.wait_ge(*wq_in[m // 2 % RING].at(16 * (m // 2 // RING + 1)))
                    if m >= 3:
                        pe.wait_ge(*q_done.at(m - 2))
                    for k in range(KD):
                        mm = pe.matmul(bank[m % 3][:, 0:TOK], wq[:, m // 2 % RING, k, (m % 2) * P:(m % 2 + 1) * P],
                                       xT[:, k, :], start=(k == 0), stop=(k == KD - 1))
                    mm.then_inc(*q_psum.by())
                pe.wait_ge(*keys_done.at(1))
                pe.wait_ge(*q_done.at(HC))
                n = 0
                for t in range(TILES):
                    for q in range(HC // 4):
                        if n >= 4:
                            pe.wait_ge(*s_done.at(n - 3))
                        for m in range(4 * q, 4 * q + 4):
                            mm = pe.matmul(bank[3 + n % 4][:, (m % 4) * P:(m % 4 + 1) * P], qT[:, m, t * P:(t + 1) * P], keysT[:, m % 2, :])
                        mm.then_inc(*s_psum.by())
                        n += 1

            @block.scalar
            def _(act):
                act.wait_ge(*keys_psum.at(1))
                act.copy(keysT[:].rearrange("p c k -> p (c k)"), bank[7][:, 0:2 * P]).then_inc(*keys_done.by())
                for m in range(HC):
                    act.wait_ge(*q_psum.at(m + 1))
                    act.copy(qT[:, m, :], bank[m % 3][:, 0:TOK]).then_inc(*q_done.by())
                for n in range(TILES * HC // 4):
                    act.wait_ge(*s_psum.at(n + 1))
                    act.copy(scores[:, n // 4, 4 * (n % 4):4 * (n % 4) + 4, :].rearrange("p m k -> p (m k)"), bank[3 + n % 4][:]).then_inc(*s_done.by())
        core.end_stage()


def top16(dve, own, passed, values, places, source):
    dve.sem_inc(*passed.by())
    for n in range(len(source)):
        ins = dve.max(values[n][:, 0:8], source[n])
    own(ins)
    dve.sem_inc(*passed.by())
    for n in range(len(source)):
        dve.max_index(places[n][:, 0:8], values[n][:, 0:8], source[n])
    for n in range(len(source)):
        ins = dve.match_replace(source[n], values[n][:, 0:8], source[n], -3.0e38)
    own(ins)
    dve.sem_inc(*passed.by())
    for n in range(len(source)):
        ins = dve.max(values[n][:, 8:16], source[n])
    own(ins)
    dve.sem_inc(*passed.by())
    for n in range(len(source)):
        ins = dve.max_index(places[n][:, 8:16], values[n][:, 8:16], source[n])
    own(ins)


def peer_experts(core, io, scores, layer):
    nc = core.nc
    RING = 8
    TURN = 2 * RING
    TURNS = SLOTS // TURN
    HC = 2 * PH
    TOPK_STEPS = 25
    u_rows, v_rows = (io[n].rearrange("l e d -> (l e) d") for n in ("peer_u", "peer_v"))
    with ExitStack() as ctx:
        def sb(name, shape, dt=F32):
            return ctx.enter_context(nc.sbuf_tensor(f"{name}_{layer}", shape, dt))

        u_ring, v_ring = sb("u_ring", [P, RING, D]), sb("v_ring", [P, RING, D])
        u_at, v_at = sb("u_at", [P, TURN], U32), sb("v_at", [P, TURN], U32)
        expert = sb("expert", [P, TILES * SLOTS], U32)
        gate, act_in, mix = sb("gate", [P, SLOTS]), sb("act_in", [P, SLOTS]), sb("mix", [P, TILES * SLOTS])
        work = sb("work", [P, HC, PK])
        row = sb("row", [P, D])
        best, best_at = sb("best", [P, HC, PTOP]), sb("best_at", [P, HC, PTOP], U32)
        best_at_f = sb("best_at_f", [P, HC, PTOP])
        cand = sb("cand", [P, PH, PTOP * PTOP])
        top, top_at = sb("top", [P, PH, PTOP]), sb("top_at", [P, PH, PTOP], U32)
        digit, digit_f = sb("digit", [P, 2, SLOTS], U32), sb("digit_f", [P, 2, SLOTS])
        hot, found = sb("hot", [P, SLOTS, PTOP]), sb("found", [P, 2, SLOTS])
        norm = sb("norm", [P, PH])
        dots = sb("dots", [P, TURN])
        mix_now = sb("mix_now", [P, TURN])
        DIAGS = 4
        diag = sb("diag", [P, DIAGS, P])
        zero = sb("zero", [P, P])
        ffn = sb("ffn", [P, TILES, D])
        ln_g, ln_b = sb("ln_g", [P, D]), sb("ln_b", [P, D])
        stats, mv, rstd = sb("pstats", [P, 2, 6]), sb("pmv", [P, 2]), sb("prstd", [P, 1])
        acc = ctx.enter_context(nc.psum_tensor(f"pacc_{layer}", [P, 2, HALF], F32))

        u_in = [core.sig(f"u_in{i}") for i in range(RING)]
        v_in = [core.sig(f"v_in{i}") for i in range(RING)]
        u_used, v_used, at_copied = core.sig("u_used"), core.sig("v_used"), core.sig("at_copied")
        chosen, gate_arg, gate_exp = core.sig("chosen"), core.sig("gate_arg"), core.sig("gate_exp")
        dots_all, gelu_done, mix_done = core.sig("dots_all"), core.sig("gelu_done"), core.sig("mix_done")
        mix_now_done, diag_done = core.sig("mix_now_done"), core.sig("diag_ready")
        zeroed, ffn_psum, ffn_done, ln_in = core.sig("zeroed"), core.sig("ffn_psum"), core.sig("ffn_done"), core.sig("vectors_in")
        dve_steps, pool_turns, passed = core.sig("dve_steps"), core.sig("pool_turns"), core.sig("dve_passed")
        dots_done, act_turns = core.sig("dots_done"), core.sig("act_turns")
        core.sig("ln_var"), core.sig("ln_rstd")

        with nc.Block() as block:
            @block.sync
            def _(sp):
                sp.dma_start(ln_g[:], io["ln_ffn_g"][layer:layer + 1, :].broadcast_to([P, D])).then_inc(*ln_in.by(16))
                sp.dma_start(ln_b[:], io["ln_ffn_b"][layer:layer + 1, :].broadcast_to([P, D])).then_inc(*ln_in.by(16))

            @block.gpsimd
            def _(pool):
                def gathers(t, table, ring, places, arrived, used):
                    with pool.Fori(0, TURNS) as s, turns(s, TURNS, counted=(at_copied, pool_turns, *arrived)):
                        for half in range(2):
                            at = places[:, half * RING:(half + 1) * RING]
                            first = t * SLOTS + s * TURN + half * RING
                            pool.wait_ge(*used.at(first + 1))
                            pool.sem_inc(*pool_turns.by())
                            pool.tensor_copy(at, expert[:, bass.ds(first, RING)]).then_inc(*at_copied.by())
                            for j in range(RING):
                                pool.wait_ge(*used.at(first + j + 1))
                                if j == 0:
                                    pool.wait_ge(*at_copied.at(at_base + t * 4 * TURNS + s * 2 + half + 1))
                                pool.sem_inc(*pool_turns.by())
                                pool.indirect_dma_start(ring[:, j, :], None, table,
                                                        bass.IndirectOffsetOnAxis(ap=at[:, j:j + 1], axis=0)).then_inc(*arrived[j].by(16))

                with pool.Fori(0, TILES) as t, turns(t, TILES, counted=(at_copied, pool_turns, *u_in, *v_in)):
                    pool.wait_ge(*chosen.at(t + 1))
                    pool.sem_inc(*pool_turns.by())
                    at_base = 0
                    gathers(t, u_rows, u_ring, u_at, u_in, u_used)
                    at_base = 2 * TURNS
                    gathers(t, v_rows, v_ring, v_at, v_in, v_used)

            @block.vector
            def _(dve):
                own = in_order(dve, dve_steps)
                x = core.x_tok
                dve.memset(zero[:], 0.0).then_inc(*zeroed.by())
                dve.sem_inc(*u_used.by(RING))
                heads4 = [P, PH, PTOP, PTOP]
                with dve.Fori(0, TILES) as t, turns(t, TILES, own=dve_steps, per=TOPK_STEPS,
                                                    counted=(chosen, gate_arg, dots_all, mix_done, u_used, dots_done, passed)):
                    dve.tensor_copy(work[:].rearrange("p m k -> p (m k)"), scores[:, bass.ds(t, 1)].rearrange("p o m k -> p (o m k)"))
                    own(dve.tensor_copy(row[:], x[:, bass.ds(t, 1)].rearrange("p o d -> p (o d)")))
                    top16(dve, own, passed, [best[:, m, :] for m in range(HC)], [best_at[:, m, :] for m in range(HC)], [work[:, m, :] for m in range(HC)])
                    two = best[:].rearrange("p (h c) k -> p h c k", c=2)
                    dve.tensor_copy(best_at_f[:], best_at[:])
                    own(dve.tensor_tensor(cand[:].rearrange("p h (i j) -> p h i j", j=PTOP), two[:, :, 0, :].unsqueeze(3).broadcast_to(heads4),
                                          two[:, :, 1, :].unsqueeze(2).broadcast_to(heads4), ALU.add))
                    top16(dve, own, passed, [top[:, h, :] for h in range(PH)], [top_at[:, h, :] for h in range(PH)], [cand[:, h, :] for h in range(PH)])
                    gate_h = gate[:].rearrange("p (h k) -> p h k", k=PTOP)
                    own(dve.tensor_tensor(gate_h, top[:], top[:, :, 0:1].broadcast_to([P, PH, PTOP]), ALU.subtract))
                    dve.sem_inc(*gate_arg.by())
                    flat = top_at[:].rearrange("p h k -> p (h k)")
                    dve.tensor_scalar(digit[:, 0, :], flat, 4, None, ALU.logical_shift_right)
                    own(dve.tensor_scalar(digit[:, 1, :], flat, 15, None, ALU.bitwise_and))
                    own(dve.tensor_copy(digit_f[:], digit[:]))
                    two_at = best_at_f[:].rearrange("p (h c) k -> p h c k", c=2)
                    hot4 = hot[:].rearrange("p (h k) j -> p h k j", k=PTOP)
                    for c in range(2):
                        own(dve.tensor_tensor(hot[:], core.const("iota").unsqueeze(1).broadcast_to([P, SLOTS, PTOP]),
                                              digit_f[:, c, :].unsqueeze(2).broadcast_to([P, SLOTS, PTOP]), ALU.is_equal))
                        own(dve.tensor_tensor(hot4, hot4, two_at[:, :, c, :].unsqueeze(2).broadcast_to(heads4), ALU.mult))
                        own(dve.tensor_reduce(found[:, c, :], hot[:], AX.X, ALU.add))
                    own(dve.tensor_scalar(found[:, 0, :], found[:, 0, :], float(PK), float(layer * EXPERTS), ALU.mult, ALU.add))
                    own(dve.tensor_tensor(expert[:, bass.ds(t * SLOTS, SLOTS)], found[:, 0, :], found[:, 1, :], ALU.add))
                    dve.sem_inc(*chosen.by())
                    with dve.Fori(0, TURNS) as s, turns(s, TURNS, counted=(u_used, dots_done)):
                        for j in range(TURN):
                            dve.wait_ge(*u_in[j % RING].at(16 * (t * 2 * TURNS + s * 2 + j // RING + 1)))
                            dve.tensor_tensor_reduce(u_ring[:, j % RING, :], u_ring[:, j % RING, :], row[:], 1.0, 0.0,
                                                     ALU.mult, ALU.add, dots[:, j:j + 1]).then_inc(*u_used.by())
                        dve.wait_ge(*u_used.at(t * SLOTS + s * TURN + TURN + RING))
                        dve.tensor_copy(act_in[:, bass.ds(s * TURN, TURN)], dots[:]).then_inc(*dots_done.by())
                        dve.wait_ge(*dots_done.at(t * TURNS + s + 1))
                    dve.sem_inc(*dots_all.by())
                    dve.wait_ge(*gate_exp.at(t + 1))
                    own(dve.tensor_reduce(norm[:], gate_h, AX.X, ALU.add))
                    own(dve.reciprocal(norm[:], norm[:]))
                    own(dve.tensor_tensor(gate_h, gate_h, norm[:].unsqueeze(2).broadcast_to([P, PH, PTOP]), ALU.mult))
                    dve.wait_ge(*gelu_done.at(t + 1))
                    own(dve.tensor_tensor(mix[:, bass.ds(t * SLOTS, SLOTS)], gate[:], act_in[:], ALU.mult))
                    dve.sem_inc(*mix_done.by())
                dve.wait_ge(*ln_in.at(32))
                for t in range(TILES):
                    dve.wait_ge(*ffn_done.at(t + 2))
                    own(dve.scalar_tensor_tensor(ffn[:, t, :], x[:, t, :], ALPHA, ffn[:, t, :], ALU.mult, ALU.add))
                    layer_norm_steps(core, dve, own, ffn[:, t, :], x[:, t, :], ln_g[:], ln_b[:], stats, mv, rstd, t + 1)

            @block.scalar
            def _(act):
                act.sem_inc(*ffn_done.by())
                with act.Fori(0, TILES) as t, turns(t, TILES, counted=(gate_exp, gelu_done, mix_now_done, diag_done, act_turns, ffn_done)):
                    act.wait_ge(*gate_arg.at(t + 1))
                    act.activation(gate[:], gate[:], ACT.Exp).then_inc(*gate_exp.by())
                    act.wait_ge(*dots_all.at(t + 1))
                    act.activation(act_in[:], act_in[:], ACT.Gelu).then_inc(*gelu_done.by())
                    act.wait_ge(*mix_done.at(t + 1))
                    act.sem_inc(*act_turns.by())
                    with act.Fori(0, TURNS) as s, turns(s, TURNS, counted=(mix_now_done, diag_done, act_turns)):
                        act.copy(mix_now[:], mix[:, bass.ds(t * SLOTS + s * TURN, TURN)]).then_inc(*mix_now_done.by())
                        for j in range(TURN):
                            if j == 0:
                                act.wait_ge(*mix_now_done.at(t * TURNS + s + 1))
                            act.wait_ge(*v_used.at(t * SLOTS + s * TURN + j + 1 + RING - DIAGS))
                            act.activation(diag[:, j % DIAGS, :], core.const("ident"), ACT.Copy, scale=mix_now[:, j:j + 1]).then_inc(*diag_done.by())
                        act.wait_ge(*diag_done.at(t * SLOTS + s * TURN + TURN))
                        act.sem_inc(*act_turns.by())
                    act.wait_ge(*ffn_psum.at(t + 1))
                    act.sem_inc(*act_turns.by())
                    act.copy(ffn[:, bass.ds(t, 1)].rearrange("p o d -> p (o d)"), acc[:].rearrange("p a d -> p (a d)")).then_inc(*ffn_done.by())
                layer_norm_roots(core, act, mv, rstd)

            @block.tensor
            def _(pe):
                x_first = core.x_tok[:, 0, :]
                pe.wait_ge(*zeroed.at(1))
                pe.sem_inc(*v_used.by(RING))
                with pe.Fori(0, TILES) as t, turns(t, TILES, counted=(v_used, ffn_psum)):
                    pe.wait_ge(*mix_done.at(t + 1))
                    pe.wait_ge(*ffn_done.at(t + 1))
                    for half in range(2):
                        pe.matmul(acc[:, half, :], zero[:], x_first[:, half * HALF:(half + 1) * HALF], start=True, stop=False)
                    with pe.Fori(0, TURNS) as s, turns(s, TURNS, counted=(v_used,)):
                        for j in range(TURN):
                            pe.wait_ge(*v_in[j % RING].at(16 * (t * 2 * TURNS + s * 2 + j // RING + 1)))
                            pe.wait_ge(*diag_done.at(t * SLOTS + s * TURN + j + 1))
                            pe.matmul(acc[:, 0, :], diag[:, j % DIAGS, :], v_ring[:, j % RING, 0:HALF], start=False, stop=False)
                            pe.matmul(acc[:, 1, :], diag[:, j % DIAGS, :], v_ring[:, j % RING, HALF:], start=False, stop=False).then_inc(*v_used.by())
                    for half in range(2):
                        mm = pe.matmul(acc[:, half, :], zero[:], x_first[:, half * HALF:(half + 1) * HALF], start=False, stop=True)
                    mm.then_inc(*ffn_psum.by())
        core.end_stage()


def attention_projections(core, io, xT, out):
    nc = core.nc
    weights = [("k", io["w_kv"][:, 0:D]), ("v", io["w_kv"][:, D:]), ("q", io["diff_w_q"][0])]
    with ExitStack() as ctx:
        RING = 12
        ring = ctx.enter_context(nc.sbuf_tensor("aw_ring", [P, RING, D], F32))
        rot = ctx.enter_context(nc.sbuf_tensor("rot", [P, 4, TILES, 2 * DH, ROT // 2], F32))
        acc = ctx.enter_context(nc.psum_tensor("aacc", [P, 6, HALF], F32))
        aw_in = [core.sig(f"loaded{i}") for i in range(RING)]
        aw_used, a_full, a_free = core.sig("w_used"), core.sig("acc_full"), core.sig("acc_free_act")
        rotated, kv_out, dve_steps = core.sig("rotated"), core.sig("kv_out"), core.sig("dve_steps")

        with nc.Block() as block:
            @block.sync
            def _(sp):
                for n in range(3 * KD):
                    if n >= RING:
                        sp.wait_ge(*aw_used.at(n - RING + 1))
                    sp.dma_start(ring[:, n % RING, :], weights[n // KD][1][n % KD * P:(n % KD + 1) * P, :]).then_inc(*aw_in[n % RING].by(16))

            @block.gpsimd
            def _(pool):
                pool.wait_ge(*a_free.at(12))
                for n, wait in (("v", None), ("k", rotated)):
                    if wait:
                        pool.wait_ge(*wait.at(1))
                    tail = "h c d -> (b s) (h c d)" if n == "k" else "h e -> (b s) (h e)"
                    rows_p, rows_s = (io[f"cache_{n}_{w}"].rearrange("b s " + tail) for w in "ps")
                    pool.dma_start(rows_p.rearrange("(t p) e -> p t e", p=P), out[n][:, 0:2, :]).then_inc(*kv_out.by(16))
                    pool.dma_start(rows_s, out[n][:, 2, :]).then_inc(*kv_out.by(16))
                pool.wait_ge(*kv_out.at(64))

            @block.tensor
            def _(pe):
                for i in range(3):
                    for k in range(KD):
                        n = i * KD + k
                        pe.wait_ge(*aw_in[n % RING].at(16 * (n // RING + 1)))
                        for b in range(6):
                            if k == 0 and i > 0:
                                pe.wait_ge(*a_free.at(6 * (i - 1) + b + 1))
                            t, h = divmod(b, 2)
                            mm = pe.matmul(acc[:, b, :], xT[:, k, t * P:(t + 1) * P], ring[:, n % RING, h * HALF:(h + 1) * HALF],
                                           start=(k == 0), stop=(k == KD - 1))
                            if k == KD - 1:
                                mm.then_inc(*a_full.by())
                        if k < KD - 1:
                            mm.then_inc(*aw_used.by())
                        else:
                            pe.wait_ge(*a_full.at(6 * (i + 1)))
                            pe.sem_inc(*aw_used.by())

            @block.scalar
            def _(act):
                for i, (n, _) in enumerate(weights):
                    for b in range(6):
                        act.wait_ge(*a_full.at(6 * i + b + 1))
                        act.copy(out[n][:, b // 2, (b % 2) * HALF:(b % 2 + 1) * HALF], acc[:, b, :]).then_inc(*a_free.by())

            @block.vector
            def _(dve):
                own = in_order(dve, dve_steps)
                angle = [core.const(n).rearrange("p (t r) -> p t r", t=TILES).unsqueeze(2).broadcast_to([P, TILES, 2 * DH, ROT // 2]) for n in ("cos", "sin")]
                for i, n in ((0, "k"), (2, "q")):
                    dve.wait_ge(*a_free.at(6 * (i + 1)))
                    x = out[n][:].rearrange("p t (g d) -> p t g d", d=DD)
                    x1, x2 = x[:, :, :, 0:ROT // 2], x[:, :, :, ROT // 2:ROT]
                    for j, (src, f) in enumerate(((x1, 0), (x2, 1), (x1, 1), (x2, 0))):
                        ins = dve.tensor_tensor(rot[:, j], src, angle[f], ALU.mult)
                    own(ins)
                    dve.tensor_tensor(x1, rot[:, 0], rot[:, 1], ALU.subtract)
                    own(dve.tensor_tensor(x2, rot[:, 2], rot[:, 3], ALU.add))
                    dve.sem_inc(*rotated.by())
        core.end_stage()


def mixing_weight(core, io, neg_lam):
    nc = core.nc
    with ExitStack() as ctx:
        lp = ctx.enter_context(nc.sbuf_tensor("lam_rows", [P, 2, 2, DD], F32))
        prod = ctx.enter_context(nc.sbuf_tensor("lam_prod", [P, 2, DD], F32))
        dot = ctx.enter_context(nc.sbuf_tensor("lam_dot", [P, 2], F32))
        lam_in, lam_dot, lam_exp, dve_steps = core.sig("vectors_in"), core.sig("lam_dot"), core.sig("lam_exp"), core.sig("dve_steps")
        with nc.Block() as block:
            @block.sync
            def _(sp):
                sp.dma_start(lp[:].rearrange("p a b d -> p (a b d)"), io["diff_lambda"].rearrange("a i d -> a (i d)").broadcast_to([P, 4 * DD])).then_inc(*lam_in.by(16))

            @block.scalar
            def _(act):
                act.wait_ge(*lam_dot.at(1))
                act.activation(dot[:], dot[:], ACT.Exp).then_inc(*lam_exp.by())

            @block.vector
            def _(dve):
                own = in_order(dve, dve_steps)
                dve.wait_ge(*lam_in.at(16))
                own(dve.tensor_tensor(prod[:], lp[:, :, 0, :], lp[:, :, 1, :], ALU.mult))
                own(dve.tensor_reduce(dot[:], prod[:], AX.X, ALU.add))
                dve.sem_inc(*lam_dot.by())
                dve.wait_ge(*lam_exp.at(1))
                own(dve.tensor_tensor(neg_lam[:], dot[:, 1:2], dot[:, 0:1], ALU.subtract))
                own(dve.tensor_scalar(neg_lam[:], neg_lam[:], -LAM_INIT, None, ALU.add))
        core.end_stage()


def prompt_attention(core, qT, kT, v_tok, oT, neg_lam):
    nc = core.nc
    SCALE = DD ** -0.5
    parts = (slice(0, P), slice(P, 3 * P))
    with ExitStack() as ctx:
        def sb(name, shape, dt=F32):
            return ctx.enter_context(nc.sbuf_tensor("pa_" + name, shape, dt))

        s, p = sb("s", [P, 2, 2, TOK]), sb("p", [P, 2, 2, TOK])
        top, low, tot = sb("top", [P, 2, 4]), sb("low", [P, 2, 4]), sb("tot", [P, 2, 4])
        attn, attnT = sb("attn", [P, 2, TOK]), sb("attnT", [P, 2, TOK])
        s_bank = [ctx.enter_context(nc.psum_tensor(f"pa_s{i}", [P, TOK], F32)) for i in range(4)]
        t_bank = [ctx.enter_context(nc.psum_tensor(f"pa_t{i}", [P, TOK], F32)) for i in range(2)]
        o_bank = [ctx.enter_context(nc.psum_tensor(f"pa_o{i}", [P, SEQ], F32)) for i in range(2)]
        sc, sm, top_done, p_done = core.sig("scores_psum"), core.sig("scores_masked"), core.sig("maxima"), core.sig("probs")
        attn_done, at_psum, at_done = core.sig("maps_mixed"), core.sig("mixedT_psum"), core.sig("mixedT")
        o_psum, o_done, dve_steps = core.sig("heads_psum"), core.sig("heads_out"), core.sig("dve_steps")
        with nc.Block() as block:
            @block.tensor
            def _(pe):
                def scores(h):
                    if h >= 2:
                        pe.wait_ge(*sm.at(2 * (h - 1)))
                    for c in range(2):
                        rows = slice(c * DD, (c + 1) * DD)
                        bank = s_bank[2 * (h % 2) + c]
                        pe.matmul(bank[:, parts[0]], qT[rows, h, 0:P], kT[rows, h, 0:P])
                        pe.matmul(bank[:, parts[1]], qT[rows, h, P:2 * P], kT[rows, h, 0:2 * P]).then_inc(*sc.by())

                scores(0)
                for h in range(DH):
                    if h + 1 < DH:
                        scores(h + 1)
                    pe.wait_ge(*attn_done.at(h + 1))
                    if h >= 2:
                        pe.wait_ge(*at_done.at(h - 1))
                    for i in range(3):
                        mm = pe.transpose(t_bank[h % 2][:, i * P:(i + 1) * P], attn[:, h % 2, i * P:(i + 1) * P], core.const("ident"))
                    mm.then_inc(*at_psum.by())
                    pe.wait_ge(*at_done.at(h + 1))
                    if h >= 2:
                        pe.wait_ge(*o_done.at(h - 1))
                    e = slice(h * P, (h + 1) * P)
                    pe.matmul(o_bank[h % 2][:, 0:P], v_tok[:, 0, e], attnT[:, h % 2, 0:P])
                    pe.matmul(o_bank[h % 2][:, P:], v_tok[:, 0, e], attnT[:, h % 2, P:2 * P], start=True, stop=False)
                    pe.matmul(o_bank[h % 2][:, P:], v_tok[:, 1, e], attnT[:, h % 2, 2 * P:], start=False, stop=True).then_inc(*o_psum.by())

            @block.scalar
            def _(act):
                def flush(h):
                    act.wait_ge(*at_psum.at(h + 1))
                    act.copy(attnT[:, h % 2, :], t_bank[h % 2][:]).then_inc(*at_done.by())
                    act.wait_ge(*o_psum.at(h + 1))
                    act.copy(oT[:, h, 0:SEQ], o_bank[h % 2][:]).then_inc(*o_done.by())

                for h in range(DH):
                    act.wait_ge(*top_done.at(h + 1))
                    if h >= 2:
                        act.wait_ge(*attn_done.at(h - 1))
                    for c in range(2):
                        for i in range(2):
                            j = 2 * c + i
                            act.activation(p[:, h % 2, c, parts[i]], s[:, h % 2, c, parts[i]], ACT.Exp, bias=low[:, h % 2, j:j + 1],
                                           scale=SCALE, accum_out=tot[:, h % 2, j:j + 1]).then_inc(*p_done.by())
                    if h >= 1:
                        flush(h - 1)
                flush(DH - 1)

            @block.vector
            def _(dve):
                own = in_order(dve, dve_steps)

                def combine(h):
                    dve.wait_ge(*p_done.at(4 * (h + 1)))
                    own(dve.reciprocal(tot[:, h % 2, :], tot[:, h % 2, :]))
                    own(dve.tensor_scalar(tot[:, h % 2, 2:4], tot[:, h % 2, 2:4], neg_lam[:, 0:1], None, ALU.mult))
                    if h >= 2:
                        dve.wait_ge(*at_psum.at(h - 1))
                    for i in range(2):
                        dve.tensor_scalar(attn[:, h % 2, parts[i]], p[:, h % 2, 1, parts[i]], tot[:, h % 2, 2 + i:3 + i], None, ALU.mult)
                    own(dve.tensor_copy(top[:, h % 2, 0:1], top[:, h % 2, 0:1]))
                    for i in range(2):
                        ins = dve.scalar_tensor_tensor(attn[:, h % 2, parts[i]], p[:, h % 2, 0, parts[i]], tot[:, h % 2, i:i + 1],
                                                       attn[:, h % 2, parts[i]], ALU.mult, ALU.add)
                    own(ins)
                    dve.sem_inc(*attn_done.by())

                for h in range(DH):
                    if h >= 2:
                        dve.wait_ge(*p_done.at(4 * (h - 1)))
                    for c in range(2):
                        dve.wait_ge(*sc.at(2 * h + c + 1))
                        dve.tensor_tensor(s[:, h % 2, c, :], s_bank[2 * (h % 2) + c][:], core.const("causal"), ALU.add).then_inc(*sm.by())
                    dve.wait_ge(*sm.at(2 * h + 2))
                    for c in range(2):
                        for i in range(2):
                            ins = dve.tensor_reduce(top[:, h % 2, 2 * c + i:2 * c + i + 1], s[:, h % 2, c, parts[i]], AX.X, ALU.max)
                    own(ins)
                    own(dve.tensor_scalar(low[:, h % 2, :], top[:, h % 2, :], -SCALE, None, ALU.mult))
                    dve.sem_inc(*top_done.by())
                    if h >= 1:
                        combine(h - 1)
                combine(DH - 1)
        core.end_stage()


def sample_attention(core, io, qT, kT, v_tok, oT, neg_lam):
    nc = core.nc
    SCALE = DD ** -0.5
    KT = PAST // P
    HQ = DH * DEC_SEQ
    assert HQ == P
    ident = core.const("ident")
    with ExitStack() as ctx:
        def sb(name, shape, dt=F32):
            return ctx.enter_context(nc.sbuf_tensor("sa_" + name, shape, dt))

        kc, vc = sb("kc", [P, 2, KT, D]), sb("vc", [P, 2, KT, D])
        kcT = sb("kcT", [P, DH, PAST])
        q_own = sb("q_own", [P, DEC_BATCH, DH, HQ])
        sn = sb("sn", [P, 2, P])
        p = sb("p", [P, 2, PAST + P])
        attn, attnT = sb("attn", [P, PAST + P]), sb("attnT", [P, KT + 1, HQ])
        top, low, tot, tot2 = sb("top", [P, 4]), sb("low", [P, 2]), sb("tot", [P, 4]), sb("tot2", [P, 2])
        bank = [ctx.enter_context(nc.psum_tensor(f"sa_b{i}", [P, HALF], F32)) for i in range(8)]
        kc_in, vc_in = [core.sig(f"kc_in{i}") for i in range(2)], [core.sig(f"vc_in{i}") for i in range(2)]
        q_zero, q_done = core.sig("sa_qz"), core.sig("sa_q")
        kt_psum, kt_act, kt_dve = core.sig("keysT_psum"), core.sig("copied_act"), core.sig("copied_dve")
        sc, sn_done, low_done, p_done = core.sig("scores_psum"), core.sig("scores_masked"), core.sig("maxima"), core.sig("probs")
        attn_done, at_psum, at_done = core.sig("maps_mixed"), core.sig("mixedT_psum"), core.sig("mixedT")
        o_psum, o_done, dve_steps = core.sig("heads_psum"), core.sig("heads_out"), core.sig("dve_steps")

        with nc.Block() as block:
            @block.sync
            def _(sp):
                for b in range(DEC_BATCH):
                    if b >= 2:
                        sp.wait_ge(*kt_psum.at(DH * (b - 1)))
                    sp.dma_start(kc[:, b % 2], io["cache_k"][b].rearrange("(j p) h c d -> p j (h c d)", p=P)).then_inc(*kc_in[b % 2].by(16))
                    if b >= 2:
                        sp.wait_ge(*o_psum.at(b - 1))
                    sp.dma_start(vc[:, b % 2], io["cache_v"][b].rearrange("(j p) h e -> p j (h e)", p=P)).then_inc(*vc_in[b % 2].by(16))

            @block.gpsimd
            def _(pool):
                pool.memset(q_own[:], 0.0).then_inc(*q_zero.by())
                pool.wait_ge(*q_zero.at(1))
                for h in range(DH):
                    ins = pool.tensor_copy(q_own[:, :, h, h * DEC_SEQ:(h + 1) * DEC_SEQ],
                                           qT[:, h, SEQ:TOK].rearrange("p (b s) -> p b s", s=DEC_SEQ))
                ins.then_inc(*q_done.by())

            @block.tensor
            def _(pe):
                def transposes(b):
                    pe.wait_ge(*kc_in[b % 2].at(16 * (b // 2 + 1)))
                    for h in range(DH):
                        n = b * DH + h
                        if n >= 2:
                            pe.wait_ge(*(kt_act, kt_dve)[n % 2].at(n // 2))
                        for j in range(KT):
                            mm = pe.transpose(bank[n % 2][:, j * P:(j + 1) * P], kc[:, b % 2, j, h * P:(h + 1) * P], ident)
                        mm.then_inc(*kt_psum.by())

                transposes(0)
                pe.wait_ge(*q_done.at(1))
                for b in range(DEC_BATCH):
                    pe.wait_ge(*kt_act.at(DH // 2 * (b + 1)))
                    pe.wait_ge(*kt_dve.at(DH // 2 * (b + 1)))
                    if b > 0:
                        pe.wait_ge(*p_done.at(4 * b))
                        pe.wait_ge(*at_done.at(2 * b))
                    for c in range(2):
                        rows = slice(c * DD, (c + 1) * DD)
                        for h in range(DH):
                            pe.matmul(bank[2 + c][:], q_own[rows, b, h, :], kcT[rows, h, :], start=(h == 0), stop=(h == DH - 1))
                        for h in range(DH):
                            mm = pe.matmul(bank[4 + c][:, 0:P], q_own[rows, b, h, :], kT[rows, h, SEQ:TOK], start=(h == 0), stop=(h == DH - 1))
                        mm.then_inc(*sc.by())
                    pe.wait_ge(*sc.at(2 * b + 2))
                    if b + 1 < DEC_BATCH:
                        transposes(b + 1)
                    pe.wait_ge(*attn_done.at(b + 1))
                    for j in range(KT + 1):
                        out = bank[6][:, j * P:(j + 1) * P] if j < KT else bank[4][:, 0:P]
                        mm = pe.transpose(out, attn[:, j * P:(j + 1) * P], ident)
                    mm.then_inc(*at_psum.by())
                    pe.wait_ge(*at_done.at(2 * b + 2))
                    pe.wait_ge(*vc_in[b % 2].at(16 * (b // 2 + 1)))
                    if b > 0:
                        pe.wait_ge(*o_done.at(b))
                    for h in range(DH):
                        q = slice(h * DEC_SEQ, (h + 1) * DEC_SEQ)
                        for j in range(KT + 1):
                            v = vc[:, b % 2, j, h * P:(h + 1) * P] if j < KT else v_tok[:, 2, h * P:(h + 1) * P]
                            mm = pe.matmul(bank[7][:, q], v, attnT[:, j, q], start=(j == 0), stop=(j == KT))
                    mm.then_inc(*o_psum.by())

            @block.scalar
            def _(act):
                def keys(b):
                    for n in range(b * DH, (b + 1) * DH, 2):
                        act.wait_ge(*kt_psum.at(n + 1))
                        if b > 0:
                            act.wait_ge(*sc.at(2 * b))
                        act.copy(kcT[:, n % DH, :], bank[0][:]).then_inc(*kt_act.by())

                keys(0)
                for b in range(DEC_BATCH):
                    act.wait_ge(*low_done.at(b + 1))
                    if b > 0:
                        act.wait_ge(*attn_done.at(b))
                    for c in range(2):
                        act.activation(p[:, c, 0:PAST], bank[2 + c][:], ACT.Exp, bias=low[:, c:c + 1], scale=SCALE,
                                       accum_out=tot[:, c:c + 1]).then_inc(*p_done.by())
                        act.activation(p[:, c, PAST:], sn[:, c, :], ACT.Exp, bias=low[:, c:c + 1], scale=SCALE,
                                       accum_out=tot[:, 2 + c:3 + c]).then_inc(*p_done.by())
                    if b + 1 < DEC_BATCH:
                        keys(b + 1)
                    act.wait_ge(*at_psum.at(b + 1))
                    act.copy(attnT[:, 0:KT, :].rearrange("p j q -> p (j q)"), bank[6][:]).then_inc(*at_done.by())
                    act.copy(attnT[:, KT, :], bank[4][:, 0:P]).then_inc(*at_done.by())
                    act.wait_ge(*o_psum.at(b + 1))
                    act.copy(oT[:, :, SEQ + b * DEC_SEQ:SEQ + (b + 1) * DEC_SEQ], bank[7][:, 0:HQ].rearrange("p (h q) -> p h q", h=DH)).then_inc(*o_done.by())

            @block.vector
            def _(dve):
                own = in_order(dve, dve_steps)

                def keys(b):
                    for n in range(b * DH + 1, (b + 1) * DH, 2):
                        dve.wait_ge(*kt_psum.at(n + 1))
                        if b > 0:
                            dve.wait_ge(*sc.at(2 * b))
                        dve.tensor_copy(kcT[:, n % DH, :], bank[1][:]).then_inc(*kt_dve.by())

                keys(0)
                for b in range(DEC_BATCH):
                    if b > 0:
                        dve.wait_ge(*p_done.at(4 * b))
                    own_keys = core.const("own_stream")[:, 112 - DEC_SEQ * b:112 - DEC_SEQ * b + P]
                    for c in range(2):
                        dve.wait_ge(*sc.at(2 * b + c + 1))
                        dve.tensor_tensor(sn[:, c, :], bank[4 + c][:, 0:P], own_keys, ALU.add).then_inc(*sn_done.by())
                        dve.tensor_reduce(top[:, c:c + 1], bank[2 + c][:], AX.X, ALU.max)
                    dve.wait_ge(*sn_done.at(2 * b + 2))
                    for c in range(2):
                        ins = dve.tensor_reduce(top[:, 2 + c:3 + c], sn[:, c, :], AX.X, ALU.max)
                    own(ins)
                    own(dve.tensor_tensor(low[:], top[:, 0:2], top[:, 2:4], ALU.max))
                    own(dve.tensor_scalar(low[:], low[:], -SCALE, None, ALU.mult))
                    dve.sem_inc(*low_done.by())
                    if b + 1 < DEC_BATCH:
                        keys(b + 1)
                    dve.wait_ge(*p_done.at(4 * b + 4))
                    own(dve.tensor_tensor(tot2[:], tot[:, 0:2], tot[:, 2:4], ALU.add))
                    own(dve.reciprocal(tot2[:], tot2[:]))
                    own(dve.tensor_scalar(tot2[:, 1:2], tot2[:, 1:2], neg_lam[:, 0:1], None, ALU.mult))
                    if b > 0:
                        dve.wait_ge(*at_psum.at(b))
                    own(dve.tensor_scalar(attn[:], p[:, 1, :], tot2[:, 1:2], None, ALU.mult))
                    own(dve.scalar_tensor_tensor(attn[:], p[:, 0, :], tot2[:, 0:1], attn[:], ALU.mult, ALU.add))
                    dve.sem_inc(*attn_done.by())
        core.end_stage()


def head_norm(core, io, oT):
    nc = core.nc
    flat = oT[:].rearrange("p h t -> p (h t)")
    COLS = DH * TOK // HALF
    with ExitStack() as ctx:
        def sb(name, shape, dt=F32):
            return ctx.enter_context(nc.sbuf_tensor("hn_" + name, shape, dt))

        sq, inv, ones, gain = sb("sq", [P, DH * TOK]), sb("inv", [P, DH * TOK]), sb("ones", [P, P]), sb("gain", [P, 1])
        bank = [ctx.enter_context(nc.psum_tensor(f"hn_b{i}", [P, HALF], F32)) for i in range(COLS)]
        hn_in, hn_sq, hn_sum, hn_inv, hn_root = (core.sig(n) for n in ("vectors_in", "squares", "rows_psum", "inverses", "rows_copied"))
        dve_steps = core.sig("dve_steps")
        with nc.Block() as block:
            @block.sync
            def _(sp):
                sp.dma_start(gain[:], io["diff_subln_g"].rearrange("a (p e) -> (a p) e", e=1)).then_inc(*hn_in.by(16))

            @block.tensor
            def _(pe):
                for i in range(COLS):
                    pe.wait_ge(*hn_sq.at(i + 1))
                    pe.matmul(bank[i][:], ones[:], sq[:, i * HALF:(i + 1) * HALF]).then_inc(*hn_sum.by())

            @block.scalar
            def _(act):
                for i in range(COLS):
                    act.wait_ge(*hn_inv.at(i + 1))
                    cols = slice(i * HALF, (i + 1) * HALF)
                    act.activation(inv[:, cols], inv[:, cols], ACT.Sqrt).then_inc(*hn_root.by())

            @block.vector
            def _(dve):
                own = in_order(dve, dve_steps)
                own(dve.memset(ones[:], 1.0))
                for i in range(COLS):
                    cols = slice(i * HALF, (i + 1) * HALF)
                    dve.tensor_tensor(sq[:, cols], flat[:, cols], flat[:, cols], ALU.mult).then_inc(*hn_sq.by())
                dve.wait_ge(*hn_in.at(16))
                own(dve.tensor_scalar(gain[:], gain[:], 1.0 - LAM_INIT, None, ALU.mult))
                for i in range(COLS):
                    cols = slice(i * HALF, (i + 1) * HALF)
                    dve.wait_ge(*hn_sum.at(i + 1))
                    own(dve.tensor_scalar(inv[:, cols], bank[i][:], 1.0 / P, SUBLN_EPS, ALU.mult, ALU.add))
                    own(dve.reciprocal(inv[:, cols], inv[:, cols]))
                    dve.sem_inc(*hn_inv.by())
                for i in range(COLS):
                    cols = slice(i * HALF, (i + 1) * HALF)
                    dve.wait_ge(*hn_root.at(i + 1))
                    own(dve.scalar_tensor_tensor(flat[:, cols], flat[:, cols], gain[:, 0:1], inv[:, cols], ALU.mult, ALU.mult))
        core.end_stage()


def attention(core, io):
    nc = core.nc
    with ExitStack() as ctx:
        def sb(name, shape, dt=F32):
            return ctx.enter_context(nc.sbuf_tensor("at_" + name, shape, dt))

        oT, qT, kT = (sb(n, [P, DH, TOK]) for n in ("oT", "qT", "kT"))
        v_tok, neg_lam = sb("v", [P, TILES, D]), sb("neg_lam", [P, 1])
        mixing_weight(core, io, neg_lam)
        with ExitStack() as proj:
            tok = {n: proj.enter_context(nc.sbuf_tensor("at_tok_" + n, [P, TILES, D], F32)) for n in "kq"}
            tok["v"] = v_tok
            xT = proj.enter_context(nc.sbuf_tensor("at_xT", [P, KD, TOK], F32))
            to_features(core, core.x_tok, xT, "at_x")
            attention_projections(core, io, xT, tok)
            to_features(core, tok["k"], kT, "at_k")
            to_features(core, tok["q"], qT, "at_q")
        prompt_attention(core, qT, kT, v_tok, oT, neg_lam)
        sample_attention(core, io, qT, kT, v_tok, oT, neg_lam)
        head_norm(core, io, oT)
        project_and_norm(core, io, oT, io["diff_w_o"][0], 1, "attention")


def store_rows(core, io):
    y_out = core.sig("y_out")
    with core.nc.Block() as block:
        @block.sync
        def _(sp):
            for t in range(TILES):
                sp.dma_start(row_tile(io["y_prompt"], io["y_sample"], t), core.x_tok[:, t, :]).then_inc(*y_out.by(16))
            sp.wait_ge(*y_out.at(16 * TILES))
    core.end_stage()


INS = ["x_prompt", "x_sample", "state_wkv", "state_shift", "cache_k", "cache_v",
       "rwkv_mu", "rwkv_w_rkv", "rwkv_w0", "rwkv_w1", "rwkv_w2", "rwkv_a0", "rwkv_a1", "rwkv_a2",
       "rwkv_g1", "rwkv_g2", "rwkv_k_k", "rwkv_k_a", "rwkv_r_k", "rwkv_lnx_g", "rwkv_lnx_b", "rwkv_w_out",
       "w_kv", "diff_w_q", "diff_lambda", "diff_subln_g", "diff_w_o",
       "ln_mix_g", "ln_mix_b", "ln_ffn_g", "ln_ffn_b",
       "peer_w_query", "peer_sub_keys", "peer_u", "peer_v"]
OUTS = {"y_prompt": (1, SEQ, D), "y_sample": (DEC_BATCH, DEC_SEQ, D),
        "wkv_p": (1, 1, H, N, N), "shift_p": (1, 1, 1, D),
        "cache_k_p": (1, SEQ, DH, 2, DD), "cache_v_p": (1, SEQ, DH, 2 * DD),
        "wkv_s": (1, DEC_BATCH, H, N, N), "shift_s": (1, DEC_BATCH, 1, D),
        "cache_k_s": (DEC_BATCH, DEC_SEQ, DH, 2, DD), "cache_v_s": (DEC_BATCH, DEC_SEQ, DH, 2 * DD)}


def program(nc, io, stages=99):
    with ExitStack() as ctx:
        core = Core(nc, ctx)
        core.where, width = constant_layout()
        core.constants = ctx.enter_context(nc.sbuf_tensor("constants_sb", [P, width], F32))
        core.spill = {n: nc.dram_tensor(f"spill_{n}", [TILES, P, D], F32, kind="Internal").ap() for n in "rkvwag"}
        with ExitStack() as proj:
            buf = {n: proj.enter_context(nc.sbuf_tensor(f"buf_{n}", [P, TILES, D], F32)) for n in "rkvzag"}
            rwkv_projections(core, io, buf)
        if stages == 1:
            return
        with ExitStack() as wkv:
            w = {"carry": wkv.enter_context(nc.sbuf_tensor("carry", [N, H, N], F32))}
            for t in range(TILES):
                with ExitStack() as per_tile:
                    def sb(name, shape):
                        return per_tile.enter_context(nc.sbuf_tensor(f"wkv_{name}_{t}", shape, F32))

                    tile = {n: sb(n, [P, D]) for n in "rkvzag"}
                    for n, shape in {"bonus": [P, D], "y": [P, D], "Y2t": [N, H, P], "Q1t": [N, H, P]}.items():
                        w[n] = sb(n, shape)
                    with ExitStack() as ops:
                        names = ["B", "B_end", "K_end", "e_end"]
                        w["G"], w["Ft"] = sb("G", [N, NCH + 1, H, N]), None
                        for n in names:
                            w[n] = ops.enter_context(nc.sbuf_tensor(f"wkv_{n}_{t}", [P, D], F32))
                        wkv_operands(core, io, tile, w, t)
                        w["Ft"] = ops.enter_context(nc.sbuf_tensor(f"wkv_Ft_{t}", [N, NCH, H, N], F32))
                        wkv_chunks(core, tile, w, t)
                        if t == 2:
                            pass
                        wkv_states_and_outputs(core, io, tile, w, t)
        if stages == 2:
            return
        core.x_tok = ctx.enter_context(nc.sbuf_tensor("x_tok", [P, TILES, D], F32))
        with ExitStack() as rwkv:
            gated = rwkv.enter_context(nc.sbuf_tensor("gated_wkv", [P, TILES, D], F32))
            mixT = rwkv.enter_context(nc.sbuf_tensor("mixT", [P, KD, TOK], F32))
            load_rows(core, io, gated)
            to_features(core, gated, mixT, "rwkv")
            project_and_norm(core, io, mixT, io["rwkv_w_out"][0], 0, "rwkv")
        if stages == 3:
            return
        peer(core, io, 0)
        if stages == 4:
            return
        attention(core, io)
        if stages == 5:
            return
        peer(core, io, 1)
        store_rows(core, io)


def peer(core, io, layer):
    with ExitStack() as ctx:
        scores = ctx.enter_context(core.nc.sbuf_tensor(f"scores_{layer}", [P, TILES, 2 * PH, PK], F32))
        with ExitStack() as feat:
            xT = feat.enter_context(core.nc.sbuf_tensor(f"peer_xT_{layer}", [P, KD, TOK], F32))
            to_features(core, core.x_tok, xT, f"peer{layer}")
            peer_scores(core, io, xT, scores, layer)
        peer_experts(core, io, scores, layer)


def kernel(**inputs):
    import concourse.bacc as bacc
    from concourse.bass_utils import run_bass_kernel_spmd

    nc = bacc.Bacc("TRN2", target_bir_lowering=False, num_devices=1)
    arrays, io = {}, {}
    for name in INS:
        a = np.ascontiguousarray(inputs[name])
        arrays[f"in_{name}"] = a
        io[name] = nc.dram_tensor(f"in_{name}", a.shape, F32, kind="ExternalInput").ap()
    c = shape_constants()
    arrays["in_constants"] = c
    io["constants"] = nc.dram_tensor("in_constants", c.shape, F32, kind="ExternalInput").ap()
    for name, shape in OUTS.items():
        io[name] = nc.dram_tensor(f"out_{name}", shape, F32, kind="ExternalOutput").ap()
    program(nc, io)
    r = run_bass_kernel_spmd(nc, [arrays], core_ids=[0])
    return tuple(r.results[0][f"out_{name}"] for name in OUTS)
```

```python
import math
from contextlib import ExitStack, contextmanager

import numpy as np

import concourse.bass as bass
from concourse import mybir

F32 = mybir.dt.float32
U32 = mybir.dt.uint32
I32 = mybir.dt.int32
ALU = mybir.AluOpType
ACT = mybir.ActivationFunctionType
AX = mybir.AxisListType

P = 128
D = 1024
KD = D // P
HALF = 512
SEQ = 256
DEC_BATCH, DEC_SEQ, PAST = 8, 16, 512
TILES = 3
TOK = TILES * P
L = 16
NCH = P // L
H, N = 16, 64
DH, DD = 8, 64
ROT = DD // 4
PH, PK, PTOP = 8, 128, 16
EXPERTS = PK * PK
SLOTS = PH * PTOP
ALPHA = (2.0 * 2) ** 0.25
LN_EPS, GN_EPS, SUBLN_EPS = 1e-5, 64e-5, 1e-5
DECAY_SCALE = -math.exp(-0.5)
LAM_INIT = 0.8 - 0.6 * math.exp(-0.3 * 1)
FAR = -1e30


def constant_layout():
    widths = [("ident", P), ("strict_incl", 2 * P), ("lower", P), ("block", P), ("chunk", NCH), ("first", NCH),
              ("causal", 3 * P), ("pair_ident", N), ("map0", 1), ("map1", 1), ("sum_maps", DD), ("iota", PTOP), ("cos", TILES * ROT // 2),
              ("sin", TILES * ROT // 2)]
    at, where = 0, {}
    for name, w in widths:
        where[name] = (at, at + w)
        at += w
    return where, at


def shape_constants():
    where, width = constant_layout()
    c = np.zeros((P, width), np.float32)
    row, col = np.arange(P)[:, None], np.arange(P)[None, :]
    same = row // L == col // L

    def put(name, value):
        c[:, where[name][0]:where[name][1]] = value

    put("ident", row == col)
    put("strict_incl", np.concatenate([same & (row < col), same & (row <= col)], 1))
    put("lower", same & (col < row))
    put("block", same)
    put("chunk", row // L == np.arange(NCH)[None, :])
    put("first", row == L * np.arange(NCH)[None, :])
    causal = np.where((row < 64) & (col >= 64), FAR, 0.0)
    put("causal", np.concatenate([causal, np.zeros((P, P)), causal], 1))
    put("pair_ident", row % N == np.arange(N)[None, :])
    second = row // L % 2
    put("map0", 1 - second)
    put("map1", second)
    put("sum_maps", (row // (2 * L) == np.arange(DD)[None, :] // L) & (row % L == np.arange(DD)[None, :] % L))
    put("iota", np.broadcast_to(np.arange(PTOP), (P, PTOP)))
    half = ROT // 2
    inv = np.power(np.float32(500000.0), -np.arange(half, dtype=np.float32) * np.float32(2.0) / np.float32(ROT))
    pos = np.stack([np.arange(P), P + np.arange(P), PAST + np.arange(P) % DEC_SEQ]).astype(np.float32)
    ang = (pos[:, :, None] * inv.astype(np.float32)).astype(np.float32)
    put("cos", np.cos(ang).astype(np.float32).transpose(1, 0, 2).reshape(P, -1))
    put("sin", np.sin(ang).astype(np.float32).transpose(1, 0, 2).reshape(P, -1))
    return c


class Signal:

    def __init__(self, ctx, nc, name):
        self.sem = ctx.enter_context(nc.semaphore(name))
        self.base = 0
        self.made = 0

    def by(self, n=1):
        self.made += n
        return self.sem, n

    def at(self, n):
        return self.sem, self.base + n

    def last(self):
        return self.sem, self.base + self.made

    def new_stage(self):
        self.base += self.made
        self.made = 0


class Core:

    def __init__(self, nc, ctx):
        self.nc, self.ctx = nc, ctx
        self.signals = {}

    def sig(self, name):
        if name not in self.signals:
            self.signals[name] = Signal(self.ctx, self.nc, name)
        return self.signals[name]

    def end_stage(self):
        for s in self.signals.values():
            s.new_stage()

    def const(self, name):
        a, b = self.where[name]
        return self.constants[:, a:b]


@contextmanager
def turns(i, times, counted=(), own=None, per=0):
    before = [s.made for s in counted]
    if own is not None:
        base, made = own.base, own.made
        own.base, own.made = base + made + i * per, 0
    yield
    if own is not None:
        assert own.made == per, own.made
        own.base, own.made = base, made + per * times
    for s, n in zip(counted, before):
        s.made = n + (s.made - n) * times


def in_order(eng, steps):

    def own(ins):
        ins.then_inc(*steps.by())
        eng.wait_ge(*steps.last())

    return own


def row_tile(x_prompt, x_sample, t):
    if t < 2:
        return x_prompt[0, t * P:(t + 1) * P, :]
    return x_sample.rearrange("b s d -> (b s) d")


def by_chunk(w):
    return w.rearrange("(k p) n -> p k n", p=P)


def rwkv_projections(core, io, buf):
    nc = core.nc
    ident = core.const("ident")
    with ExitStack() as ctx:
        def sb(name, shape, dt=F32):
            return ctx.enter_context(nc.sbuf_tensor(name, shape, dt))

        x_tok = sb("x_rows", [P, TILES, D])
        shift_rows = sb("shift_rows", [DEC_BATCH, D])
        mu_rows = sb("mu_rows", [6 * KD, P])
        mu_cols = sb("mu_cols", [P, 6 * KD])
        xT = sb("xT", [P, KD, TOK + DEC_BATCH])
        dxT = sb("dxT", [P, KD, TOK])
        mixed = sb("mixed", [P, 2, KD, TOK])
        RING = 7
        w_ring = sb("w_ring", [P, RING, D])
        lora_in = {"w": sb("w1_sb", [P, KD, 64]), "a": sb("a1_sb", [P, KD, 64]), "g": sb("g1_sb", [P, KD, P])}
        lora_out = {"w": sb("w2_sb", [64, D]), "a": sb("a2_sb", [64, D]), "g": sb("g2_sb", [P, D])}
        lora_bias = {"w": sb("w0_sb", [P, D]), "a": sb("a0_sb", [P, D])}
        hidden = sb("hidden", [P, TOK])
        acc = ctx.enter_context(nc.psum_tensor("acc", [P, 6, HALF], F32))
        aux = ctx.enter_context(nc.psum_tensor("aux", [P, 2, HALF], F32))

        rows_in, xT_psum, xT_done = core.sig("rows_in"), core.sig("rows_psum"), core.sig("rows_copied")
        mu_psum, mu_done = core.sig("mu_psum"), core.sig("mu_done")
        mixed_done, mixed_used = core.sig("mixed_done"), core.sig("mixed_used")
        w_in = [core.sig(f"loaded{i}") for i in range(RING)]
        w_used, acc_full = core.sig("w_used"), core.sig("acc_full")
        free_by = {m: core.sig("acc_free_dve" if m in "wa" else "acc_free_act") for m in "rkvwag"}
        lora_w_in, hid_psum, hid_done = core.sig("lora_w_in"), core.sig("hid_psum"), core.sig("hid_done")
        dve_steps, act_steps = core.sig("dve_steps"), core.sig("act_steps")
        shift_out, spilled = core.sig("shift_out"), core.sig("spilled")

        PLAN = [("r", 0), ("k", 1), ("v", 2), ("w", 3), ("a", 4), ("g", 5)]
        into = {"r": buf["r"], "k": buf["k"], "v": buf["v"], "w": buf["z"], "a": buf["a"], "g": buf["g"]}

        def bank_free(eng, j, b):
            if j > 0:
                m = PLAN[j - 1][0]
                before = sum(free_by[q] is free_by[m] for q, _ in PLAN[:j - 1])
                eng.wait_ge(*free_by[m].at(6 * before + b + 1))

        with nc.Block() as block:
            @block.sync
            def _(sp):
                sp.dma_start(core.constants[:], io["constants"]).then_inc(*rows_in.by(16))
                for t in range(TILES):
                    sp.dma_start(x_tok[:, t, :], row_tile(io["x_prompt"], io["x_sample"], t)).then_inc(*rows_in.by(16))
                sp.dma_start(shift_rows[:], io["state_shift"].rearrange("a b c d -> (a b c) d")).then_inc(*rows_in.by(16))
                sp.dma_start(mu_rows[:], io["rwkv_mu"].rearrange("a i (k p) -> (a i k) p", p=P)).then_inc(*rows_in.by(16))
                n = 0
                for i in range(3):
                    for k in range(KD):
                        if n >= RING:
                            sp.wait_ge(*w_used.at(n - RING + 1))
                        sp.dma_start(w_ring[:, n % RING, :], io["rwkv_w_rkv"][0, i, k * P:(k + 1) * P, :]).then_inc(*w_in[n % RING].by(16))
                        n += 1

            @block.gpsimd
            def _(pool):
                for m, (w1, w2) in {"w": ("rwkv_w1", "rwkv_w2"), "a": ("rwkv_a1", "rwkv_a2"), "g": ("rwkv_g1", "rwkv_g2")}.items():
                    pool.dma_start(lora_in[m][:], by_chunk(io[w1][0])).then_inc(*lora_w_in.by(16))
                    pool.dma_start(lora_out[m][:], io[w2][0]).then_inc(*lora_w_in.by(16))
                for m, w0 in {"w": "rwkv_w0", "a": "rwkv_a0"}.items():
                    pool.dma_start(lora_bias[m][:], io[w0].broadcast_to([P, D])).then_inc(*lora_w_in.by(16))
                pool.dma_start(io["shift_p"].rearrange("a b c d -> (a b c) d"), io["x_prompt"][0, SEQ - 1:SEQ, :]).then_inc(*shift_out.by(16))
                pool.dma_start(io["shift_s"].rearrange("a b c d -> (a b c) d"), io["x_sample"][:, DEC_SEQ - 1, :]).then_inc(*shift_out.by(16))
                for j, (m, _) in enumerate(PLAN):
                    before = sum(free_by[q] is free_by[m] for q, _ in PLAN[:j])
                    pool.wait_ge(*free_by[m].at(6 * (before + 1)))
                    pool.dma_start(core.spill[m].rearrange("t p d -> p t d"), into[m][:]).then_inc(*spilled.by(16))
                pool.wait_ge(*spilled.at(16 * 6))
                pool.wait_ge(*shift_out.at(32))

            @block.tensor
            def _(pe):
                pe.wait_ge(*rows_in.at(96))
                pe.transpose(acc[:, 0, 0:6 * KD], mu_rows[:], ident[0:6 * KD, 0:6 * KD]).then_inc(*mu_psum.by())
                for k in range(KD):
                    if k >= 2:
                        pe.wait_ge(*xT_done.at(k - 1))
                    for t in range(TILES):
                        pe.transpose(aux[:, k % 2, t * P:(t + 1) * P], x_tok[:, t, k * P:(k + 1) * P], ident)
                    pe.transpose(aux[:, k % 2, TOK:TOK + DEC_BATCH], shift_rows[:, k * P:(k + 1) * P],
                                 ident[0:DEC_BATCH, 0:DEC_BATCH]).then_inc(*xT_psum.by())
                n = 0
                pe.wait_ge(*mu_done.at(1))
                for j, (m, _) in enumerate(PLAN):
                    pe.wait_ge(*mixed_done.at(j + 1))
                    xm = mixed[:, j % 2]
                    if j < 3:
                        for k in range(KD):
                            pe.wait_ge(*w_in[n % RING].at(16 * (n // RING + 1)))
                            for t in range(TILES):
                                for h in range(2):
                                    if k == 0:
                                        bank_free(pe, j, 2 * t + h)
                                    mm = pe.matmul(acc[:, 2 * t + h, :], xm[:, k, t * P:(t + 1) * P],
                                                   w_ring[:, n % RING, h * HALF:(h + 1) * HALF],
                                                   start=(k == 0), stop=(k == KD - 1))
                                    if k == KD - 1 and (t, h) != (TILES - 1, 1):
                                        mm.then_inc(*acc_full.by())
                            mm.then_inc(*(w_used.by() if k < KD - 1 else acc_full.by()))
                            n += 1
                        pe.wait_ge(*acc_full.at(6 * (j + 1)))
                        pe.sem_inc(*w_used.by())
                        pe.sem_inc(*mixed_used.by())
                    else:
                        if j == 3:
                            pe.wait_ge(*lora_w_in.at(16 * 8))
                        r = 64 if m != "g" else P
                        for k in range(KD):
                            mm = pe.matmul(aux[0:r, j % 2, 0:TOK], lora_in[m][:, k, :], xm[:, k, :],
                                           start=(k == 0), stop=(k == KD - 1))
                        mm.then_inc(*hid_psum.by())
                        pe.wait_ge(*hid_done.at(j - 2))
                        pe.sem_inc(*mixed_used.by())
                        for t in range(TILES):
                            for h in range(2):
                                bank_free(pe, j, 2 * t + h)
                                pe.matmul(acc[:, 2 * t + h, :], hidden[0:r, t * P:(t + 1) * P],
                                          lora_out[m][:, h * HALF:(h + 1) * HALF]).then_inc(*acc_full.by())

            @block.scalar
            def _(act):
                for k in range(KD):
                    act.wait_ge(*xT_psum.at(k + 1))
                    act.copy(xT[:, k, :], aux[:, k % 2, 0:TOK + DEC_BATCH]).then_inc(*xT_done.by())
                for j, (m, _) in enumerate(PLAN):
                    if j >= 3:
                        r = 64 if m != "g" else P
                        act.wait_ge(*hid_psum.at(j - 2))
                        if j > 3:
                            act.wait_ge(*acc_full.at(6 * j))
                        act.activation(hidden[0:r, :], aux[0:r, j % 2, 0:TOK],
                                       {"w": ACT.Tanh, "a": ACT.Copy, "g": ACT.Sigmoid}[m]).then_inc(*hid_done.by())
                    if m in "rkvg":
                        for b in range(6):
                            act.wait_ge(*acc_full.at(6 * j + b + 1))
                            act.copy(into[m][:, b // 2, (b % 2) * HALF:(b % 2 + 1) * HALF],
                                     acc[:, b, :]).then_inc(*free_by[m].by())

            @block.vector
            def _(dve):
                own = in_order(dve, dve_steps)
                dve.wait_ge(*mu_psum.at(1))
                own(dve.tensor_copy(mu_cols[:], acc[:, 0, 0:6 * KD]))
                dve.sem_inc(*mu_done.by())
                dve.wait_ge(*xT_done.at(KD))
                s_cur = xT[:, :, SEQ:TOK].rearrange("p k (b s) -> p k b s", s=DEC_SEQ)
                s_dx = dxT[:, :, SEQ:TOK].rearrange("p k (b s) -> p k b s", s=DEC_SEQ)
                dve.tensor_tensor(dxT[:, :, 1:SEQ], xT[:, :, 0:SEQ - 1], xT[:, :, 1:SEQ], ALU.subtract)
                dve.tensor_scalar(dxT[:, :, 0:1], xT[:, :, 0:1], -1.0, None, ALU.mult)
                for b in range(DEC_BATCH):
                    dve.tensor_tensor(s_dx[:, :, b, 1:], s_cur[:, :, b, :DEC_SEQ - 1], s_cur[:, :, b, 1:], ALU.subtract)
                own(dve.tensor_tensor(s_dx[:, :, :, 0], xT[:, :, TOK:], s_cur[:, :, :, 0], ALU.subtract))
                for j, (m, i) in enumerate(PLAN):
                    if j >= 2:
                        dve.wait_ge(*mixed_used.at(j - 1))
                    for k in range(KD):
                        ins = dve.scalar_tensor_tensor(mixed[:, j % 2, k, :], dxT[:, k, :],
                                                       mu_cols[:, i * KD + k:i * KD + k + 1],
                                                       xT[:, k, 0:TOK], ALU.mult, ALU.add)
                    ins.then_inc(*mixed_done.by())
                    if j >= 1 and PLAN[j - 1][0] in "wa":
                        if j == 4:
                            dve.wait_ge(*lora_w_in.at(16 * 8))
                        for b in range(6):
                            dve.wait_ge(*acc_full.at(6 * (j - 1) + b + 1))
                            q = PLAN[j - 1][0]
                            dve.tensor_tensor(into[q][:, b // 2, (b % 2) * HALF:(b % 2 + 1) * HALF], acc[:, b, :],
                                              lora_bias[q][:, (b % 2) * HALF:(b % 2 + 1) * HALF],
                                              ALU.add).then_inc(*free_by[q].by())

        core.end_stage()


def wkv_operands(core, io, buf, w, t):
    nc = core.nc
    r, k, v, z, a = (buf[n][:] for n in "rkvza")
    heads = lambda x: x.rearrange("p (h n) -> p h n", n=N)
    with ExitStack() as ctx:
        def sb(name, shape, dt=F32):
            return ctx.enter_context(nc.sbuf_tensor(f"{name}_{t}", shape, dt))

        kk, kka, tmp = sb("kk", [P, D]), sb("kka", [P, D]), sb("tmp", [P, D])
        e_incl, e_neg, e_excl = sb("e_incl", [P, D]), sb("e_neg", [P, D]), sb("e_excl", [P, D])
        norm2, rnorm, bonus_dot = sb("norm2", [P, H]), sb("rnorm", [P, H]), sb("bonus_dot", [P, H])
        run = ctx.enter_context(nc.psum_tensor(f"run_{t}", [P, D], F32))
        end = ctx.enter_context(nc.psum_tensor(f"end_{t}", [P, D], F32))
        vec = {n: sb(n, [P, D]) for n in ("k_k", "k_a", "r_k")}
        loaded = "zakrvg"
        proj_in = [core.sig(f"loaded{i}") for i in range(6)]
        vec_in, gates, logd = core.sig("vectors_in"), core.sig("gates"), core.sig("logd")
        sums, norms, rnorms = core.sig("sums"), core.sig("norms"), core.sig("rnorms")
        excl_arg, exps, dve_steps = core.sig("excl_arg"), core.sig("exps"), core.sig("dve_steps")

        with nc.Block() as block:
            @block.sync
            def _(sp):
                for i, n in enumerate(loaded):
                    sp.dma_start(buf[n][:], core.spill["w" if n == "z" else n][t]).then_inc(*proj_in[i].by(16))
                for name in ("k_k", "k_a"):
                    sp.dma_start(vec[name][:], io["rwkv_" + name].broadcast_to([P, D])).then_inc(*vec_in.by(16))
                sp.dma_start(vec["r_k"][:], io["rwkv_r_k"].rearrange("a h n -> a (h n)").broadcast_to([P, D])).then_inc(*vec_in.by(16))
                sp.wait_ge(*proj_in[loaded.index("g")].at(16))

            @block.scalar
            def _(act):
                act.wait_ge(*proj_in[0].at(16))
                act.activation(z, z, ACT.Sigmoid).then_inc(*gates.by())
                act.wait_ge(*proj_in[1].at(16))
                act.activation(a, a, ACT.Sigmoid).then_inc(*gates.by())
                act.wait_ge(*norms.at(1))
                act.activation(rnorm[:], norm2[:], ACT.Sqrt).then_inc(*rnorms.by())
                act.wait_ge(*sums.at(2))
                act.activation(e_incl[:], run[:], ACT.Exp).then_inc(*exps.by())
                act.activation(e_neg[:], run[:], ACT.Exp, scale=-1.0).then_inc(*exps.by())
                act.activation(w["e_end"][:], end[:], ACT.Exp).then_inc(*exps.by())
                act.wait_ge(*excl_arg.at(1))
                act.activation(e_excl[:], e_excl[:], ACT.Exp).then_inc(*exps.by())

            @block.tensor
            def _(pe):
                pe.wait_ge(*logd.at(1))
                _, incl = core.const("strict_incl")[:, 0:P], core.const("strict_incl")[:, P:]
                for out, ones in ((run, incl), (end, core.const("block"))):
                    for h in range(2):
                        mm = pe.matmul(out[:, h * HALF:(h + 1) * HALF], ones, z[:, h * HALF:(h + 1) * HALF])
                    mm.then_inc(*sums.by())

            @block.vector
            def _(dve):
                own = in_order(dve, dve_steps)
                dve.wait_ge(*gates.at(1))
                own(dve.tensor_scalar(z, z, DECAY_SCALE, None, ALU.mult))
                dve.sem_inc(*logd.by())
                dve.wait_ge(*vec_in.at(48))
                dve.wait_ge(*proj_in[2].at(16))
                own(dve.tensor_tensor(kk[:], k, vec["k_k"][:], ALU.mult))
                own(dve.tensor_tensor(tmp[:], kk[:], kk[:], ALU.mult))
                own(dve.tensor_reduce(norm2[:], heads(tmp[:]), AX.X, ALU.add))
                own(dve.tensor_scalar(norm2[:], norm2[:], 1e-24, None, ALU.max))
                own(dve.reciprocal(norm2[:], norm2[:]))
                dve.sem_inc(*norms.by())
                dve.wait_ge(*gates.at(2))
                own(dve.scalar_tensor_tensor(tmp[:], a, -1.0, vec["k_a"][:], ALU.add, ALU.mult))
                own(dve.scalar_tensor_tensor(k, tmp[:], 1.0, k, ALU.add, ALU.mult))
                dve.wait_ge(*proj_in[3].at(16))
                own(dve.tensor_tensor(tmp[:], r, k, ALU.mult))
                own(dve.tensor_tensor(tmp[:], tmp[:], vec["r_k"][:], ALU.mult))
                own(dve.tensor_reduce(bonus_dot[:], heads(tmp[:]), AX.X, ALU.add))
                dve.wait_ge(*proj_in[4].at(16))
                dve.tensor_tensor(heads(w["bonus"][:]), heads(v), bonus_dot[:].unsqueeze(2).broadcast_to([P, H, N]), ALU.mult)
                dve.wait_ge(*rnorms.at(1))
                own(dve.tensor_tensor(heads(kk[:]), heads(kk[:]), rnorm[:].unsqueeze(2).broadcast_to([P, H, N]), ALU.mult))
                own(dve.tensor_tensor(kka[:], kk[:], a, ALU.mult))
                dve.wait_ge(*exps.at(2))
                own(dve.tensor_tensor(e_excl[:], run[:], z, ALU.subtract))
                dve.sem_inc(*excl_arg.by())
                dve.wait_ge(*exps.at(3))
                dve.tensor_tensor(r, r, e_incl[:], ALU.mult)
                own(dve.scalar_tensor_tensor(w["B"][:], kka[:], -1.0, e_neg[:], ALU.mult, ALU.mult))
                own(dve.tensor_tensor(k, k, e_neg[:], ALU.mult))
                dve.tensor_tensor(w["B_end"][:], w["B"][:], w["e_end"][:], ALU.mult)
                dve.tensor_tensor(w["K_end"][:], k, w["e_end"][:], ALU.mult)
                dve.wait_ge(*exps.at(4))
                own(dve.tensor_tensor(a, kk[:], e_excl[:], ALU.mult))
        core.end_stage()


def wkv_chunks(core, buf, w, t):
    nc = core.nc
    GH, GP = 4, 2
    ident = core.const("ident")
    token = {"A": buf["a"], "R": buf["r"], "B": w["B"], "K": buf["k"]}
    v = buf["v"]
    with ExitStack() as ctx:
        def sb(name, shape, dt=F32):
            return ctx.enter_context(nc.sbuf_tensor(f"{name}_{t}", shape, dt))

        feat = sb("feat", [P, GP, 4, P])
        by_b = sb("by_b", [P, GH, 2 * P])
        by_k = sb("by_k", [P, GH, 2 * P])
        m1 = sb("m1", [P, GH, P])
        m2, m2t, m4, m4t, m8t = (sb(n, [P, GH, P]) for n in ("m2", "m2t", "m4", "m4t", "m8t"))
        x = sb("x", [P, 2, GH, 2 * N])
        B_by_chunk, K_by_chunk = sb("B_by_chunk", [P, GH, NCH, N]), sb("K_by_chunk", [P, GH, NCH, N])
        p_end = sb("p_end", [P, GP, NCH])
        decay_diag = sb("decay_diag", [P, GP, NCH, N])
        bank = [ctx.enter_context(nc.psum_tensor(f"bank{i}_{t}", [P, HALF], F32)) for i in range(8)]

        tp, feat_done = core.sig("tp"), core.sig("feat_done")
        gram, gram_done = core.sig("gram"), core.sig("gram_done")
        nv, x_done, pw, pw_done = core.sig("nv"), core.sig("x_done"), core.sig("pw"), core.sig("pw_done")
        xp, q1, q1_done, y2, y2_done = core.sig("xp"), core.sig("q1"), core.sig("q1_done"), core.sig("y2"), core.sig("y2_done")
        pend_done, diag_done, exp_done = core.sig("pend_done"), core.sig("diag_done"), core.sig("exp_done")
        fp, fp_done, gp, gp_done = core.sig("fp"), core.sig("fp_done"), core.sig("gp"), core.sig("gp_done")
        a_copied = core.sig("a_copied")
        NG = H // GH
        quad = lambda b, n: b[:, 0:GH * n].rearrange("p (h n) -> p h n", h=GH)
        pairs = lambda b: b[:, 0:GP * P].rearrange("p (q t) -> p q t", q=GP)
        half = lambda h: slice(h % 2 * N, (h % 2 + 1) * N)

        with nc.Block() as block:
            @block.tensor
            def _(pe):
                for g in range(NG):
                    if g > 0:
                        pe.wait_ge(*gp_done.at(GP * g))
                        pe.wait_ge(*fp_done.at(GP * g))
                        pe.wait_ge(*q1_done.at(g))
                        pe.wait_ge(*x_done.at(5 * g))
                    for q in range(GP):
                        qc = slice((g * GP + q) * P, (g * GP + q + 1) * P)
                        for i, n in enumerate("ARBK"):
                            mm = pe.transpose(bank[q][:, i * P:(i + 1) * P], token[n][:, qc], ident)
                        mm.then_inc(*tp.by())
                    for h in range(GH):
                        q, rows = h // 2, half(h)
                        pe.wait_ge(*feat_done.at(GP * g + q + 1))
                        if g > 0 and h == 0:
                            pe.wait_ge(*y2_done.at(g))
                        ar = feat[rows, q, 0:2, :].rearrange("k i t -> k (i t)")
                        pe.matmul(bank[4 + h % 2][:, q * 2 * P:(q + 1) * 2 * P], feat[rows, q, 2, :], ar)
                        mm = pe.matmul(bank[6 + h % 2][:, q * 2 * P:(q + 1) * 2 * P], feat[rows, q, 3, :], ar)
                        if q == GP - 1:
                            mm.then_inc(*gram.by())
                    for h in range(GH):
                        mm = pe.matmul(bank[h % 2][:, h // 2 * P:(h // 2 + 1) * P], feat[half(h), h // 2, 0, :], feat[half(h), h // 2, 2, :])
                        if h // 2 == GP - 1:
                            mm.then_inc(*gram.by())
                    pe.wait_ge(*gram_done.at(6 * g + 6))
                    for h in range(GH):
                        hc = slice((g * GH + h) * N, (g * GH + h + 1) * N)
                        pe.matmul(bank[1][:, h * N:(h + 1) * N], by_k[:, h, 0:P], v[:, hc])
                    for q in range(GP):
                        qc = slice((g * GP + q) * P, (g * GP + q + 1) * P)
                        mm = pe.matmul(bank[1][:, GH * N + q * NCH:GH * N + (q + 1) * NCH], w["e_end"][:, qc], core.const("first"))
                    mm.then_inc(*nv.by())
                    for h in range(GH):
                        mm = pe.matmul(bank[2][:, h * P:(h + 1) * P], m1[:, h, :], by_b[:, h, 0:P])
                    mm.then_inc(*pw.by())
                    for h in range(GH):
                        mm = pe.matmul(bank[3][:, h * P:(h + 1) * P], by_b[:, h, 0:P], m1[:, h, :])
                    mm.then_inc(*pw.by())
                    pe.wait_ge(*x_done.at(5 * g + 1))
                    for h in range(GH):
                        mm = pe.matmul(bank[4][:, h * P:(h + 1) * P], by_b[:, h, 0:P], x[:, 0, h, :])
                    mm.then_inc(*xp.by())
                    pe.wait_ge(*pw_done.at(5 * g + 2))
                    for h in range(GH):
                        mm = pe.matmul(bank[5][:, h * P:(h + 1) * P], m2[:, h, :], m2t[:, h, :])
                    mm.then_inc(*pw.by())
                    for h in range(GH):
                        mm = pe.matmul(bank[6][:, h * P:(h + 1) * P], m2t[:, h, :], m2[:, h, :])
                    mm.then_inc(*pw.by())
                    pe.wait_ge(*x_done.at(5 * g + 2))
                    for h in range(GH):
                        mm = pe.matmul(bank[7][:, h * P:(h + 1) * P], m2t[:, h, :], x[:, 1, h, :])
                    mm.then_inc(*xp.by())
                    pe.wait_ge(*pw_done.at(5 * g + 4))
                    for h in range(GH):
                        mm = pe.matmul(bank[0][:, h * P:(h + 1) * P], m4[:, h, :], m4t[:, h, :])
                    mm.then_inc(*pw.by())
                    pe.wait_ge(*x_done.at(5 * g + 3))
                    for h in range(GH):
                        mm = pe.matmul(bank[1][:, h * P:(h + 1) * P], m4t[:, h, :], x[:, 0, h, :])
                    mm.then_inc(*xp.by())
                    pe.wait_ge(*pw_done.at(5 * g + 5))
                    pe.wait_ge(*x_done.at(5 * g + 4))
                    for h in range(GH):
                        mm = pe.matmul(bank[2][:, h * P:(h + 1) * P], m8t[:, h, :], x[:, 1, h, :])
                    mm.then_inc(*xp.by())
                    pe.wait_ge(*x_done.at(5 * g + 5))
                    for h in range(GH):
                        mm = pe.matmul(bank[3][half(h), h // 2 * P:(h // 2 + 1) * P], x[:, 0, h, 0:N], by_b[:, h, P:], tile_position=(0, h % 2 * N))
                    mm.then_inc(*q1.by())
                    for h in range(GH):
                        hc = slice((g * GH + h) * N, (g * GH + h + 1) * N)
                        out = bank[4][half(h), h // 2 * P:(h // 2 + 1) * P]
                        pe.matmul(out, x[:, 0, h, N:], by_b[:, h, P:], start=True, stop=False, tile_position=(0, h % 2 * N))
                        mm = pe.matmul(out, v[:, hc], by_k[:, h, P:], start=False, stop=True, tile_position=(0, h % 2 * N))
                    mm.then_inc(*y2.by())
                    pe.wait_ge(*exp_done.at(2 * GH * (g + 1)))
                    for q in range(GP):
                        f, gg = bank[(5, 7)[q]], bank[(6, 0)[q]]
                        for h in (2 * q, 2 * q + 1):
                            mm = pe.matmul(f[half(h), :], x[:, 0, h, 0:N], B_by_chunk[:, h].rearrange("p c n -> p (c n)"), tile_position=(0, h % 2 * N))
                        mm.then_inc(*fp.by())
                        for c in range(NCH):
                            for h in (2 * q, 2 * q + 1):
                                hc = slice((g * GH + h) * N, (g * GH + h + 1) * N)
                                out = gg[half(h), c * N:(c + 1) * N]
                                pe.matmul(out, B_by_chunk[:, h, c, :], x[:, 0, h, N:], start=True, stop=False, tile_position=(0, h % 2 * N))
                                mm = pe.matmul(out, K_by_chunk[:, h, c, :], v[:, hc], start=False, stop=True, tile_position=(0, h % 2 * N))
                        mm.then_inc(*gp.by())

            @block.scalar
            def _(act):
                for g in range(NG):
                    for q in range(GP):
                        act.wait_ge(*tp.at(GP * g + q + 1))
                        if g > 0 and q == 0:
                            act.wait_ge(*q1_done.at(g))
                        act.copy(feat[:, q].rearrange("k i t -> k (i t)"), bank[q][:]).then_inc(*feat_done.by())
                    for i, (dst, b) in enumerate(((m2t, 2), (m2, 3), (m4t, 5), (m4, 6), (m8t, 0))):
                        act.wait_ge(*pw.at(5 * g + i + 1))
                        act.copy(dst[:], quad(bank[b], P)).then_inc(*pw_done.by())
                    act.wait_ge(*y2.at(g + 1))
                    act.copy(w["Y2t"][:, g * GP:(g + 1) * GP, :], pairs(bank[4])).then_inc(*y2_done.by())
                    for q in range(GP):
                        act.wait_ge(*gp.at(GP * g + q + 1))
                        act.copy(w["G"][:, 1:, g * GP + q, :], bank[(6, 0)[q]].rearrange("k (c n) -> k c n", n=N)).then_inc(*gp_done.by())

            @block.vector
            def _(dve):
                both = core.const("strict_incl").unsqueeze(1).broadcast_to([P, 2, 2 * P])
                for g in range(NG):
                    for r in range(2):
                        dve.wait_ge(*gram.at(4 * g + r + 1))
                        if g > 0 and r == 0:
                            dve.wait_ge(*y2.at(g))
                        for dst, b in ((by_b, 4), (by_k, 6)):
                            dve.tensor_tensor(dst[:].rearrange("p (q r) s -> p q r s", r=2)[:, :, r, :], bank[b + r].rearrange("p (q s) -> p q s", q=GP),
                                              both, ALU.mult).then_inc(*gram_done.by())
                    for r in range(2):
                        dve.wait_ge(*gram.at(4 * g + r + 3))
                        dve.tensor_tensor(m1[:].rearrange("p (q r) s -> p q r s", r=2)[:, :, r, :], pairs(bank[r]),
                                          core.const("lower").unsqueeze(1).broadcast_to([P, GP, P]), ALU.mult).then_inc(*gram_done.by())
                    dve.wait_ge(*a_copied.at(g + 1))
                    dve.wait_ge(*nv.at(g + 1))
                    dve.tensor_copy(x[:, 0, :, N:], quad(bank[1], N)).then_inc(*x_done.by())
                    if g > 0:
                        dve.wait_ge(*diag_done.at(g))
                    dve.tensor_copy(p_end[:].rearrange("k h c -> k (h c)"), bank[1][:, GH * N:GH * N + GP * NCH]).then_inc(*pend_done.by())
                    for i, b in enumerate((4, 7, 1, 2)):
                        dve.wait_ge(*xp.at(4 * g + i + 1))
                        dve.wait_ge(*x_done.at(5 * g + i + 1))
                        dve.tensor_tensor(x[:, (i + 1) % 2], quad(bank[b], P), x[:, i % 2], ALU.add).then_inc(*x_done.by())
                    dve.wait_ge(*q1.at(g + 1))
                    dve.tensor_tensor(w["Q1t"][:, g * GP:(g + 1) * GP, :], pairs(bank[3]), feat[:, :, 1, :], ALU.add).then_inc(*q1_done.by())
                    dve.wait_ge(*diag_done.at(g + 1))
                    for q in range(GP):
                        dve.wait_ge(*fp.at(GP * g + q + 1))
                        dve.tensor_tensor(w["Ft"][:, :, g * GP + q, :], bank[(5, 7)[q]].rearrange("k (c n) -> k c n", n=N), decay_diag[:, q], ALU.add).then_inc(*fp_done.by())

            @block.gpsimd
            def _(pool):
                spread = core.const("chunk").unsqueeze(2).broadcast_to([P, NCH, N])
                for g in range(NG):
                    gc = slice(g * GH * N, (g + 1) * GH * N)
                    if g > 0:
                        pool.wait_ge(*gp.at(GP * g))
                    pool.tensor_copy(x[:, 0, :, 0:N], token["A"][:, gc].rearrange("p (h n) -> p h n", n=N)).then_inc(*a_copied.by())
                    for h in range(GH):
                        hc = slice((g * GH + h) * N, (g * GH + h + 1) * N)
                        for dst, src in ((B_by_chunk, w["B_end"]), (K_by_chunk, w["K_end"])):
                            pool.tensor_tensor(dst[:, h], src[:, hc].unsqueeze(1).broadcast_to([P, NCH, N]), spread, ALU.mult).then_inc(*exp_done.by())
                    pool.wait_ge(*pend_done.at(g + 1))
                    if g > 0:
                        pool.wait_ge(*fp_done.at(GP * g))
                    for q in range(GP):
                        ins = pool.tensor_tensor(decay_diag[:, q], core.const("pair_ident").unsqueeze(1).broadcast_to([P, NCH, N]),
                                                 p_end[:, q, :].unsqueeze(2).broadcast_to([P, NCH, N]), ALU.mult)
                    ins.then_inc(*diag_done.by())
        core.end_stage()


def wkv_states(core, io, buf, w, t):
    nc = core.nc
    ident = core.const("ident")
    G, Ft, carry = w["G"], w["Ft"], w["carry"]
    sample = t == 2
    St = w["start"] if sample else G
    PAIRS, PH2 = H // 2, H // 4
    by_value = lambda s: s.rearrange("h v k -> v h k")
    half = lambda r: slice(r * N, (r + 1) * N)
    with ExitStack() as ctx:
        def sb(name, shape, dt=F32):
            return ctx.enter_context(nc.sbuf_tensor(f"{name}_{t}", shape, dt))

        natural = sb("natural", [N, 1 if not sample else DEC_BATCH, H, N])
        Yt = sb("Yt", [P, PAIRS, P])
        bank = [ctx.enter_context(nc.psum_tensor(f"sbank{i}_{t}", [P, HALF], F32)) for i in range(8)]
        state_in, s_psum, s_done = core.sig("vectors_in"), core.sig("s_psum"), core.sig("s_done")
        step_psum, step_done = core.sig("step_psum"), core.sig("step_done")
        y_psum, y_sum, y_tok, y_tok_done = core.sig("rows_psum"), core.sig("rows_copied"), core.sig("y_tok"), core.sig("y_tok_done")
        fin_psum, fin_done, fin_out = core.sig("fin_psum"), core.sig("fin_done"), core.sig("fin_out")
        first = core.sig("first_state")
        finals = range(DEC_BATCH) if sample else range(1) if t == 1 else ()

        with nc.Block() as block:
            if sample:
                @block.sync
                def _(sp):
                    for b in range(DEC_BATCH):
                        sp.dma_start(natural[:, b], by_value(io["state_wkv"][0, b])).then_inc(*state_in.by(16))
                    for b in range(DEC_BATCH):
                        sp.wait_ge(*fin_done.at(2 * b + 2))
                        sp.dma_start(by_value(io["wkv_s"][0, b]), natural[:, b]).then_inc(*fin_out.by(16))
                    sp.wait_ge(*fin_out.at(16 * DEC_BATCH))
            elif t == 1:
                @block.sync
                def _(sp):
                    sp.wait_ge(*fin_done.at(2))
                    sp.dma_start(by_value(io["wkv_p"][0, 0]), natural[:, 0]).then_inc(*fin_out.by(16))
                    sp.wait_ge(*fin_out.at(16))

            @block.tensor
            def _(pe):
                def step(c, part):
                    for i in range(PH2):
                        for r in range(2):
                            mm = pe.matmul(bank[2 * (c % 2) + part][half(r), i * N:(i + 1) * N], Ft[half(r), c, PH2 * part + i, :],
                                           St[half(r), c, PH2 * part + i, :], tile_position=(r * N, r * N))
                    mm.then_inc(*step_psum.by())

                def outputs(part):
                    for i in range(PH2):
                        for c in range(NCH):
                            for r in range(2):
                                mm = pe.matmul(bank[4 + part][half(r), i * P + c * L:i * P + (c + 1) * L], St[half(r), c, PH2 * part + i, :],
                                               w["Q1t"][half(r), PH2 * part + i, c * L:(c + 1) * L], tile_position=(r * N, r * N))
                    mm.then_inc(*y_psum.by())

                if sample:
                    pe.wait_ge(*state_in.at(16 * DEC_BATCH))
                    for b in range(DEC_BATCH):
                        if b >= 2:
                            pe.wait_ge(*s_done.at(b - 1))
                        for q in range(PAIRS):
                            mm = pe.transpose(bank[6 + b % 2][:, q * N:(q + 1) * N], natural[:, b, 2 * q:2 * q + 2, :].rearrange("v r k -> v (r k)"), ident[0:N, 0:N])
                        mm.then_inc(*s_psum.by())
                    pe.wait_ge(*s_done.at(DEC_BATCH))
                else:
                    pe.wait_ge(*first.at(1))
                for c in range(NCH):
                    for part in range(2):
                        if c > 0 and not sample:
                            pe.wait_ge(*step_done.at(2 * c - 1 + part))
                        elif c > 1:
                            pe.wait_ge(*step_done.at(2 * c - 3 + part))
                        step(c, part)
                for part in range(2):
                    if not sample:
                        pe.wait_ge(*step_done.at(2 * NCH - 3 + part))
                    outputs(part)
                pe.wait_ge(*step_done.at(2 * NCH))
                for part in range(2):
                    pe.wait_ge(*y_sum.at(part + 1))
                    for i in range(PH2):
                        mm = pe.transpose(bank[part][:, i * P:(i + 1) * P], Yt[:, PH2 * part + i, :], ident)
                    mm.then_inc(*y_tok.by())
                for b in finals:
                    for part in range(2):
                        n = 2 * b + part
                        if n >= 2:
                            pe.wait_ge(*fin_done.at(n - 1))
                        for i in range(PH2):
                            src = G[:, b + 1 if sample else NCH, PH2 * part + i, :]
                            mm = pe.transpose(bank[2 + n % 2][0:N, i * P:(i + 1) * P], src, ident)
                        mm.then_inc(*fin_psum.by())

            @block.vector
            def _(dve):
                if t == 0:
                    dve.memset(St[:, 0], 0.0).then_inc(*first.by())
                elif t == 1:
                    dve.tensor_copy(St[:, 0], carry[:]).then_inc(*first.by())
                for c in range(NCH):
                    for part in range(2):
                        dve.wait_ge(*step_psum.at(2 * c + part + 1))
                        dst = G[:, c + 1, PH2 * part:PH2 * (part + 1), :]
                        dve.tensor_tensor(dst, bank[2 * (c % 2) + part][:, 0:PH2 * N].rearrange("k (q v) -> k q v", v=N), dst, ALU.add).then_inc(*step_done.by())
                if t == 0:
                    dve.wait_ge(*step_done.at(2 * NCH))
                    dve.tensor_copy(carry[:], G[:, NCH])
                for part in range(2):
                    dve.wait_ge(*y_psum.at(part + 1))
                    qs = slice(PH2 * part, PH2 * (part + 1))
                    dve.tensor_tensor(Yt[:, qs, :], bank[4 + part][:].rearrange("k (q t) -> k q t", t=P), w["Y2t"][:, qs, :], ALU.add).then_inc(*y_sum.by())

            @block.scalar
            def _(act):
                if sample:
                    for b in range(DEC_BATCH):
                        act.wait_ge(*s_psum.at(b + 1))
                        act.copy(St[:, b], bank[6 + b % 2].rearrange("k (q v) -> k q v", v=N)).then_inc(*s_done.by())
                for part in range(2):
                    act.wait_ge(*y_tok.at(part + 1))
                    act.copy(w["y"][:, part * HALF:(part + 1) * HALF], bank[part][:]).then_inc(*y_tok_done.by())
                for b in finals:
                    for part in range(2):
                        n = 2 * b + part
                        act.wait_ge(*fin_psum.at(n + 1))
                        act.copy(natural[:, b, 8 * part:8 * part + 8, :].rearrange("v h k -> v (h k)"), bank[2 + n % 2][0:N, :]).then_inc(*fin_done.by())
        core.end_stage()


def wkv_states_and_outputs(core, io, buf, w, t):
    with ExitStack() as ctx:
        if t == 2:
            w["start"] = ctx.enter_context(core.nc.sbuf_tensor("wkv_start", [P, NCH, H // 2, N], F32))
        wkv_states(core, io, buf, w, t)
    wkv_outputs(core, io, buf, w, t)


def load_rows(core, io, gated):
    rows_back = core.sig("rows_back")
    with core.nc.Block() as block:
        @block.sync
        def _(sp):
            for t in range(TILES):
                sp.dma_start(core.x_tok[:, t, :], row_tile(io["x_prompt"], io["x_sample"], t)).then_inc(*rows_back.by(16))
            sp.dma_start(gated[:], core.spill["g"].rearrange("t p d -> p t d")).then_inc(*rows_back.by(16))
            sp.wait_ge(*rows_back.at(16 * (TILES + 1)))
    core.end_stage()


def wkv_outputs(core, io, buf, w, t):
    nc = core.nc
    y, gate = w["y"], buf["g"][:]
    heads = lambda x: x.rearrange("p (h n) -> p h n", n=N)
    wide = lambda x: x[:].unsqueeze(2).broadcast_to([P, H, N])
    with ExitStack() as ctx:
        def sb(name, shape, dt=F32):
            return ctx.enter_context(nc.sbuf_tensor(f"{name}_{t}", shape, dt))

        sq, mean, var, rstd = sb("sq", [P, D]), sb("mean", [P, H]), sb("var", [P, H]), sb("rstd", [P, H])
        lnx_g, lnx_b = sb("lnx_g", [P, D]), sb("lnx_b", [P, D])
        gated, gated_out = core.sig("gated"), core.sig("gated_out")
        lnx_in, var_done, rstd_done, dve_steps = core.sig("vectors_in"), core.sig("var_done"), core.sig("rstd_done"), core.sig("dve_steps")
        with nc.Block() as block:
            @block.sync
            def _(sp):
                sp.dma_start(lnx_g[:], io["rwkv_lnx_g"].broadcast_to([P, D])).then_inc(*lnx_in.by(16))
                sp.dma_start(lnx_b[:], io["rwkv_lnx_b"].broadcast_to([P, D])).then_inc(*lnx_in.by(16))
                sp.wait_ge(*gated.at(1))
                sp.dma_start(core.spill["g"][t], gate).then_inc(*gated_out.by(16))
                sp.wait_ge(*gated_out.at(16))

            @block.scalar
            def _(act):
                act.wait_ge(*var_done.at(1))
                act.activation(rstd[:], var[:], ACT.Sqrt).then_inc(*rstd_done.by())

            @block.vector
            def _(dve):
                own = in_order(dve, dve_steps)
                own(dve.tensor_reduce(mean[:], heads(y[:]), AX.X, ALU.add))
                own(dve.tensor_scalar(mean[:], mean[:], 1.0 / N, None, ALU.mult))
                own(dve.tensor_tensor(heads(y[:]), heads(y[:]), wide(mean), ALU.subtract))
                own(dve.tensor_tensor(sq[:], y[:], y[:], ALU.mult))
                own(dve.tensor_reduce(var[:], heads(sq[:]), AX.X, ALU.add))
                own(dve.tensor_scalar(var[:], var[:], 1.0 / N, GN_EPS, ALU.mult, ALU.add))
                own(dve.reciprocal(var[:], var[:]))
                dve.sem_inc(*var_done.by())
                dve.wait_ge(*lnx_in.at(32))
                dve.wait_ge(*rstd_done.at(1))
                own(dve.tensor_tensor(heads(y[:]), heads(y[:]), wide(rstd), ALU.mult))
                own(dve.tensor_tensor(y[:], y[:], lnx_g[:], ALU.mult))
                own(dve.tensor_tensor(y[:], y[:], lnx_b[:], ALU.add))
                own(dve.tensor_tensor(y[:], y[:], w["bonus"][:], ALU.add))
                dve.tensor_tensor(gate, y[:], gate, ALU.mult).then_inc(*gated.by())
        core.end_stage()


def to_features(core, src, dst, name):
    nc = core.nc
    with ExitStack() as ctx:
        bank = [ctx.enter_context(nc.psum_tensor(f"tf{i}_{name}", [P, TOK], F32)) for i in range(4)]
        tf_psum, tf_act, tf_dve = core.sig("rows_psum"), core.sig("copied_act"), core.sig("copied_dve")
        with nc.Block() as block:
            @block.tensor
            def _(pe):
                for k in range(KD):
                    if k >= 4:
                        pe.wait_ge(*(tf_act, tf_dve)[k % 2].at((k - 4) // 2 + 1))
                    for t in range(TILES):
                        mm = pe.transpose(bank[k % 4][:, t * P:(t + 1) * P], src[:, t, k * P:(k + 1) * P], core.const("ident"))
                    mm.then_inc(*tf_psum.by())

            @block.scalar
            def _(act):
                for k in range(0, KD, 2):
                    act.wait_ge(*tf_psum.at(k + 1))
                    act.copy(dst[:, k, :], bank[k % 4][:]).then_inc(*tf_act.by())

            @block.vector
            def _(dve):
                for k in range(1, KD, 2):
                    dve.wait_ge(*tf_psum.at(k + 1))
                    dve.tensor_copy(dst[:, k, :], bank[k % 4][:]).then_inc(*tf_dve.by())
        core.end_stage()


def layer_norm_steps(core, dve, own, res, out, g, b, stats, mv, rstd, n):
    for half in range(2):
        ins = dve.bn_stats(stats[:, half, :], res[:, half * HALF:(half + 1) * HALF])
    own(ins)
    own(dve.bn_aggr(mv[:], stats[:].rearrange("p a s -> p (a s)")))
    own(dve.tensor_scalar(mv[:, 1:2], mv[:, 1:2], LN_EPS, None, ALU.add))
    own(dve.reciprocal(mv[:, 1:2], mv[:, 1:2]))
    dve.sem_inc(*core.sig("ln_var").by())
    dve.wait_ge(*core.sig("ln_rstd").at(n))
    own(dve.tensor_scalar(res, res, mv[:, 0:1], rstd[:], ALU.subtract, ALU.mult))
    own(dve.tensor_tensor(res, res, g, ALU.mult))
    own(dve.tensor_tensor(out, res, b, ALU.add))


def layer_norm_roots(core, act, mv, rstd):
    for t in range(TILES):
        act.wait_ge(*core.sig("ln_var").at(t + 1))
        act.activation(rstd[:], mv[:, 1:2], ACT.Sqrt).then_inc(*core.sig("ln_rstd").by())


def project_and_norm(core, io, actT, weight, layer, name):
    nc = core.nc
    with ExitStack() as ctx:
        def sb(name_, shape, dt=F32):
            return ctx.enter_context(nc.sbuf_tensor(f"{name_}_{name}", shape, dt))

        wt = sb("pn_w", [P, KD, D])
        g, b = sb("pn_g", [P, D]), sb("pn_b", [P, D])
        res = sb("pn_res", [P, 2, D])
        stats, mv, rstd = sb("pn_stats", [P, 2, 6]), sb("pn_mv", [P, 2]), sb("pn_rstd", [P, 1])
        acc = ctx.enter_context(nc.psum_tensor(f"pn_acc_{name}", [P, TILES, D], F32))
        pn_w = [core.sig(f"loaded{k}") for k in range(KD)]
        pn_vec, pn_psum, dve_steps = core.sig("vectors_in"), core.sig("rows_psum"), core.sig("dve_steps")
        core.sig("ln_var"), core.sig("ln_rstd")
        with nc.Block() as block:
            @block.sync
            def _(sp):
                for k in range(KD):
                    sp.dma_start(wt[:, k, :], weight[k * P:(k + 1) * P, :]).then_inc(*pn_w[k].by(16))
                sp.dma_start(g[:], io["ln_mix_g"][layer:layer + 1, :].broadcast_to([P, D])).then_inc(*pn_vec.by(16))
                sp.dma_start(b[:], io["ln_mix_b"][layer:layer + 1, :].broadcast_to([P, D])).then_inc(*pn_vec.by(16))

            @block.tensor
            def _(pe):
                for t in range(TILES):
                    for k in range(KD):
                        if t == 0:
                            pe.wait_ge(*pn_w[k].at(16))
                        for h in range(2):
                            mm = pe.matmul(acc[:, t, h * HALF:(h + 1) * HALF], actT[:, k, t * P:(t + 1) * P],
                                           wt[:, k, h * HALF:(h + 1) * HALF], start=(k == 0), stop=(k == KD - 1))
                    mm.then_inc(*pn_psum.by())

            @block.scalar
            def _(act):
                layer_norm_roots(core, act, mv, rstd)

            @block.vector
            def _(dve):
                own = in_order(dve, dve_steps)
                dve.wait_ge(*pn_vec.at(32))
                for t in range(TILES):
                    dve.wait_ge(*pn_psum.at(t + 1))
                    x = core.x_tok[:, t, :]
                    own(dve.scalar_tensor_tensor(res[:, t % 2], x, ALPHA, acc[:, t, :], ALU.mult, ALU.add))
                    layer_norm_steps(core, dve, own, res[:, t % 2], x, g[:], b[:], stats, mv, rstd, t + 1)
        core.end_stage()


def peer_scores(core, io, xT, scores, layer):
    nc = core.nc
    HC = 2 * PH
    with ExitStack() as ctx:
        def sb(name, shape, dt=F32):
            return ctx.enter_context(nc.sbuf_tensor(f"{name}_{layer}", shape, dt))

        RING, PAIR = 4, 2 * P
        wq = sb("wq", [P, RING, KD, PAIR])
        keys, keysT = sb("keys", [P, 2, P]), sb("keysT", [P, 2, P])
        qT = sb("qT", [P, HC, TOK])
        bank = [ctx.enter_context(nc.psum_tensor(f"pbank{i}_{layer}", [P, HALF], F32)) for i in range(8)]
        wq_in = [core.sig(f"loaded{i}") for i in range(RING)]
        keys_in, keys_psum, keys_done = core.sig("vectors_in"), core.sig("keysT_psum"), core.sig("keys_done")
        q_psum, q_done, s_psum, s_done = core.sig("rows_psum"), core.sig("rows_copied"), core.sig("s_psum"), core.sig("ps_done")

        with nc.Block() as block:
            @block.sync
            def _(sp):
                sp.dma_start(keys[:], io["peer_sub_keys"][layer].rearrange("c k d -> k c d")).then_inc(*keys_in.by(16))
                for i in range(PH):
                    if i >= RING:
                        sp.wait_ge(*q_psum.at(2 * (i - RING) + 2))
                    sp.dma_start(wq[:, i % RING], by_chunk(io["peer_w_query"][layer][:, i * PAIR:(i + 1) * PAIR])).then_inc(*wq_in[i % RING].by(16))

            @block.tensor
            def _(pe):
                pe.wait_ge(*keys_in.at(16))
                for c in range(2):
                    mm = pe.transpose(bank[7][:, c * P:(c + 1) * P], keys[:, c, :], core.const("ident"))
                mm.then_inc(*keys_psum.by())
                for m in range(HC):
                    if m % 2 == 0:
                        pe.wait_ge(*wq_in[m // 2 % RING].at(16 * (m // 2 // RING + 1)))
                    if m >= 3:
                        pe.wait_ge(*q_done.at(m - 2))
                    for k in range(KD):
                        mm = pe.matmul(bank[m % 3][:, 0:TOK], wq[:, m // 2 % RING, k, (m % 2) * P:(m % 2 + 1) * P],
                                       xT[:, k, :], start=(k == 0), stop=(k == KD - 1))
                    mm.then_inc(*q_psum.by())
                pe.wait_ge(*keys_done.at(1))
                pe.wait_ge(*q_done.at(HC))
                n = 0
                for t in range(TILES):
                    for q in range(HC // 4):
                        if n >= 4:
                            pe.wait_ge(*s_done.at(n - 3))
                        for m in range(4 * q, 4 * q + 4):
                            mm = pe.matmul(bank[3 + n % 4][:, (m % 4) * P:(m % 4 + 1) * P], qT[:, m, t * P:(t + 1) * P], keysT[:, m % 2, :])
                        mm.then_inc(*s_psum.by())
                        n += 1

            @block.scalar
            def _(act):
                act.wait_ge(*keys_psum.at(1))
                act.copy(keysT[:].rearrange("p c k -> p (c k)"), bank[7][:, 0:2 * P]).then_inc(*keys_done.by())
                for m in range(HC):
                    act.wait_ge(*q_psum.at(m + 1))
                    act.copy(qT[:, m, :], bank[m % 3][:, 0:TOK]).then_inc(*q_done.by())
                for n in range(TILES * HC // 4):
                    act.wait_ge(*s_psum.at(n + 1))
                    act.copy(scores[:, n // 4, 4 * (n % 4):4 * (n % 4) + 4, :].rearrange("p m k -> p (m k)"), bank[3 + n % 4][:]).then_inc(*s_done.by())
        core.end_stage()


def top16(dve, own, passed, values, places, source):
    dve.sem_inc(*passed.by())
    for n in range(len(source)):
        ins = dve.max(values[n][:, 0:8], source[n])
    own(ins)
    dve.sem_inc(*passed.by())
    for n in range(len(source)):
        dve.max_index(places[n][:, 0:8], values[n][:, 0:8], source[n])
    for n in range(len(source)):
        ins = dve.match_replace(source[n], values[n][:, 0:8], source[n], -3.0e38)
    own(ins)
    dve.sem_inc(*passed.by())
    for n in range(len(source)):
        ins = dve.max(values[n][:, 8:16], source[n])
    own(ins)
    dve.sem_inc(*passed.by())
    for n in range(len(source)):
        ins = dve.max_index(places[n][:, 8:16], values[n][:, 8:16], source[n])
    own(ins)


def peer_experts(core, io, scores, layer):
    nc = core.nc
    RING = 8
    TURN = 2 * RING
    TURNS = SLOTS // TURN
    HC = 2 * PH
    TOPK_STEPS = 25
    u_rows, v_rows = (io[n].rearrange("l e d -> (l e) d") for n in ("peer_u", "peer_v"))
    with ExitStack() as ctx:
        def sb(name, shape, dt=F32):
            return ctx.enter_context(nc.sbuf_tensor(f"{name}_{layer}", shape, dt))

        u_ring, v_ring = sb("u_ring", [P, RING, D]), sb("v_ring", [P, RING, D])
        u_at, v_at = sb("u_at", [P, TURN], U32), sb("v_at", [P, TURN], U32)
        expert = sb("expert", [P, TILES * SLOTS], U32)
        gate, act_in, mix = sb("gate", [P, SLOTS]), sb("act_in", [P, SLOTS]), sb("mix", [P, TILES * SLOTS])
        work = sb("work", [P, HC, PK])
        row = sb("row", [P, D])
        best, best_at = sb("best", [P, HC, PTOP]), sb("best_at", [P, HC, PTOP], U32)
        best_at_f = sb("best_at_f", [P, HC, PTOP])
        cand = sb("cand", [P, PH, PTOP * PTOP])
        top, top_at = sb("top", [P, PH, PTOP]), sb("top_at", [P, PH, PTOP], U32)
        digit, digit_f = sb("digit", [P, 2, SLOTS], U32), sb("digit_f", [P, 2, SLOTS])
        hot, found = sb("hot", [P, SLOTS, PTOP]), sb("found", [P, 2, SLOTS])
        norm = sb("norm", [P, PH])
        dots = sb("dots", [P, TURN])
        mix_now = sb("mix_now", [P, TURN])
        DIAGS = 4
        diag = sb("diag", [P, DIAGS, P])
        zero = sb("zero", [P, P])
        ffn = sb("ffn", [P, TILES, D])
        ln_g, ln_b = sb("ln_g", [P, D]), sb("ln_b", [P, D])
        stats, mv, rstd = sb("pstats", [P, 2, 6]), sb("pmv", [P, 2]), sb("prstd", [P, 1])
        acc = ctx.enter_context(nc.psum_tensor(f"pacc_{layer}", [P, 2, HALF], F32))

        u_in = [core.sig(f"u_in{i}") for i in range(RING)]
        v_in = [core.sig(f"v_in{i}") for i in range(RING)]
        u_used, v_used, at_copied = core.sig("u_used"), core.sig("v_used"), core.sig("at_copied")
        chosen, gate_arg, gate_exp = core.sig("chosen"), core.sig("gate_arg"), core.sig("gate_exp")
        dots_all, gelu_done, mix_done = core.sig("dots_all"), core.sig("gelu_done"), core.sig("mix_done")
        mix_now_done, diag_done = core.sig("mix_now_done"), core.sig("diag_ready")
        zeroed, ffn_psum, ffn_done, ln_in = core.sig("zeroed"), core.sig("ffn_psum"), core.sig("ffn_done"), core.sig("vectors_in")
        dve_steps, pool_turns, passed = core.sig("dve_steps"), core.sig("pool_turns"), core.sig("dve_passed")
        dots_done, act_turns = core.sig("dots_done"), core.sig("act_turns")
        core.sig("ln_var"), core.sig("ln_rstd")

        with nc.Block() as block:
            @block.sync
            def _(sp):
                sp.dma_start(ln_g[:], io["ln_ffn_g"][layer:layer + 1, :].broadcast_to([P, D])).then_inc(*ln_in.by(16))
                sp.dma_start(ln_b[:], io["ln_ffn_b"][layer:layer + 1, :].broadcast_to([P, D])).then_inc(*ln_in.by(16))

            @block.gpsimd
            def _(pool):
                def gathers(t, table, ring, places, arrived, used):
                    with pool.Fori(0, TURNS) as s, turns(s, TURNS, counted=(at_copied, pool_turns, *arrived)):
                        for half in range(2):
                            at = places[:, half * RING:(half + 1) * RING]
                            first = t * SLOTS + s * TURN + half * RING
                            pool.wait_ge(*used.at(first + 1))
                            pool.sem_inc(*pool_turns.by())
                            pool.tensor_copy(at, expert[:, bass.ds(first, RING)]).then_inc(*at_copied.by())
                            for j in range(RING):
                                pool.wait_ge(*used.at(first + j + 1))
                                if j == 0:
                                    pool.wait_ge(*at_copied.at(at_base + t * 4 * TURNS + s * 2 + half + 1))
                                pool.sem_inc(*pool_turns.by())
                                pool.indirect_dma_start(ring[:, j, :], None, table,
                                                        bass.IndirectOffsetOnAxis(ap=at[:, j:j + 1], axis=0)).then_inc(*arrived[j].by(16))

                with pool.Fori(0, TILES) as t, turns(t, TILES, counted=(at_copied, pool_turns, *u_in, *v_in)):
                    pool.wait_ge(*chosen.at(t + 1))
                    pool.sem_inc(*pool_turns.by())
                    at_base = 0
                    gathers(t, u_rows, u_ring, u_at, u_in, u_used)
                    at_base = 2 * TURNS
                    gathers(t, v_rows, v_ring, v_at, v_in, v_used)

            @block.vector
            def _(dve):
                own = in_order(dve, dve_steps)
                x = core.x_tok
                dve.memset(zero[:], 0.0).then_inc(*zeroed.by())
                dve.sem_inc(*u_used.by(RING))
                heads4 = [P, PH, PTOP, PTOP]
                with dve.Fori(0, TILES) as t, turns(t, TILES, own=dve_steps, per=TOPK_STEPS,
                                                    counted=(chosen, gate_arg, dots_all, mix_done, u_used, dots_done, passed)):
                    dve.tensor_copy(work[:].rearrange("p m k -> p (m k)"), scores[:, bass.ds(t, 1)].rearrange("p o m k -> p (o m k)"))
                    own(dve.tensor_copy(row[:], x[:, bass.ds(t, 1)].rearrange("p o d -> p (o d)")))
                    top16(dve, own, passed, [best[:, m, :] for m in range(HC)], [best_at[:, m, :] for m in range(HC)], [work[:, m, :] for m in range(HC)])
                    two = best[:].rearrange("p (h c) k -> p h c k", c=2)
                    dve.tensor_copy(best_at_f[:], best_at[:])
                    own(dve.tensor_tensor(cand[:].rearrange("p h (i j) -> p h i j", j=PTOP), two[:, :, 0, :].unsqueeze(3).broadcast_to(heads4),
                                          two[:, :, 1, :].unsqueeze(2).broadcast_to(heads4), ALU.add))
                    top16(dve, own, passed, [top[:, h, :] for h in range(PH)], [top_at[:, h, :] for h in range(PH)], [cand[:, h, :] for h in range(PH)])
                    gate_h = gate[:].rearrange("p (h k) -> p h k", k=PTOP)
                    own(dve.tensor_tensor(gate_h, top[:], top[:, :, 0:1].broadcast_to([P, PH, PTOP]), ALU.subtract))
                    dve.sem_inc(*gate_arg.by())
                    flat = top_at[:].rearrange("p h k -> p (h k)")
                    dve.tensor_scalar(digit[:, 0, :], flat, 4, None, ALU.logical_shift_right)
                    own(dve.tensor_scalar(digit[:, 1, :], flat, 15, None, ALU.bitwise_and))
                    own(dve.tensor_copy(digit_f[:], digit[:]))
                    two_at = best_at_f[:].rearrange("p (h c) k -> p h c k", c=2)
                    hot4 = hot[:].rearrange("p (h k) j -> p h k j", k=PTOP)
                    for c in range(2):
                        own(dve.tensor_tensor(hot[:], core.const("iota").unsqueeze(1).broadcast_to([P, SLOTS, PTOP]),
                                              digit_f[:, c, :].unsqueeze(2).broadcast_to([P, SLOTS, PTOP]), ALU.is_equal))
                        own(dve.tensor_tensor(hot4, hot4, two_at[:, :, c, :].unsqueeze(2).broadcast_to(heads4), ALU.mult))
                        own(dve.tensor_reduce(found[:, c, :], hot[:], AX.X, ALU.add))
                    own(dve.tensor_scalar(found[:, 0, :], found[:, 0, :], float(PK), float(layer * EXPERTS), ALU.mult, ALU.add))
                    own(dve.tensor_tensor(expert[:, bass.ds(t * SLOTS, SLOTS)], found[:, 0, :], found[:, 1, :], ALU.add))
                    dve.sem_inc(*chosen.by())
                    with dve.Fori(0, TURNS) as s, turns(s, TURNS, counted=(u_used, dots_done)):
                        for j in range(TURN):
                            dve.wait_ge(*u_in[j % RING].at(16 * (t * 2 * TURNS + s * 2 + j // RING + 1)))
                            dve.tensor_tensor_reduce(u_ring[:, j % RING, :], u_ring[:, j % RING, :], row[:], 1.0, 0.0,
                                                     ALU.mult, ALU.add, dots[:, j:j + 1]).then_inc(*u_used.by())
                        dve.wait_ge(*u_used.at(t * SLOTS + s * TURN + TURN + RING))
                        dve.tensor_copy(act_in[:, bass.ds(s * TURN, TURN)], dots[:]).then_inc(*dots_done.by())
                        dve.wait_ge(*dots_done.at(t * TURNS + s + 1))
                    dve.sem_inc(*dots_all.by())
                    dve.wait_ge(*gate_exp.at(t + 1))
                    own(dve.tensor_reduce(norm[:], gate_h, AX.X, ALU.add))
                    own(dve.reciprocal(norm[:], norm[:]))
                    own(dve.tensor_tensor(gate_h, gate_h, norm[:].unsqueeze(2).broadcast_to([P, PH, PTOP]), ALU.mult))
                    dve.wait_ge(*gelu_done.at(t + 1))
                    own(dve.tensor_tensor(mix[:, bass.ds(t * SLOTS, SLOTS)], gate[:], act_in[:], ALU.mult))
                    dve.sem_inc(*mix_done.by())
                dve.wait_ge(*ln_in.at(32))
                for t in range(TILES):
                    dve.wait_ge(*ffn_done.at(t + 2))
                    own(dve.scalar_tensor_tensor(ffn[:, t, :], x[:, t, :], ALPHA, ffn[:, t, :], ALU.mult, ALU.add))
                    layer_norm_steps(core, dve, own, ffn[:, t, :], x[:, t, :], ln_g[:], ln_b[:], stats, mv, rstd, t + 1)

            @block.scalar
            def _(act):
                act.sem_inc(*ffn_done.by())
                with act.Fori(0, TILES) as t, turns(t, TILES, counted=(gate_exp, gelu_done, mix_now_done, diag_done, act_turns, ffn_done)):
                    act.wait_ge(*gate_arg.at(t + 1))
                    act.activation(gate[:], gate[:], ACT.Exp).then_inc(*gate_exp.by())
                    act.wait_ge(*dots_all.at(t + 1))
                    act.activation(act_in[:], act_in[:], ACT.Gelu).then_inc(*gelu_done.by())
                    act.wait_ge(*mix_done.at(t + 1))
                    act.sem_inc(*act_turns.by())
                    with act.Fori(0, TURNS) as s, turns(s, TURNS, counted=(mix_now_done, diag_done, act_turns)):
                        act.copy(mix_now[:], mix[:, bass.ds(t * SLOTS + s * TURN, TURN)]).then_inc(*mix_now_done.by())
                        for j in range(TURN):
                            if j == 0:
                                act.wait_ge(*mix_now_done.at(t * TURNS + s + 1))
                            act.wait_ge(*v_used.at(t * SLOTS + s * TURN + j + 1 + RING - DIAGS))
                            act.activation(diag[:, j % DIAGS, :], core.const("ident"), ACT.Copy, scale=mix_now[:, j:j + 1]).then_inc(*diag_done.by())
                        act.wait_ge(*diag_done.at(t * SLOTS + s * TURN + TURN))
                        act.sem_inc(*act_turns.by())
                    act.wait_ge(*ffn_psum.at(t + 1))
                    act.sem_inc(*act_turns.by())
                    act.copy(ffn[:, bass.ds(t, 1)].rearrange("p o d -> p (o d)"), acc[:].rearrange("p a d -> p (a d)")).then_inc(*ffn_done.by())
                layer_norm_roots(core, act, mv, rstd)

            @block.tensor
            def _(pe):
                x_first = core.x_tok[:, 0, :]
                pe.wait_ge(*zeroed.at(1))
                pe.sem_inc(*v_used.by(RING))
                with pe.Fori(0, TILES) as t, turns(t, TILES, counted=(v_used, ffn_psum)):
                    pe.wait_ge(*mix_done.at(t + 1))
                    pe.wait_ge(*ffn_done.at(t + 1))
                    for half in range(2):
                        pe.matmul(acc[:, half, :], zero[:], x_first[:, half * HALF:(half + 1) * HALF], start=True, stop=False)
                    with pe.Fori(0, TURNS) as s, turns(s, TURNS, counted=(v_used,)):
                        for j in range(TURN):
                            pe.wait_ge(*v_in[j % RING].at(16 * (t * 2 * TURNS + s * 2 + j // RING + 1)))
                            pe.wait_ge(*diag_done.at(t * SLOTS + s * TURN + j + 1))
                            pe.matmul(acc[:, 0, :], diag[:, j % DIAGS, :], v_ring[:, j % RING, 0:HALF], start=False, stop=False)
                            pe.matmul(acc[:, 1, :], diag[:, j % DIAGS, :], v_ring[:, j % RING, HALF:], start=False, stop=False).then_inc(*v_used.by())
                    for half in range(2):
                        mm = pe.matmul(acc[:, half, :], zero[:], x_first[:, half * HALF:(half + 1) * HALF], start=False, stop=True)
                    mm.then_inc(*ffn_psum.by())
        core.end_stage()


def attention_projections(core, io, xT, out):
    nc = core.nc
    weights = [("k", io["w_kv"][:, 0:D]), ("v", io["w_kv"][:, D:]), ("q", io["diff_w_q"][0])]
    with ExitStack() as ctx:
        RING = 12
        ring = ctx.enter_context(nc.sbuf_tensor("aw_ring", [P, RING, D], F32))
        rot = ctx.enter_context(nc.sbuf_tensor("rot", [P, 4, TILES, 2 * DH, ROT // 2], F32))
        acc = ctx.enter_context(nc.psum_tensor("aacc", [P, 6, HALF], F32))
        aw_in = [core.sig(f"loaded{i}") for i in range(RING)]
        aw_used, a_full, a_free = core.sig("w_used"), core.sig("acc_full"), core.sig("acc_free_act")
        rotated, kv_out, dve_steps = core.sig("rotated"), core.sig("kv_out"), core.sig("dve_steps")

        with nc.Block() as block:
            @block.sync
            def _(sp):
                for n in range(3 * KD):
                    if n >= RING:
                        sp.wait_ge(*aw_used.at(n - RING + 1))
                    sp.dma_start(ring[:, n % RING, :], weights[n // KD][1][n % KD * P:(n % KD + 1) * P, :]).then_inc(*aw_in[n % RING].by(16))

            @block.gpsimd
            def _(pool):
                pool.wait_ge(*a_free.at(12))
                for n, wait in (("v", None), ("k", rotated)):
                    if wait:
                        pool.wait_ge(*wait.at(1))
                    tail = "h c d -> (b s) (h c d)" if n == "k" else "h e -> (b s) (h e)"
                    rows_p, rows_s = (io[f"cache_{n}_{w}"].rearrange("b s " + tail) for w in "ps")
                    pool.dma_start(rows_p.rearrange("(t p) e -> p t e", p=P), out[n][:, 0:2, :]).then_inc(*kv_out.by(16))
                    pool.dma_start(rows_s, out[n][:, 2, :]).then_inc(*kv_out.by(16))
                pool.wait_ge(*kv_out.at(64))

            @block.tensor
            def _(pe):
                for i in range(3):
                    for k in range(KD):
                        n = i * KD + k
                        pe.wait_ge(*aw_in[n % RING].at(16 * (n // RING + 1)))
                        for b in range(6):
                            if k == 0 and i > 0:
                                pe.wait_ge(*a_free.at(6 * (i - 1) + b + 1))
                            t, h = divmod(b, 2)
                            mm = pe.matmul(acc[:, b, :], xT[:, k, t * P:(t + 1) * P], ring[:, n % RING, h * HALF:(h + 1) * HALF],
                                           start=(k == 0), stop=(k == KD - 1))
                            if k == KD - 1:
                                mm.then_inc(*a_full.by())
                        if k < KD - 1:
                            mm.then_inc(*aw_used.by())
                        else:
                            pe.wait_ge(*a_full.at(6 * (i + 1)))
                            pe.sem_inc(*aw_used.by())

            @block.scalar
            def _(act):
                for i, (n, _) in enumerate(weights):
                    for b in range(6):
                        act.wait_ge(*a_full.at(6 * i + b + 1))
                        act.copy(out[n][:, b // 2, (b % 2) * HALF:(b % 2 + 1) * HALF], acc[:, b, :]).then_inc(*a_free.by())

            @block.vector
            def _(dve):
                own = in_order(dve, dve_steps)
                angle = [core.const(n).rearrange("p (t r) -> p t r", t=TILES).unsqueeze(2).broadcast_to([P, TILES, 2 * DH, ROT // 2]) for n in ("cos", "sin")]
                for i, n in ((0, "k"), (2, "q")):
                    dve.wait_ge(*a_free.at(6 * (i + 1)))
                    x = out[n][:].rearrange("p t (g d) -> p t g d", d=DD)
                    x1, x2 = x[:, :, :, 0:ROT // 2], x[:, :, :, ROT // 2:ROT]
                    for j, (src, f) in enumerate(((x1, 0), (x2, 1), (x1, 1), (x2, 0))):
                        ins = dve.tensor_tensor(rot[:, j], src, angle[f], ALU.mult)
                    own(ins)
                    dve.tensor_tensor(x1, rot[:, 0], rot[:, 1], ALU.subtract)
                    own(dve.tensor_tensor(x2, rot[:, 2], rot[:, 3], ALU.add))
                    dve.sem_inc(*rotated.by())
        core.end_stage()


def mixing_weight(core, io, neg_lam):
    nc = core.nc
    with ExitStack() as ctx:
        lp = ctx.enter_context(nc.sbuf_tensor("lam_rows", [P, 2, 2, DD], F32))
        prod = ctx.enter_context(nc.sbuf_tensor("lam_prod", [P, 2, DD], F32))
        dot = ctx.enter_context(nc.sbuf_tensor("lam_dot", [P, 2], F32))
        lam_in, lam_dot, lam_exp, dve_steps = core.sig("vectors_in"), core.sig("lam_dot"), core.sig("lam_exp"), core.sig("dve_steps")
        with nc.Block() as block:
            @block.sync
            def _(sp):
                sp.dma_start(lp[:].rearrange("p a b d -> p (a b d)"), io["diff_lambda"].rearrange("a i d -> a (i d)").broadcast_to([P, 4 * DD])).then_inc(*lam_in.by(16))

            @block.scalar
            def _(act):
                act.wait_ge(*lam_dot.at(1))
                act.activation(dot[:], dot[:], ACT.Exp).then_inc(*lam_exp.by())

            @block.vector
            def _(dve):
                own = in_order(dve, dve_steps)
                dve.wait_ge(*lam_in.at(16))
                own(dve.tensor_tensor(prod[:], lp[:, :, 0, :], lp[:, :, 1, :], ALU.mult))
                own(dve.tensor_reduce(dot[:], prod[:], AX.X, ALU.add))
                dve.sem_inc(*lam_dot.by())
                dve.wait_ge(*lam_exp.at(1))
                own(dve.tensor_tensor(neg_lam[:], dot[:, 1:2], dot[:, 0:1], ALU.subtract))
                own(dve.tensor_scalar(neg_lam[:], neg_lam[:], -LAM_INIT, None, ALU.add))
        core.end_stage()


def prompt_attention(core, qT, kT, v_tok, oT, neg_lam):
    nc = core.nc
    SCALE = DD ** -0.5
    parts = (slice(0, P), slice(P, 3 * P))
    with ExitStack() as ctx:
        def sb(name, shape, dt=F32):
            return ctx.enter_context(nc.sbuf_tensor("pa_" + name, shape, dt))

        s, p = sb("s", [P, 2, 2, TOK]), sb("p", [P, 2, 2, TOK])
        top, low, tot = sb("top", [P, 2, 4]), sb("low", [P, 2, 4]), sb("tot", [P, 2, 4])
        attn, attnT = sb("attn", [P, 2, TOK]), sb("attnT", [P, 2, TOK])
        s_bank = [ctx.enter_context(nc.psum_tensor(f"pa_s{i}", [P, TOK], F32)) for i in range(4)]
        t_bank = [ctx.enter_context(nc.psum_tensor(f"pa_t{i}", [P, TOK], F32)) for i in range(2)]
        o_bank = [ctx.enter_context(nc.psum_tensor(f"pa_o{i}", [P, SEQ], F32)) for i in range(2)]
        sc, sm, top_done, p_done = core.sig("scores_psum"), core.sig("scores_masked"), core.sig("maxima"), core.sig("probs")
        attn_done, at_psum, at_done = core.sig("maps_mixed"), core.sig("mixedT_psum"), core.sig("mixedT")
        o_psum, o_done, dve_steps = core.sig("heads_psum"), core.sig("heads_out"), core.sig("dve_steps")
        with nc.Block() as block:
            @block.tensor
            def _(pe):
                def scores(h):
                    if h >= 2:
                        pe.wait_ge(*sm.at(2 * (h - 1)))
                    for c in range(2):
                        rows = slice(c * DD, (c + 1) * DD)
                        bank = s_bank[2 * (h % 2) + c]
                        pe.matmul(bank[:, parts[0]], qT[rows, h, 0:P], kT[rows, h, 0:P])
                        pe.matmul(bank[:, parts[1]], qT[rows, h, P:2 * P], kT[rows, h, 0:2 * P]).then_inc(*sc.by())

                scores(0)
                for h in range(DH):
                    if h + 1 < DH:
                        scores(h + 1)
                    pe.wait_ge(*attn_done.at(h + 1))
                    if h >= 2:
                        pe.wait_ge(*at_done.at(h - 1))
                    for i in range(3):
                        mm = pe.transpose(t_bank[h % 2][:, i * P:(i + 1) * P], attn[:, h % 2, i * P:(i + 1) * P], core.const("ident"))
                    mm.then_inc(*at_psum.by())
                    pe.wait_ge(*at_done.at(h + 1))
                    if h >= 2:
                        pe.wait_ge(*o_done.at(h - 1))
                    e = slice(h * P, (h + 1) * P)
                    pe.matmul(o_bank[h % 2][:, 0:P], v_tok[:, 0, e], attnT[:, h % 2, 0:P])
                    pe.matmul(o_bank[h % 2][:, P:], v_tok[:, 0, e], attnT[:, h % 2, P:2 * P], start=True, stop=False)
                    pe.matmul(o_bank[h % 2][:, P:], v_tok[:, 1, e], attnT[:, h % 2, 2 * P:], start=False, stop=True).then_inc(*o_psum.by())

            @block.scalar
            def _(act):
                def flush(h):
                    act.wait_ge(*at_psum.at(h + 1))
                    act.copy(attnT[:, h % 2, :], t_bank[h % 2][:]).then_inc(*at_done.by())
                    act.wait_ge(*o_psum.at(h + 1))
                    act.copy(oT[:, h, 0:SEQ], o_bank[h % 2][:]).then_inc(*o_done.by())

                for h in range(DH):
                    act.wait_ge(*top_done.at(h + 1))
                    if h >= 2:
                        act.wait_ge(*attn_done.at(h - 1))
                    for c in range(2):
                        for i in range(2):
                            j = 2 * c + i
                            act.activation(p[:, h % 2, c, parts[i]], s[:, h % 2, c, parts[i]], ACT.Exp, bias=low[:, h % 2, j:j + 1],
                                           scale=SCALE, accum_out=tot[:, h % 2, j:j + 1]).then_inc(*p_done.by())
                    if h >= 1:
                        flush(h - 1)
                flush(DH - 1)

            @block.vector
            def _(dve):
                own = in_order(dve, dve_steps)

                def combine(h):
                    dve.wait_ge(*p_done.at(4 * (h + 1)))
                    own(dve.reciprocal(tot[:, h % 2, :], tot[:, h % 2, :]))
                    own(dve.tensor_scalar(tot[:, h % 2, 2:4], tot[:, h % 2, 2:4], neg_lam[:, 0:1], None, ALU.mult))
                    if h >= 2:
                        dve.wait_ge(*at_psum.at(h - 1))
                    for i in range(2):
                        dve.tensor_scalar(attn[:, h % 2, parts[i]], p[:, h % 2, 1, parts[i]], tot[:, h % 2, 2 + i:3 + i], None, ALU.mult)
                    own(dve.tensor_copy(top[:, h % 2, 0:1], top[:, h % 2, 0:1]))
                    for i in range(2):
                        ins = dve.scalar_tensor_tensor(attn[:, h % 2, parts[i]], p[:, h % 2, 0, parts[i]], tot[:, h % 2, i:i + 1],
                                                       attn[:, h % 2, parts[i]], ALU.mult, ALU.add)
                    own(ins)
                    dve.sem_inc(*attn_done.by())

                for h in range(DH):
                    if h >= 2:
                        dve.wait_ge(*p_done.at(4 * (h - 1)))
                    for c in range(2):
                        dve.wait_ge(*sc.at(2 * h + c + 1))
                        dve.tensor_tensor(s[:, h % 2, c, :], s_bank[2 * (h % 2) + c][:], core.const("causal"), ALU.add).then_inc(*sm.by())
                    dve.wait_ge(*sm.at(2 * h + 2))
                    for c in range(2):
                        for i in range(2):
                            ins = dve.tensor_reduce(top[:, h % 2, 2 * c + i:2 * c + i + 1], s[:, h % 2, c, parts[i]], AX.X, ALU.max)
                    own(ins)
                    own(dve.tensor_scalar(low[:, h % 2, :], top[:, h % 2, :], -SCALE, None, ALU.mult))
                    dve.sem_inc(*top_done.by())
                    if h >= 1:
                        combine(h - 1)
                combine(DH - 1)
        core.end_stage()


def sample_attention(core, io, qT, kT, v_tok, oT, neg_lam):
    nc = core.nc
    SCALE = DD ** -0.5
    KT = PAST // P
    GROUPS, PER = 2, 4
    HR = 2 * DEC_SEQ
    assert PER * HR == P
    ident = core.const("ident")
    with ExitStack() as ctx:
        def sb(name, shape, dt=F32):
            return ctx.enter_context(nc.sbuf_tensor("sa_" + name, shape, dt))

        kc, vc = sb("kc", [P, 2, KT, D]), sb("vc", [P, 3, KT, D])
        kcT = sb("kcT", [P, DH, PAST])
        q_maps = sb("q_maps", [P, DEC_BATCH, DH, HR])
        p = sb("p", [P, GROUPS, PAST])
        p_new = sb("p_new", [P, GROUPS, DEC_BATCH, P])
        pT = sb("pT", [P, GROUPS, KT + 1, P])
        top, low, tot = sb("top", [P, 2, GROUPS]), sb("low", [P, GROUPS]), sb("tot", [P, 2, GROUPS])
        row_w, map_w = sb("row_w", [P, GROUPS]), sb("map_w", [P, 1])
        o_rows = sb("o_rows", [P, GROUPS, P])
        bank = [ctx.enter_context(nc.psum_tensor(f"sa_b{i}", [P, HALF], F32)) for i in range(8)]
        s_bank, new_bank, pT_bank, pT_new_bank, o_bank, oT_bank = bank[2:4], bank[4], bank[5:7], bank[7], bank[5], bank[6]
        kc_in, vc_in = [core.sig(f"loaded{i}") for i in range(2)], [core.sig(f"loaded{2 + i}") for i in range(3)]
        zeros, q_done = core.sig("zeros"), core.sig("q_maps")
        kt_psum, kt_act, kt_dve = core.sig("keysT_psum"), core.sig("copied_act"), core.sig("copied_dve")
        sc, low_done, p_done = core.sig("scores_psum"), core.sig("maxima"), core.sig("probs")
        pT_psum, pT_act, pT_dve = core.sig("probsT_psum"), core.sig("probsT_act"), core.sig("probsT_dve")
        o_psum, o_scaled, oT_psum, o_done = (core.sig(n) for n in ("rows_psum", "rows_copied", "heads_psum", "heads_out"))
        dve_steps = core.sig("dve_steps")

        with nc.Block() as block:
            @block.sync
            def _(sp):
                for b in range(DEC_BATCH):
                    if b >= 2:
                        sp.wait_ge(*kt_psum.at(DH * (b - 1)))
                    sp.dma_start(kc[:, b % 2], io["cache_k"][b].rearrange("(j p) h c d -> p j (h c d)", p=P)).then_inc(*kc_in[b % 2].by(16))
                    if b >= 3:
                        sp.wait_ge(*o_psum.at(b - 2))
                    sp.dma_start(vc[:, b % 3], io["cache_v"][b].rearrange("(j p) h e -> p j (h e)", p=P)).then_inc(*vc_in[b % 3].by(16))

            @block.gpsimd
            def _(pool):
                pool.memset(q_maps[:], 0.0).then_inc(*zeros.by())
                pool.memset(p_new[:], 0.0).then_inc(*zeros.by())

            @block.tensor
            def _(pe):
                def key_transposes(b):
                    pe.wait_ge(*kc_in[b % 2].at(16 * (b // 2 + 1)))
                    for h in range(DH):
                        n = b * DH + h
                        if n >= 2:
                            pe.wait_ge(*(kt_act if n % 2 == 0 else kt_dve).at(n // 2))
                        for j in range(KT):
                            mm = pe.transpose(bank[n % 2][:, j * P:(j + 1) * P], kc[:, b % 2, j, h * P:(h + 1) * P], ident)
                        mm.then_inc(*kt_psum.by())

                def scores(b, between):
                    pe.wait_ge(*kt_act.at(DH * (b + 1) // 2))
                    pe.wait_ge(*kt_dve.at(DH * (b + 1) // 2))
                    if b > 0:
                        pe.wait_ge(*p_done.at(4 * b))
                    for h in range(DH):
                        g, rows = h // PER, slice(h % PER * HR, (h % PER + 1) * HR)
                        mm = pe.matmul(new_bank[rows, g * DEC_SEQ:(g + 1) * DEC_SEQ], q_maps[:, b, h, :], kT[:, h, SEQ + b * DEC_SEQ:SEQ + (b + 1) * DEC_SEQ],
                                       tile_position=(0, h % PER * HR))
                    mm.then_inc(*sc.by())
                    for h in range(DH):
                        g, rows = h // PER, slice(h % PER * HR, (h % PER + 1) * HR)
                        mm = pe.matmul(s_bank[g][rows, :], q_maps[:, b, h, :], kcT[:, h, :], tile_position=(0, h % PER * HR))
                        if h % PER == PER - 1:
                            mm.then_inc(*sc.by())
                        if h == PER - 1 and between is not None:
                            mix_maps(between)

                def turn_probs(b):
                    pe.wait_ge(*p_done.at(4 * (b + 1)))
                    if b > 0:
                        pe.wait_ge(*o_scaled.at(b))
                        pe.wait_ge(*o_done.at(b))
                    for g in range(GROUPS):
                        for j in range(KT):
                            pe.transpose(pT_bank[g][:, j * P:(j + 1) * P], p[:, g, j * P:(j + 1) * P], ident)
                        mm = pe.transpose(pT_new_bank[:, g * P:(g + 1) * P], p_new[:, g, b, :], ident)
                        mm.then_inc(*pT_psum.by())

                def values(b):
                    pe.wait_ge(*pT_act.at(2 * (b + 1)))
                    pe.wait_ge(*pT_dve.at(b + 1))
                    pe.wait_ge(*vc_in[b % 3].at(16 * (b // 3 + 1)))
                    for h in range(DH):
                        g, rows, e = h // PER, slice(h % PER * HR, (h % PER + 1) * HR), slice(h * P, (h + 1) * P)
                        for j in range(KT + 1):
                            v = vc[:, b % 3, j, e] if j < KT else v_tok[:, 2, e]
                            mm = pe.matmul(o_bank[rows, g * P:(g + 1) * P], pT[:, g, j, rows], v, start=(j == 0), stop=(j == KT),
                                           tile_position=(0, h % PER * HR))
                    mm.then_inc(*o_psum.by())

                def mix_maps(b):
                    pe.wait_ge(*o_scaled.at(b + 1))
                    for g in range(GROUPS):
                        mm = pe.matmul(oT_bank[:, g * DD:(g + 1) * DD], o_rows[:, g, :], core.const("sum_maps"))
                    mm.then_inc(*oT_psum.by())

                key_transposes(0)
                pe.wait_ge(*q_done.at(1))
                for b in range(DEC_BATCH):
                    scores(b, b - 2 if b >= 2 else None)
                    if b > 0:
                        turn_probs(b - 1)
                    if b + 1 < DEC_BATCH:
                        key_transposes(b + 1)
                    if b > 0:
                        values(b - 1)
                last = DEC_BATCH - 1
                mix_maps(last - 1)
                turn_probs(last)
                values(last)
                mix_maps(last)

            @block.scalar
            def _(act):
                def keys(b):
                    for n in range(b * DH, (b + 1) * DH, 2):
                        act.wait_ge(*kt_psum.at(n + 1))
                        if b > 0:
                            act.wait_ge(*sc.at(3 * b))
                        act.copy(kcT[:, n % DH, :], bank[0][:]).then_inc(*kt_act.by())

                def probs_turned(b):
                    act.wait_ge(*pT_psum.at(2 * b + 2))
                    if b > 0:
                        act.wait_ge(*o_psum.at(b))
                    act.copy(pT[:, 0, 0:KT, :].rearrange("p j r -> p (j r)"), pT_bank[0][:]).then_inc(*pT_act.by())
                    act.copy(pT[:, :, KT, :], pT_new_bank[:, 0:2 * P].rearrange("p (g r) -> p g r", g=GROUPS)).then_inc(*pT_act.by())

                keys(0)
                act.wait_ge(*zeros.at(2))
                for b in range(DEC_BATCH):
                    if b > 0:
                        probs_turned(b - 1)
                    if b + 1 < DEC_BATCH:
                        keys(b + 1)
                    act.wait_ge(*low_done.at(b + 1))
                    if b > 0:
                        act.wait_ge(*pT_psum.at(2 * b))
                    for g in range(GROUPS):
                        act.activation(p[:, g, :], s_bank[g][:], ACT.Exp, bias=low[:, g:g + 1], scale=SCALE,
                                       accum_out=tot[:, 0, g:g + 1]).then_inc(*p_done.by())
                        act.activation(p_new[:, g, b, b * DEC_SEQ:(b + 1) * DEC_SEQ], new_bank[:, g * DEC_SEQ:(g + 1) * DEC_SEQ], ACT.Exp,
                                       bias=low[:, g:g + 1], scale=SCALE, accum_out=tot[:, 1, g:g + 1]).then_inc(*p_done.by())
                probs_turned(DEC_BATCH - 1)

            @block.vector
            def _(dve):
                own = in_order(dve, dve_steps)

                def keys(b):
                    for n in range(b * DH + 1, (b + 1) * DH, 2):
                        dve.wait_ge(*kt_psum.at(n + 1))
                        if b > 0:
                            dve.wait_ge(*sc.at(3 * b))
                        dve.tensor_copy(kcT[:, n % DH, :], bank[1][:]).then_inc(*kt_dve.by())

                def probs_turned(b):
                    dve.wait_ge(*pT_psum.at(2 * b + 2))
                    if b > 0:
                        dve.wait_ge(*o_psum.at(b))
                    dve.tensor_copy(pT[:, 1, 0:KT, :].rearrange("p j r -> p (j r)"), pT_bank[1][:]).then_inc(*pT_dve.by())

                def scale_rows(b):
                    dve.wait_ge(*o_psum.at(b + 1))
                    if b > 0:
                        dve.wait_ge(*oT_psum.at(b))
                    for g in range(GROUPS):
                        ins = dve.tensor_scalar(o_rows[:, g, :], o_bank[:, g * P:(g + 1) * P], row_w[:, g:g + 1], None, ALU.mult)
                    own(ins)
                    dve.sem_inc(*o_scaled.by())

                def row_weights(b):
                    dve.wait_ge(*p_done.at(4 * (b + 1)))
                    own(dve.tensor_tensor(row_w[:], tot[:, 0, :], tot[:, 1, :], ALU.add))
                    own(dve.reciprocal(row_w[:], row_w[:]))
                    own(dve.tensor_scalar(row_w[:], row_w[:], map_w[:, 0:1], None, ALU.mult))

                def copy_out(b):
                    dve.wait_ge(*oT_psum.at(b + 1))
                    dve.tensor_copy(oT[:, :, SEQ + b * DEC_SEQ:SEQ + (b + 1) * DEC_SEQ],
                                    oT_bank[:, 0:P].rearrange("p (h q) -> p h q", h=DH)).then_inc(*o_done.by())

                own(dve.scalar_tensor_tensor(map_w[:], core.const("map1"), neg_lam[:, 0:1], core.const("map0"), ALU.mult, ALU.add))
                dve.wait_ge(*zeros.at(1))
                for c in range(2):
                    rows = slice(c * DD, (c + 1) * DD)
                    for h in range(DH):
                        ins = dve.tensor_copy(q_maps[rows, :, h, c * DEC_SEQ:(c + 1) * DEC_SEQ],
                                               qT[rows, h, SEQ:TOK].rearrange("p (b s) -> p b s", s=DEC_SEQ))
                ins.then_inc(*q_done.by())
                keys(0)
                for b in range(DEC_BATCH):
                    dve.wait_ge(*sc.at(3 * b + 1))
                    dve.tensor_reduce(top[:, 1, :], new_bank[:, 0:GROUPS * DEC_SEQ].rearrange("p (g k) -> p g k", g=GROUPS), AX.X, ALU.max)
                    dve.wait_ge(*sc.at(3 * b + 2))
                    dve.tensor_reduce(top[:, 0, 0:1], s_bank[0][:], AX.X, ALU.max)
                    if b >= 2:
                        copy_out(b - 2)
                    dve.wait_ge(*sc.at(3 * b + 3))
                    if b > 0:
                        probs_turned(b - 1)
                    if b + 1 < DEC_BATCH:
                        keys(b + 1)
                    own(dve.tensor_reduce(top[:, 0, 1:2], s_bank[1][:], AX.X, ALU.max))
                    own(dve.tensor_tensor(low[:], top[:, 0, :], top[:, 1, :], ALU.max))
                    own(dve.tensor_scalar(low[:], low[:], -SCALE, None, ALU.mult))
                    dve.sem_inc(*low_done.by())
                    if b > 0:
                        scale_rows(b - 1)
                    row_weights(b)
                last = DEC_BATCH - 1
                copy_out(last - 1)
                probs_turned(last)
                scale_rows(last)
                copy_out(last)
        core.end_stage()


def head_norm(core, io, oT):
    nc = core.nc
    flat = oT[:].rearrange("p h t -> p (h t)")
    COLS = DH * TOK // HALF
    with ExitStack() as ctx:
        def sb(name, shape, dt=F32):
            return ctx.enter_context(nc.sbuf_tensor("hn_" + name, shape, dt))

        sq, inv, ones, gain = sb("sq", [P, DH * TOK]), sb("inv", [P, DH * TOK]), sb("ones", [P, P]), sb("gain", [P, 1])
        bank = [ctx.enter_context(nc.psum_tensor(f"hn_b{i}", [P, HALF], F32)) for i in range(COLS)]
        hn_in, hn_sq, hn_sum, hn_inv, hn_root = (core.sig(n) for n in ("vectors_in", "squares", "rows_psum", "inverses", "rows_copied"))
        dve_steps = core.sig("dve_steps")
        with nc.Block() as block:
            @block.sync
            def _(sp):
                sp.dma_start(gain[:], io["diff_subln_g"].rearrange("a (p e) -> (a p) e", e=1)).then_inc(*hn_in.by(16))

            @block.tensor
            def _(pe):
                for i in range(COLS):
                    pe.wait_ge(*hn_sq.at(i + 1))
                    pe.matmul(bank[i][:], ones[:], sq[:, i * HALF:(i + 1) * HALF]).then_inc(*hn_sum.by())

            @block.scalar
            def _(act):
                for i in range(COLS):
                    act.wait_ge(*hn_inv.at(i + 1))
                    cols = slice(i * HALF, (i + 1) * HALF)
                    act.activation(inv[:, cols], inv[:, cols], ACT.Sqrt).then_inc(*hn_root.by())

            @block.vector
            def _(dve):
                own = in_order(dve, dve_steps)
                own(dve.memset(ones[:], 1.0))
                for i in range(COLS):
                    cols = slice(i * HALF, (i + 1) * HALF)
                    dve.tensor_tensor(sq[:, cols], flat[:, cols], flat[:, cols], ALU.mult).then_inc(*hn_sq.by())
                dve.wait_ge(*hn_in.at(16))
                own(dve.tensor_scalar(gain[:], gain[:], 1.0 - LAM_INIT, None, ALU.mult))
                for i in range(COLS):
                    cols = slice(i * HALF, (i + 1) * HALF)
                    dve.wait_ge(*hn_sum.at(i + 1))
                    own(dve.tensor_scalar(inv[:, cols], bank[i][:], 1.0 / P, SUBLN_EPS, ALU.mult, ALU.add))
                    own(dve.reciprocal(inv[:, cols], inv[:, cols]))
                    dve.sem_inc(*hn_inv.by())
                for i in range(COLS):
                    cols = slice(i * HALF, (i + 1) * HALF)
                    dve.wait_ge(*hn_root.at(i + 1))
                    own(dve.scalar_tensor_tensor(flat[:, cols], flat[:, cols], gain[:, 0:1], inv[:, cols], ALU.mult, ALU.mult))
        core.end_stage()


def attention(core, io):
    nc = core.nc
    with ExitStack() as ctx:
        def sb(name, shape, dt=F32):
            return ctx.enter_context(nc.sbuf_tensor("at_" + name, shape, dt))

        oT, qT, kT = (sb(n, [P, DH, TOK]) for n in ("oT", "qT", "kT"))
        v_tok, neg_lam = sb("v", [P, TILES, D]), sb("neg_lam", [P, 1])
        mixing_weight(core, io, neg_lam)
        with ExitStack() as proj:
            tok = {n: proj.enter_context(nc.sbuf_tensor("at_tok_" + n, [P, TILES, D], F32)) for n in "kq"}
            tok["v"] = v_tok
            xT = proj.enter_context(nc.sbuf_tensor("at_xT", [P, KD, TOK], F32))
            to_features(core, core.x_tok, xT, "at_x")
            attention_projections(core, io, xT, tok)
            to_features(core, tok["k"], kT, "at_k")
            to_features(core, tok["q"], qT, "at_q")
        prompt_attention(core, qT, kT, v_tok, oT, neg_lam)
        sample_attention(core, io, qT, kT, v_tok, oT, neg_lam)
        head_norm(core, io, oT)
        project_and_norm(core, io, oT, io["diff_w_o"][0], 1, "attention")


def store_rows(core, io):
    y_out = core.sig("y_out")
    with core.nc.Block() as block:
        @block.sync
        def _(sp):
            for t in range(TILES):
                sp.dma_start(row_tile(io["y_prompt"], io["y_sample"], t), core.x_tok[:, t, :]).then_inc(*y_out.by(16))
            sp.wait_ge(*y_out.at(16 * TILES))
    core.end_stage()


INS = ["x_prompt", "x_sample", "state_wkv", "state_shift", "cache_k", "cache_v",
       "rwkv_mu", "rwkv_w_rkv", "rwkv_w0", "rwkv_w1", "rwkv_w2", "rwkv_a0", "rwkv_a1", "rwkv_a2",
       "rwkv_g1", "rwkv_g2", "rwkv_k_k", "rwkv_k_a", "rwkv_r_k", "rwkv_lnx_g", "rwkv_lnx_b", "rwkv_w_out",
       "w_kv", "diff_w_q", "diff_lambda", "diff_subln_g", "diff_w_o",
       "ln_mix_g", "ln_mix_b", "ln_ffn_g", "ln_ffn_b",
       "peer_w_query", "peer_sub_keys", "peer_u", "peer_v"]
OUTS = {"y_prompt": (1, SEQ, D), "y_sample": (DEC_BATCH, DEC_SEQ, D),
        "wkv_p": (1, 1, H, N, N), "shift_p": (1, 1, 1, D),
        "cache_k_p": (1, SEQ, DH, 2, DD), "cache_v_p": (1, SEQ, DH, 2 * DD),
        "wkv_s": (1, DEC_BATCH, H, N, N), "shift_s": (1, DEC_BATCH, 1, D),
        "cache_k_s": (DEC_BATCH, DEC_SEQ, DH, 2, DD), "cache_v_s": (DEC_BATCH, DEC_SEQ, DH, 2 * DD)}


def program(nc, io, stages=99):
    with ExitStack() as ctx:
        core = Core(nc, ctx)
        core.where, width = constant_layout()
        core.constants = ctx.enter_context(nc.sbuf_tensor("constants_sb", [P, width], F32))
        core.spill = {n: nc.dram_tensor(f"spill_{n}", [TILES, P, D], F32, kind="Internal").ap() for n in "rkvwag"}
        with ExitStack() as proj:
            buf = {n: proj.enter_context(nc.sbuf_tensor(f"buf_{n}", [P, TILES, D], F32)) for n in "rkvzag"}
            rwkv_projections(core, io, buf)
        if stages == 1:
            return
        with ExitStack() as wkv:
            w = {"carry": wkv.enter_context(nc.sbuf_tensor("carry", [P, H // 2, N], F32))}
            for t in range(TILES):
                with ExitStack() as per_tile:
                    def sb(name, shape):
                        return per_tile.enter_context(nc.sbuf_tensor(f"wkv_{name}_{t}", shape, F32))

                    tile = {n: sb(n, [P, D]) for n in "rkvzag"}
                    for n, shape in {"bonus": [P, D], "y": [P, D], "Y2t": [P, H // 2, P], "Q1t": [P, H // 2, P]}.items():
                        w[n] = sb(n, shape)
                    with ExitStack() as ops:
                        names = ["B", "B_end", "K_end", "e_end"]
                        w["G"], w["Ft"] = sb("G", [P, NCH + 1, H // 2, N]), None
                        for n in names:
                            w[n] = ops.enter_context(nc.sbuf_tensor(f"wkv_{n}_{t}", [P, D], F32))
                        wkv_operands(core, io, tile, w, t)
                        w["Ft"] = ops.enter_context(nc.sbuf_tensor(f"wkv_Ft_{t}", [P, NCH, H // 2, N], F32))
                        wkv_chunks(core, tile, w, t)
                        wkv_states_and_outputs(core, io, tile, w, t)
        if stages == 2:
            return
        core.x_tok = ctx.enter_context(nc.sbuf_tensor("x_tok", [P, TILES, D], F32))
        with ExitStack() as rwkv:
            gated = rwkv.enter_context(nc.sbuf_tensor("gated_wkv", [P, TILES, D], F32))
            mixT = rwkv.enter_context(nc.sbuf_tensor("mixT", [P, KD, TOK], F32))
            load_rows(core, io, gated)
            to_features(core, gated, mixT, "rwkv")
            project_and_norm(core, io, mixT, io["rwkv_w_out"][0], 0, "rwkv")
        if stages == 3:
            return
        peer(core, io, 0)
        if stages == 4:
            return
        attention(core, io)
        if stages == 5:
            return
        peer(core, io, 1)
        store_rows(core, io)


def peer(core, io, layer):
    with ExitStack() as ctx:
        scores = ctx.enter_context(core.nc.sbuf_tensor(f"scores_{layer}", [P, TILES, 2 * PH, PK], F32))
        with ExitStack() as feat:
            xT = feat.enter_context(core.nc.sbuf_tensor(f"peer_xT_{layer}", [P, KD, TOK], F32))
            to_features(core, core.x_tok, xT, f"peer{layer}")
            peer_scores(core, io, xT, scores, layer)
        peer_experts(core, io, scores, layer)


def kernel(**inputs):
    import concourse.bacc as bacc
    from concourse.bass_utils import run_bass_kernel_spmd

    nc = bacc.Bacc("TRN2", target_bir_lowering=False, num_devices=1)
    arrays, io = {}, {}
    for name in INS:
        a = np.ascontiguousarray(inputs[name])
        arrays[f"in_{name}"] = a
        io[name] = nc.dram_tensor(f"in_{name}", a.shape, F32, kind="ExternalInput").ap()
    c = shape_constants()
    arrays["in_constants"] = c
    io["constants"] = nc.dram_tensor("in_constants", c.shape, F32, kind="ExternalInput").ap()
    for name, shape in OUTS.items():
        io[name] = nc.dram_tensor(f"out_{name}", shape, F32, kind="ExternalOutput").ap()
    program(nc, io)
    r = run_bass_kernel_spmd(nc, [arrays], core_ids=[0])
    return tuple(r.results[0][f"out_{name}"] for name in OUTS)
```

```python
import math
from contextlib import ExitStack, contextmanager

import numpy as np

import concourse.bass as bass
from concourse import mybir

F32 = mybir.dt.float32
U32 = mybir.dt.uint32
I32 = mybir.dt.int32
ALU = mybir.AluOpType
ACT = mybir.ActivationFunctionType
AX = mybir.AxisListType

P = 128
D = 1024
KD = D // P
HALF = 512
SEQ = 256
DEC_BATCH, DEC_SEQ, PAST = 8, 16, 512
TILES = 3
TOK = TILES * P
L = 16
NCH = P // L
H, N = 16, 64
DH, DD = 8, 64
ROT = DD // 4
PH, PK, PTOP = 8, 128, 16
EXPERTS = PK * PK
SLOTS = PH * PTOP
ALPHA = (2.0 * 2) ** 0.25
LN_EPS, GN_EPS, SUBLN_EPS = 1e-5, 64e-5, 1e-5
DECAY_SCALE = -math.exp(-0.5)
LAM_INIT = 0.8 - 0.6 * math.exp(-0.3 * 1)
FAR = -1e30


def constant_layout():
    widths = [("ident", P), ("strict_incl", 2 * P), ("lower", P), ("block", P), ("chunk", NCH), ("first", NCH),
              ("causal", 3 * P), ("pair_ident", N), ("map0", 1), ("map1", 1), ("sum_maps", DD), ("iota", PTOP), ("cos", TILES * ROT // 2),
              ("sin", TILES * ROT // 2)]
    at, where = 0, {}
    for name, w in widths:
        where[name] = (at, at + w)
        at += w
    return where, at


def shape_constants():
    where, width = constant_layout()
    c = np.zeros((P, width), np.float32)
    row, col = np.arange(P)[:, None], np.arange(P)[None, :]
    same = row // L == col // L

    def put(name, value):
        c[:, where[name][0]:where[name][1]] = value

    put("ident", row == col)
    put("strict_incl", np.concatenate([same & (row < col), same & (row <= col)], 1))
    put("lower", same & (col < row))
    put("block", same)
    put("chunk", row // L == np.arange(NCH)[None, :])
    put("first", row == L * np.arange(NCH)[None, :])
    causal = np.where((row < 64) & (col >= 64), FAR, 0.0)
    put("causal", np.concatenate([causal, np.zeros((P, P)), causal], 1))
    put("pair_ident", row % N == np.arange(N)[None, :])
    second = row // L % 2
    put("map0", 1 - second)
    put("map1", second)
    put("sum_maps", (row // (2 * L) == np.arange(DD)[None, :] // L) & (row % L == np.arange(DD)[None, :] % L))
    put("iota", np.broadcast_to(np.arange(PTOP), (P, PTOP)))
    half = ROT // 2
    inv = np.power(np.float32(500000.0), -np.arange(half, dtype=np.float32) * np.float32(2.0) / np.float32(ROT))
    pos = np.stack([np.arange(P), P + np.arange(P), PAST + np.arange(P) % DEC_SEQ]).astype(np.float32)
    ang = (pos[:, :, None] * inv.astype(np.float32)).astype(np.float32)
    put("cos", np.cos(ang).astype(np.float32).transpose(1, 0, 2).reshape(P, -1))
    put("sin", np.sin(ang).astype(np.float32).transpose(1, 0, 2).reshape(P, -1))
    return c


class Signal:

    def __init__(self, ctx, nc, name):
        self.sem = ctx.enter_context(nc.semaphore(name))
        self.base = 0
        self.made = 0

    def by(self, n=1):
        self.made += n
        return self.sem, n

    def at(self, n):
        return self.sem, self.base + n

    def last(self):
        return self.sem, self.base + self.made

    def new_stage(self):
        self.base += self.made
        self.made = 0


class Core:

    def __init__(self, nc, ctx):
        self.nc, self.ctx = nc, ctx
        self.signals = {}

    def sig(self, name):
        if name not in self.signals:
            self.signals[name] = Signal(self.ctx, self.nc, name)
        return self.signals[name]

    def end_stage(self):
        for s in self.signals.values():
            s.new_stage()

    def const(self, name):
        a, b = self.where[name]
        return self.constants[:, a:b]


@contextmanager
def turns(i, times, counted=(), own=None, per=0):
    before = [s.made for s in counted]
    if own is not None:
        base, made = own.base, own.made
        own.base, own.made = base + made + i * per, 0
    yield
    if own is not None:
        assert own.made == per, own.made
        own.base, own.made = base, made + per * times
    for s, n in zip(counted, before):
        s.made = n + (s.made - n) * times


def in_order(eng, steps):

    def own(ins):
        ins.then_inc(*steps.by())
        eng.wait_ge(*steps.last())

    return own


def row_tile(x_prompt, x_sample, t):
    if t < 2:
        return x_prompt[0, t * P:(t + 1) * P, :]
    return x_sample.rearrange("b s d -> (b s) d")


def by_chunk(w):
    return w.rearrange("(k p) n -> p k n", p=P)


def rwkv_projections(core, io, buf):
    nc = core.nc
    ident = core.const("ident")
    with ExitStack() as ctx:
        def sb(name, shape, dt=F32):
            return ctx.enter_context(nc.sbuf_tensor(name, shape, dt))

        x_tok = sb("x_rows", [P, TILES, D])
        shift_rows = sb("shift_rows", [DEC_BATCH, D])
        mu_rows = sb("mu_rows", [6 * KD, P])
        mu_cols = sb("mu_cols", [P, 6 * KD])
        xT = sb("xT", [P, KD, TOK + DEC_BATCH])
        dxT = sb("dxT", [P, KD, TOK])
        mixed = sb("mixed", [P, 2, KD, TOK])
        RING = 7
        w_ring = sb("w_ring", [P, RING, D])
        lora_in = {"w": sb("w1_sb", [P, KD, 64]), "a": sb("a1_sb", [P, KD, 64]), "g": sb("g1_sb", [P, KD, P])}
        lora_out = {"w": sb("w2_sb", [64, D]), "a": sb("a2_sb", [64, D]), "g": sb("g2_sb", [P, D])}
        lora_bias = {"w": sb("w0_sb", [P, D]), "a": sb("a0_sb", [P, D])}
        hidden = sb("hidden", [P, TOK])
        acc = ctx.enter_context(nc.psum_tensor("acc", [P, 6, HALF], F32))
        aux = ctx.enter_context(nc.psum_tensor("aux", [P, 2, HALF], F32))

        rows_in, xT_psum, xT_done = core.sig("rows_in"), core.sig("rows_psum"), core.sig("rows_copied")
        mu_psum, mu_done = core.sig("mu_psum"), core.sig("mu_done")
        mixed_done, mixed_used = core.sig("mixed_done"), core.sig("mixed_used")
        w_in = [core.sig(f"loaded{i}") for i in range(RING)]
        w_used, acc_full = core.sig("w_used"), core.sig("acc_full")
        free_by = {m: core.sig("acc_free_dve" if m in "wa" else "acc_free_act") for m in "rkvwag"}
        lora_w_in, hid_psum, hid_done = core.sig("lora_w_in"), core.sig("hid_psum"), core.sig("hid_done")
        dve_steps, act_steps = core.sig("dve_steps"), core.sig("act_steps")
        shift_out, spilled = core.sig("shift_out"), core.sig("spilled")

        PLAN = [("r", 0), ("k", 1), ("v", 2), ("w", 3), ("a", 4), ("g", 5)]
        into = {"r": buf["r"], "k": buf["k"], "v": buf["v"], "w": buf["z"], "a": buf["a"], "g": buf["g"]}

        def bank_free(eng, j, b):
            if j > 0:
                m = PLAN[j - 1][0]
                before = sum(free_by[q] is free_by[m] for q, _ in PLAN[:j - 1])
                eng.wait_ge(*free_by[m].at(6 * before + b + 1))

        with nc.Block() as block:
            @block.sync
            def _(sp):
                sp.dma_start(core.constants[:], io["constants"]).then_inc(*rows_in.by(16))
                for t in range(TILES):
                    sp.dma_start(x_tok[:, t, :], row_tile(io["x_prompt"], io["x_sample"], t)).then_inc(*rows_in.by(16))
                sp.dma_start(shift_rows[:], io["state_shift"].rearrange("a b c d -> (a b c) d")).then_inc(*rows_in.by(16))
                sp.dma_start(mu_rows[:], io["rwkv_mu"].rearrange("a i (k p) -> (a i k) p", p=P)).then_inc(*rows_in.by(16))
                n = 0
                for i in range(3):
                    for k in range(KD):
                        if n >= RING:
                            sp.wait_ge(*w_used.at(n - RING + 1))
                        sp.dma_start(w_ring[:, n % RING, :], io["rwkv_w_rkv"][0, i, k * P:(k + 1) * P, :]).then_inc(*w_in[n % RING].by(16))
                        n += 1

            @block.gpsimd
            def _(pool):
                for m, (w1, w2) in {"w": ("rwkv_w1", "rwkv_w2"), "a": ("rwkv_a1", "rwkv_a2"), "g": ("rwkv_g1", "rwkv_g2")}.items():
                    pool.dma_start(lora_in[m][:], by_chunk(io[w1][0])).then_inc(*lora_w_in.by(16))
                    pool.dma_start(lora_out[m][:], io[w2][0]).then_inc(*lora_w_in.by(16))
                for m, w0 in {"w": "rwkv_w0", "a": "rwkv_a0"}.items():
                    pool.dma_start(lora_bias[m][:], io[w0].broadcast_to([P, D])).then_inc(*lora_w_in.by(16))
                pool.dma_start(io["shift_p"].rearrange("a b c d -> (a b c) d"), io["x_prompt"][0, SEQ - 1:SEQ, :]).then_inc(*shift_out.by(16))
                pool.dma_start(io["shift_s"].rearrange("a b c d -> (a b c) d"), io["x_sample"][:, DEC_SEQ - 1, :]).then_inc(*shift_out.by(16))
                for j, (m, _) in enumerate(PLAN):
                    before = sum(free_by[q] is free_by[m] for q, _ in PLAN[:j])
                    pool.wait_ge(*free_by[m].at(6 * (before + 1)))
                    pool.dma_start(core.spill[m].rearrange("t p d -> p t d"), into[m][:]).then_inc(*spilled.by(16))
                pool.wait_ge(*spilled.at(16 * 6))
                pool.wait_ge(*shift_out.at(32))

            @block.tensor
            def _(pe):
                pe.wait_ge(*rows_in.at(96))
                pe.transpose(acc[:, 0, 0:6 * KD], mu_rows[:], ident[0:6 * KD, 0:6 * KD]).then_inc(*mu_psum.by())
                for k in range(KD):
                    if k >= 2:
                        pe.wait_ge(*xT_done.at(k - 1))
                    for t in range(TILES):
                        pe.transpose(aux[:, k % 2, t * P:(t + 1) * P], x_tok[:, t, k * P:(k + 1) * P], ident)
                    pe.transpose(aux[:, k % 2, TOK:TOK + DEC_BATCH], shift_rows[:, k * P:(k + 1) * P],
                                 ident[0:DEC_BATCH, 0:DEC_BATCH]).then_inc(*xT_psum.by())
                n = 0
                pe.wait_ge(*mu_done.at(1))
                for j, (m, _) in enumerate(PLAN):
                    pe.wait_ge(*mixed_done.at(j + 1))
                    xm = mixed[:, j % 2]
                    if j < 3:
                        for k in range(KD):
                            pe.wait_ge(*w_in[n % RING].at(16 * (n // RING + 1)))
                            for t in range(TILES):
                                for h in range(2):
                                    if k == 0:
                                        bank_free(pe, j, 2 * t + h)
                                    mm = pe.matmul(acc[:, 2 * t + h, :], xm[:, k, t * P:(t + 1) * P],
                                                   w_ring[:, n % RING, h * HALF:(h + 1) * HALF],
                                                   start=(k == 0), stop=(k == KD - 1))
                                    if k == KD - 1 and (t, h) != (TILES - 1, 1):
                                        mm.then_inc(*acc_full.by())
                            mm.then_inc(*(w_used.by() if k < KD - 1 else acc_full.by()))
                            n += 1
                        pe.wait_ge(*acc_full.at(6 * (j + 1)))
                        pe.sem_inc(*w_used.by())
                        pe.sem_inc(*mixed_used.by())
                    else:
                        if j == 3:
                            pe.wait_ge(*lora_w_in.at(16 * 8))
                        r = 64 if m != "g" else P
                        for k in range(KD):
                            mm = pe.matmul(aux[0:r, j % 2, 0:TOK], lora_in[m][:, k, :], xm[:, k, :],
                                           start=(k == 0), stop=(k == KD - 1))
                        mm.then_inc(*hid_psum.by())
                        pe.wait_ge(*hid_done.at(j - 2))
                        pe.sem_inc(*mixed_used.by())
                        for t in range(TILES):
                            for h in range(2):
                                bank_free(pe, j, 2 * t + h)
                                pe.matmul(acc[:, 2 * t + h, :], hidden[0:r, t * P:(t + 1) * P],
                                          lora_out[m][:, h * HALF:(h + 1) * HALF]).then_inc(*acc_full.by())

            @block.scalar
            def _(act):
                for k in range(KD):
                    act.wait_ge(*xT_psum.at(k + 1))
                    act.copy(xT[:, k, :], aux[:, k % 2, 0:TOK + DEC_BATCH]).then_inc(*xT_done.by())
                for j, (m, _) in enumerate(PLAN):
                    if j >= 3:
                        r = 64 if m != "g" else P
                        act.wait_ge(*hid_psum.at(j - 2))
                        if j > 3:
                            act.wait_ge(*acc_full.at(6 * j))
                        act.activation(hidden[0:r, :], aux[0:r, j % 2, 0:TOK],
                                       {"w": ACT.Tanh, "a": ACT.Copy, "g": ACT.Sigmoid}[m]).then_inc(*hid_done.by())
                    if m in "rkvg":
                        for b in range(6):
                            act.wait_ge(*acc_full.at(6 * j + b + 1))
                            act.copy(into[m][:, b // 2, (b % 2) * HALF:(b % 2 + 1) * HALF],
                                     acc[:, b, :]).then_inc(*free_by[m].by())

            @block.vector
            def _(dve):
                own = in_order(dve, dve_steps)
                dve.wait_ge(*mu_psum.at(1))
                own(dve.tensor_copy(mu_cols[:], acc[:, 0, 0:6 * KD]))
                dve.sem_inc(*mu_done.by())
                dve.wait_ge(*xT_done.at(KD))
                s_cur = xT[:, :, SEQ:TOK].rearrange("p k (b s) -> p k b s", s=DEC_SEQ)
                s_dx = dxT[:, :, SEQ:TOK].rearrange("p k (b s) -> p k b s", s=DEC_SEQ)
                dve.tensor_tensor(dxT[:, :, 1:SEQ], xT[:, :, 0:SEQ - 1], xT[:, :, 1:SEQ], ALU.subtract)
                dve.tensor_scalar(dxT[:, :, 0:1], xT[:, :, 0:1], -1.0, None, ALU.mult)
                for b in range(DEC_BATCH):
                    dve.tensor_tensor(s_dx[:, :, b, 1:], s_cur[:, :, b, :DEC_SEQ - 1], s_cur[:, :, b, 1:], ALU.subtract)
                own(dve.tensor_tensor(s_dx[:, :, :, 0], xT[:, :, TOK:], s_cur[:, :, :, 0], ALU.subtract))
                for j, (m, i) in enumerate(PLAN):
                    if j >= 2:
                        dve.wait_ge(*mixed_used.at(j - 1))
                    for k in range(KD):
                        ins = dve.scalar_tensor_tensor(mixed[:, j % 2, k, :], dxT[:, k, :],
                                                       mu_cols[:, i * KD + k:i * KD + k + 1],
                                                       xT[:, k, 0:TOK], ALU.mult, ALU.add)
                    ins.then_inc(*mixed_done.by())
                    if j >= 1 and PLAN[j - 1][0] in "wa":
                        if j == 4:
                            dve.wait_ge(*lora_w_in.at(16 * 8))
                        for b in range(6):
                            dve.wait_ge(*acc_full.at(6 * (j - 1) + b + 1))
                            q = PLAN[j - 1][0]
                            dve.tensor_tensor(into[q][:, b // 2, (b % 2) * HALF:(b % 2 + 1) * HALF], acc[:, b, :],
                                              lora_bias[q][:, (b % 2) * HALF:(b % 2 + 1) * HALF],
                                              ALU.add).then_inc(*free_by[q].by())

        core.end_stage()


def wkv_operands(core, io, buf, w, t):
    nc = core.nc
    r, k, v, z, a = (buf[n][:] for n in "rkvza")
    heads = lambda x: x.rearrange("p (h n) -> p h n", n=N)
    with ExitStack() as ctx:
        def sb(name, shape, dt=F32):
            return ctx.enter_context(nc.sbuf_tensor(f"{name}_{t}", shape, dt))

        kk, kka, tmp = sb("kk", [P, D]), sb("kka", [P, D]), sb("tmp", [P, D])
        e_incl, e_neg, e_excl = sb("e_incl", [P, D]), sb("e_neg", [P, D]), sb("e_excl", [P, D])
        norm2, rnorm, bonus_dot = sb("norm2", [P, H]), sb("rnorm", [P, H]), sb("bonus_dot", [P, H])
        run = ctx.enter_context(nc.psum_tensor(f"run_{t}", [P, D], F32))
        end = ctx.enter_context(nc.psum_tensor(f"end_{t}", [P, D], F32))
        vec = {n: sb(n, [P, D]) for n in ("k_k", "k_a", "r_k")}
        loaded = "zakrvg"
        proj_in = [core.sig(f"loaded{i}") for i in range(6)]
        vec_in, gates, logd = core.sig("vectors_in"), core.sig("gates"), core.sig("logd")
        sums, norms, rnorms = core.sig("sums"), core.sig("norms"), core.sig("rnorms")
        excl_arg, exps, dve_steps = core.sig("excl_arg"), core.sig("exps"), core.sig("dve_steps")

        with nc.Block() as block:
            @block.sync
            def _(sp):
                for i, n in enumerate(loaded):
                    sp.dma_start(buf[n][:], core.spill["w" if n == "z" else n][t]).then_inc(*proj_in[i].by(16))
                for name in ("k_k", "k_a"):
                    sp.dma_start(vec[name][:], io["rwkv_" + name].broadcast_to([P, D])).then_inc(*vec_in.by(16))
                sp.dma_start(vec["r_k"][:], io["rwkv_r_k"].rearrange("a h n -> a (h n)").broadcast_to([P, D])).then_inc(*vec_in.by(16))
                if t == 2:
                    for b in range(DEC_BATCH):
                        sp.dma_start(w["natural"][:, b], by_value(io["state_wkv"][0, b])).then_inc(*core.sig("states_in").by(16))
                sp.wait_ge(*proj_in[loaded.index("g")].at(16))

            @block.scalar
            def _(act):
                act.wait_ge(*proj_in[0].at(16))
                act.activation(z, z, ACT.Sigmoid).then_inc(*gates.by())
                act.wait_ge(*proj_in[1].at(16))
                act.activation(a, a, ACT.Sigmoid).then_inc(*gates.by())
                act.wait_ge(*norms.at(1))
                act.activation(rnorm[:], norm2[:], ACT.Sqrt).then_inc(*rnorms.by())
                act.wait_ge(*sums.at(2))
                act.activation(e_incl[:], run[:], ACT.Exp).then_inc(*exps.by())
                act.activation(e_neg[:], run[:], ACT.Exp, scale=-1.0).then_inc(*exps.by())
                act.activation(w["e_end"][:], end[:], ACT.Exp).then_inc(*exps.by())
                act.wait_ge(*excl_arg.at(1))
                act.activation(e_excl[:], e_excl[:], ACT.Exp).then_inc(*exps.by())

            @block.tensor
            def _(pe):
                pe.wait_ge(*logd.at(1))
                _, incl = core.const("strict_incl")[:, 0:P], core.const("strict_incl")[:, P:]
                for out, ones in ((run, incl), (end, core.const("block"))):
                    for h in range(2):
                        mm = pe.matmul(out[:, h * HALF:(h + 1) * HALF], ones, z[:, h * HALF:(h + 1) * HALF])
                    mm.then_inc(*sums.by())

            @block.vector
            def _(dve):
                own = in_order(dve, dve_steps)
                dve.wait_ge(*gates.at(1))
                own(dve.tensor_scalar(z, z, DECAY_SCALE, None, ALU.mult))
                dve.sem_inc(*logd.by())
                dve.wait_ge(*vec_in.at(48))
                dve.wait_ge(*proj_in[2].at(16))
                own(dve.tensor_tensor(kk[:], k, vec["k_k"][:], ALU.mult))
                own(dve.tensor_tensor(tmp[:], kk[:], kk[:], ALU.mult))
                own(dve.tensor_reduce(norm2[:], heads(tmp[:]), AX.X, ALU.add))
                own(dve.tensor_scalar(norm2[:], norm2[:], 1e-24, None, ALU.max))
                own(dve.reciprocal(norm2[:], norm2[:]))
                dve.sem_inc(*norms.by())
                dve.wait_ge(*gates.at(2))
                own(dve.scalar_tensor_tensor(tmp[:], a, -1.0, vec["k_a"][:], ALU.add, ALU.mult))
                own(dve.scalar_tensor_tensor(k, tmp[:], 1.0, k, ALU.add, ALU.mult))
                dve.wait_ge(*proj_in[3].at(16))
                own(dve.tensor_tensor(tmp[:], r, k, ALU.mult))
                own(dve.tensor_tensor(tmp[:], tmp[:], vec["r_k"][:], ALU.mult))
                own(dve.tensor_reduce(bonus_dot[:], heads(tmp[:]), AX.X, ALU.add))
                dve.wait_ge(*proj_in[4].at(16))
                dve.tensor_tensor(heads(w["bonus"][:]), heads(v), bonus_dot[:].unsqueeze(2).broadcast_to([P, H, N]), ALU.mult)
                dve.wait_ge(*rnorms.at(1))
                own(dve.tensor_tensor(heads(kk[:]), heads(kk[:]), rnorm[:].unsqueeze(2).broadcast_to([P, H, N]), ALU.mult))
                own(dve.tensor_tensor(kka[:], kk[:], a, ALU.mult))
                dve.wait_ge(*exps.at(2))
                own(dve.tensor_tensor(e_excl[:], run[:], z, ALU.subtract))
                dve.sem_inc(*excl_arg.by())
                dve.wait_ge(*exps.at(3))
                dve.tensor_tensor(r, r, e_incl[:], ALU.mult)
                own(dve.scalar_tensor_tensor(w["B"][:], kka[:], -1.0, e_neg[:], ALU.mult, ALU.mult))
                own(dve.tensor_tensor(k, k, e_neg[:], ALU.mult))
                dve.tensor_tensor(w["B_end"][:], w["B"][:], w["e_end"][:], ALU.mult)
                dve.tensor_tensor(w["K_end"][:], k, w["e_end"][:], ALU.mult)
                dve.wait_ge(*exps.at(4))
                own(dve.tensor_tensor(a, kk[:], e_excl[:], ALU.mult))
        core.end_stage()


def by_value(state):
    return state.rearrange("h v k -> v h k")


def wkv_chunks(core, buf, w, t):
    nc = core.nc
    GH, GP = 4, 2
    NG = H // GH
    ident = core.const("ident")
    token = {"A": buf["a"], "R": buf["r"], "B": w["B"], "K": buf["k"]}
    v = buf["v"]
    with ExitStack() as ctx:
        def sb(name, shape, dt=F32):
            return ctx.enter_context(nc.sbuf_tensor(f"{name}_{t}", shape, dt))

        feat = sb("feat", [P, 2, GP, 3, P])
        own_ar = sb("own_ar", [P, GH, 2, P])
        by_b = sb("by_b", [P, 2, GH, 2 * P])
        by_k = sb("by_k", [P, 2, GH, 2 * P])
        m1, m2, m4 = (sb(n, [P, GH, P]) for n in ("m1", "m2", "m4"))
        m2t, m4t, m8t = (sb(n, [P, 2, GH, P]) for n in ("m2t", "m4t", "m8t"))
        x = sb("x", [P, 2, 2, GH, 2 * N])
        B_by_chunk, K_by_chunk = sb("B_by_chunk", [P, GH, NCH, N]), sb("K_by_chunk", [P, GH, NCH, N])
        p_end = sb("p_end", [P, GP, NCH])
        decay_diag = sb("decay_diag", [P, GP, NCH, N])
        bank = [ctx.enter_context(nc.psum_tensor(f"bank{i}_{t}", [P, HALF], F32)) for i in range(8)]

        tp, feat_done = core.sig("tp"), core.sig("feat_done")
        gram, gram_done = core.sig("gram"), core.sig("gram_done")
        nv, nv_done, x_done, pw, pw_done = core.sig("nv"), core.sig("nv_done"), core.sig("x_done"), core.sig("pw"), core.sig("pw_done")
        xp, q1, q1_done, y2, y2_done = core.sig("xp"), core.sig("q1"), core.sig("q1_done"), core.sig("y2"), core.sig("y2_done")
        pend_done, diag_done, exp_done = core.sig("pend_done"), core.sig("diag_done"), core.sig("exp_done")
        fp, fp_done, gp, gp_done = core.sig("fp"), core.sig("fp_done"), core.sig("gp"), core.sig("gp_done")
        a_copied, zeroed = core.sig("a_copied"), core.sig("zeroed")
        quad = lambda b, n: b[:, 0:GH * n].rearrange("p (h n) -> p h n", h=GH)
        pairs = lambda b: b[:, 0:GP * P].rearrange("p (q t) -> p q t", q=GP)
        half = lambda h: slice(h % 2 * N, (h % 2 + 1) * N)
        head = lambda g, h: slice((g * GH + h) * N, (g * GH + h + 1) * N)
        pair = lambda g, q: slice((g * GP + q) * P, (g * GP + q + 1) * P)

        with nc.Block() as block:
            @block.tensor
            def _(pe):
                def features(g):
                    if g > 0:
                        pe.wait_ge(*pw_done.at(5 * g))
                    for q in range(GP):
                        for i, n in enumerate("ARBK"):
                            mm = pe.transpose(bank[q][:, i * P:(i + 1) * P], token[n][:, pair(g, q)], ident)
                        mm.then_inc(*tp.by())

                def products(g, n, first):
                    pe.wait_ge(*feat_done.at(3 * GP * (g + 1)))
                    for h in range(GH):
                        q, r = divmod(h, 2)
                        mm = pe.matmul(bank[first + q][:, r * 2 * P:(r + 1) * 2 * P], feat[:, g % 2, q, n, :], own_ar[:, h].rearrange("k i t -> k (i t)"))
                        if r:
                            mm.then_inc(*gram.by())

                def product_m(g):
                    pe.wait_ge(*gram_done.at(5 * g + 1))
                    for h in range(GH):
                        mm = pe.matmul(bank[2][:, h * P:(h + 1) * P], own_ar[:, h, 0, :], feat[:, g % 2, h // 2, 1, :])
                    mm.then_inc(*gram.by())

                def weigh_values(g):
                    pe.wait_ge(*gram_done.at(5 * g + 4))
                    for h in range(GH):
                        pe.matmul(bank[0][:, h * N:(h + 1) * N], by_k[:, g % 2, h, 0:P], v[:, head(g, h)])
                    for q in range(GP):
                        mm = pe.matmul(bank[0][:, GH * N + q * NCH:GH * N + (q + 1) * NCH], w["e_end"][:, pair(g, q)], core.const("first"))
                    mm.then_inc(*nv.by())

                def squares(g, out, left, right):
                    for h in range(GH):
                        mm = pe.matmul(bank[out][:, h * P:(h + 1) * P], left[:, h], right[:, h])
                    mm.then_inc(*pw.by())

                def second_powers(g):
                    pe.wait_ge(*gram_done.at(5 * g + 5))
                    squares(g, 1, m1, by_b[:, g % 2, :, 0:P])
                    squares(g, 2, by_b[:, g % 2, :, 0:P], m1)

                def fourth_power_t(g):
                    pe.wait_ge(*pw_done.at(5 * g + 2))
                    squares(g, 3, m2, m2t[:, g % 2])

                def fourth_power(g):
                    pe.wait_ge(*nv_done.at(g + 1))
                    pe.wait_ge(*pend_done.at(g + 1))
                    squares(g, 0, m2t[:, g % 2], m2)

                def eighth_power_t(g):
                    pe.wait_ge(*pw_done.at(5 * g + 4))
                    squares(g, 1, m4, m4t[:, g % 2])

                def apply(g, i, power):
                    if i == 0:
                        pe.wait_ge(*nv_done.at(g + 1))
                        pe.wait_ge(*a_copied.at(g + 1))
                        pe.wait_ge(*pw_done.at(5 * (g + 1)))
                        if g > 0:
                            pe.wait_ge(*fp_done.at(GP * g))
                    else:
                        pe.wait_ge(*x_done.at(4 * g + i))
                    for h in range(GH):
                        mm = pe.matmul(bank[4 + i % 2][:, h * P:(h + 1) * P], power[:, h], x[:, g % 2, i % 2, h, :])
                    mm.then_inc(*xp.by())

                def outputs(g):
                    pe.wait_ge(*x_done.at(4 * g + 4))
                    if g > 0:
                        pe.wait_ge(*gp_done.at(GP * g))
                    for h in range(GH):
                        mm = pe.matmul(bank[6][half(h), h // 2 * P:(h // 2 + 1) * P], x[:, g % 2, 0, h, 0:N], by_b[:, g % 2, h, P:], tile_position=(0, h % 2 * N))
                    mm.then_inc(*q1.by())
                    for h in range(GH):
                        out = bank[7][half(h), h // 2 * P:(h // 2 + 1) * P]
                        pe.matmul(out, x[:, g % 2, 0, h, N:], by_b[:, g % 2, h, P:], start=True, stop=False, tile_position=(0, h % 2 * N))
                        mm = pe.matmul(out, v[:, head(g, h)], by_k[:, g % 2, h, P:], start=False, stop=True, tile_position=(0, h % 2 * N))
                    mm.then_inc(*y2.by())

                def state_factors(g):
                    pe.wait_ge(*exp_done.at(2 * GH * (g + 1)))
                    for q in range(GP):
                        for h in (2 * q, 2 * q + 1):
                            mm = pe.matmul(bank[4 + q][half(h), :], x[:, g % 2, 0, h, 0:N], B_by_chunk[:, h].rearrange("p c n -> p (c n)"), tile_position=(0, h % 2 * N))
                        mm.then_inc(*fp.by())

                def state_terms(g, q):
                    pe.wait_ge(*(q1_done, y2_done)[q].at(g + 1))
                    for c in range(NCH):
                        for h in (2 * q, 2 * q + 1):
                            out = bank[6 + q][half(h), c * N:(c + 1) * N]
                            pe.matmul(out, B_by_chunk[:, h, c, :], x[:, g % 2, 0, h, N:], start=True, stop=False, tile_position=(0, h % 2 * N))
                            mm = pe.matmul(out, K_by_chunk[:, h, c, :], v[:, head(g, h)], start=False, stop=True, tile_position=(0, h % 2 * N))
                    mm.then_inc(*gp.by())

                for g in range(NG + 1):
                    front, b = g < NG, g - 1
                    back = b >= 0
                    if front:
                        features(g)
                    if back:
                        apply(b, 0, by_b[:, b % 2, :, 0:P])
                    if front:
                        products(g, 1, 2)
                        products(g, 2, 0)
                    if back:
                        apply(b, 1, m2t[:, b % 2])
                    if front:
                        product_m(g)
                    if back:
                        apply(b, 2, m4t[:, b % 2])
                    if front:
                        weigh_values(g)
                    if back:
                        apply(b, 3, m8t[:, b % 2])
                    if front:
                        second_powers(g)
                    if back:
                        outputs(b)
                    if front:
                        fourth_power_t(g)
                    if back:
                        state_factors(b)
                    if front:
                        fourth_power(g)
                    if back:
                        state_terms(b, 0)
                    if front:
                        eighth_power_t(g)
                    if back:
                        state_terms(b, 1)

            @block.scalar
            def _(act):
                def power(g, i, dst, b):
                    act.wait_ge(*pw.at(5 * g + i + 1))
                    act.copy(dst[:] if i in (1, 3) else dst[:, g % 2], quad(bank[b], P)).then_inc(*pw_done.by())

                def terms(g, q):
                    act.wait_ge(*gp.at(GP * g + q + 1))
                    act.copy(w["G"][:, 1:, g * GP + q, :], bank[6 + q].rearrange("k (c n) -> k c n", n=N)).then_inc(*gp_done.by())

                for g in range(NG + 1):
                    front, b = g < NG, g - 1
                    back = b >= 0
                    if front:
                        act.wait_ge(*zeroed.at(1))
                        if g > 0:
                            act.wait_ge(*gram.at(5 * g))
                        if g >= 2:
                            act.wait_ge(*q1_done.at(g - 1))
                        for q in range(GP):
                            act.wait_ge(*tp.at(GP * g + q + 1))
                            act.copy(feat[:, g % 2, q].rearrange("k i t -> k (i t)"), bank[q][:, P:]).then_inc(*feat_done.by())
                            for h in (2 * q, 2 * q + 1):
                                act.copy(own_ar[half(h), h].rearrange("k i t -> k (i t)"), bank[q][half(h), 0:2 * P]).then_inc(*feat_done.by())
                        if g >= 2:
                            act.wait_ge(*xp.at(4 * (g - 1)))
                        power(g, 0, m2t, 1)
                        power(g, 1, m2, 2)
                    if back:
                        act.wait_ge(*y2.at(b + 1))
                        act.copy(w["Y2t"][:, b * GP:(b + 1) * GP, :], pairs(bank[7])).then_inc(*y2_done.by())
                    if front:
                        power(g, 2, m4t, 3)
                        power(g, 3, m4, 0)
                    if back:
                        terms(b, 0)
                    if front:
                        power(g, 4, m8t, 1)
                    if back:
                        terms(b, 1)

            @block.vector
            def _(dve):
                both = core.const("strict_incl").unsqueeze(1).broadcast_to([P, GP, 2 * P])
                lower = core.const("lower").unsqueeze(1).broadcast_to([P, GH, P])

                def masked(g, n, dst, first):
                    for q in range(GP):
                        dve.wait_ge(*gram.at(5 * g + 2 * n + q + 1))
                        dve.tensor_tensor(dst[:, g % 2, 2 * q:2 * q + 2, :], bank[first + q].rearrange("p (h s) -> p h s", h=2), both, ALU.mult).then_inc(*gram_done.by())

                def masked_m(g):
                    dve.wait_ge(*gram.at(5 * g + 5))
                    dve.tensor_tensor(m1[:], quad(bank[2], P), lower, ALU.mult).then_inc(*gram_done.by())

                def values(g):
                    dve.wait_ge(*nv.at(g + 1))
                    dve.tensor_copy(x[:, g % 2, 0, :, N:], quad(bank[0], N)).then_inc(*nv_done.by())
                    if g > 0:
                        dve.wait_ge(*diag_done.at(g))
                    dve.tensor_copy(p_end[:].rearrange("k h c -> k (h c)"), bank[0][:, GH * N:GH * N + GP * NCH]).then_inc(*pend_done.by())

                def add(g, i):
                    if i == 0:
                        dve.wait_ge(*nv_done.at(g + 1))
                        dve.wait_ge(*a_copied.at(g + 1))
                    else:
                        dve.wait_ge(*x_done.at(4 * g + i))
                    dve.wait_ge(*xp.at(4 * g + i + 1))
                    dve.tensor_tensor(x[:, g % 2, (i + 1) % 2], quad(bank[4 + i % 2], P), x[:, g % 2, i % 2], ALU.add).then_inc(*x_done.by())

                for g in range(NG + 1):
                    front, b = g < NG, g - 1
                    back = b >= 0
                    if back:
                        add(b, 0)
                    if front:
                        if g >= 2:
                            dve.wait_ge(*y2.at(g - 1))
                        masked(g, 0, by_b, 2)
                        masked(g, 1, by_k, 0)
                    if back:
                        add(b, 1)
                    if front:
                        masked_m(g)
                    if back:
                        add(b, 2)
                    if front:
                        if g >= 2:
                            dve.wait_ge(*gp.at(GP * (g - 1)))
                        values(g)
                    if back:
                        add(b, 3)
                        dve.wait_ge(*q1.at(b + 1))
                        dve.tensor_tensor(w["Q1t"][:, b * GP:(b + 1) * GP, :], pairs(bank[6]), feat[:, b % 2, :, 0, :], ALU.add).then_inc(*q1_done.by())
                        dve.wait_ge(*diag_done.at(b + 1))
                        for q in range(GP):
                            dve.wait_ge(*fp.at(GP * b + q + 1))
                            dve.tensor_tensor(w["Ft"][:, :, b * GP + q, :], bank[4 + q].rearrange("k (c n) -> k c n", n=N), decay_diag[:, q], ALU.add).then_inc(*fp_done.by())

            @block.gpsimd
            def _(pool):
                spread = core.const("chunk").unsqueeze(2).broadcast_to([P, NCH, N])

                def copy_a(g):
                    if g >= 2:
                        pool.wait_ge(*gp.at(GP * (g - 1)))
                    pool.tensor_copy(x[:, g % 2, 0, :, 0:N], token["A"][:, g * GH * N:(g + 1) * GH * N].rearrange("p (h n) -> p h n", n=N)).then_inc(*a_copied.by())

                pool.memset(own_ar[:], 0.0).then_inc(*zeroed.by())
                copy_a(0)
                for g in range(NG):
                    if g + 1 < NG:
                        copy_a(g + 1)
                    if g > 0:
                        pool.wait_ge(*gp.at(GP * g))
                    for h in range(GH):
                        for dst, src in ((B_by_chunk, w["B_end"]), (K_by_chunk, w["K_end"])):
                            pool.tensor_tensor(dst[:, h], src[:, head(g, h)].unsqueeze(1).broadcast_to([P, NCH, N]), spread, ALU.mult).then_inc(*exp_done.by())
                    pool.wait_ge(*pend_done.at(g + 1))
                    if g > 0:
                        pool.wait_ge(*fp_done.at(GP * g))
                    for q in range(GP):
                        ins = pool.tensor_tensor(decay_diag[:, q], core.const("pair_ident").unsqueeze(1).broadcast_to([P, NCH, N]),
                                                 p_end[:, q, :].unsqueeze(2).broadcast_to([P, NCH, N]), ALU.mult)
                    ins.then_inc(*diag_done.by())
        core.end_stage()


def wkv_states(core, io, buf, w, t):
    nc = core.nc
    ident = core.const("ident")
    G, Ft, carry = w["G"], w["Ft"], w["carry"]
    sample = t == 2
    St = w["start"] if sample else G
    PAIRS, PH2 = H // 2, H // 4
    half = lambda r: slice(r * N, (r + 1) * N)
    with ExitStack() as ctx:
        def sb(name, shape, dt=F32):
            return ctx.enter_context(nc.sbuf_tensor(f"{name}_{t}", shape, dt))

        natural = w["natural"]
        Yt = sb("Yt", [P, PAIRS, P])
        bank = [ctx.enter_context(nc.psum_tensor(f"sbank{i}_{t}", [P, HALF], F32)) for i in range(8)]
        state_in, s_psum, s_done = core.sig("states_in"), core.sig("s_psum"), core.sig("s_done")
        step_psum, step_done = core.sig("step_psum"), core.sig("step_done")
        y_psum, y_sum, y_tok, y_tok_done = core.sig("rows_psum"), core.sig("rows_copied"), core.sig("y_tok"), core.sig("y_tok_done")
        fin_psum, fin_done, fin_out = core.sig("fin_psum"), core.sig("fin_done"), core.sig("fin_out")
        first = core.sig("first_state")
        finals = range(DEC_BATCH) if sample else range(1) if t == 1 else ()

        with nc.Block() as block:
            if sample:
                @block.sync
                def _(sp):
                    for b in range(DEC_BATCH):
                        sp.wait_ge(*fin_done.at(2 * b + 2))
                        sp.dma_start(by_value(io["wkv_s"][0, b]), natural[:, b]).then_inc(*fin_out.by(16))
            elif t == 1:
                @block.sync
                def _(sp):
                    sp.wait_ge(*fin_done.at(2))
                    sp.dma_start(by_value(io["wkv_p"][0, 0]), natural[:, 0]).then_inc(*fin_out.by(16))

            @block.tensor
            def _(pe):
                def step(c, part):
                    for i in range(PH2):
                        for r in range(2):
                            mm = pe.matmul(bank[2 * (c % 2) + part][half(r), i * N:(i + 1) * N], Ft[half(r), c, PH2 * part + i, :],
                                           St[half(r), c, PH2 * part + i, :], tile_position=(r * N, r * N))
                    mm.then_inc(*step_psum.by())

                def outputs(part):
                    for i in range(PH2):
                        for c in range(NCH):
                            for r in range(2):
                                mm = pe.matmul(bank[4 + part][half(r), i * P + c * L:i * P + (c + 1) * L], St[half(r), c, PH2 * part + i, :],
                                               w["Q1t"][half(r), PH2 * part + i, c * L:(c + 1) * L], tile_position=(r * N, r * N))
                    mm.then_inc(*y_psum.by())

                if sample:
                    pe.wait_ge(*state_in.at(0))
                    for b in range(DEC_BATCH):
                        if b >= 2:
                            pe.wait_ge(*s_done.at(b - 1))
                        for q in range(PAIRS):
                            mm = pe.transpose(bank[6 + b % 2][:, q * N:(q + 1) * N], natural[:, b, 2 * q:2 * q + 2, :].rearrange("v r k -> v (r k)"), ident[0:N, 0:N])
                        mm.then_inc(*s_psum.by())
                    pe.wait_ge(*s_done.at(DEC_BATCH))
                else:
                    pe.wait_ge(*first.at(1))
                for c in range(NCH):
                    for part in range(2):
                        if c > 0 and not sample:
                            pe.wait_ge(*step_done.at(2 * c - 1 + part))
                        elif c > 1:
                            pe.wait_ge(*step_done.at(2 * c - 3 + part))
                        step(c, part)
                for part in range(2):
                    if not sample:
                        pe.wait_ge(*step_done.at(2 * NCH - 3 + part))
                    outputs(part)
                pe.wait_ge(*step_done.at(2 * NCH))
                for part in range(2):
                    pe.wait_ge(*y_sum.at(part + 1))
                    for i in range(PH2):
                        mm = pe.transpose(bank[part][:, i * P:(i + 1) * P], Yt[:, PH2 * part + i, :], ident)
                    mm.then_inc(*y_tok.by())
                for b in finals:
                    for part in range(2):
                        n = 2 * b + part
                        if n >= 2:
                            pe.wait_ge(*fin_done.at(n - 1))
                        for i in range(PH2):
                            src = G[:, b + 1 if sample else NCH, PH2 * part + i, :]
                            mm = pe.transpose(bank[2 + n % 2][0:N, i * P:(i + 1) * P], src, ident)
                        mm.then_inc(*fin_psum.by())

            @block.vector
            def _(dve):
                if t == 0:
                    dve.memset(St[:, 0], 0.0).then_inc(*first.by())
                elif t == 1:
                    dve.tensor_copy(St[:, 0], carry[:]).then_inc(*first.by())
                for c in range(NCH):
                    for part in range(2):
                        dve.wait_ge(*step_psum.at(2 * c + part + 1))
                        dst = G[:, c + 1, PH2 * part:PH2 * (part + 1), :]
                        dve.tensor_tensor(dst, bank[2 * (c % 2) + part][:, 0:PH2 * N].rearrange("k (q v) -> k q v", v=N), dst, ALU.add).then_inc(*step_done.by())
                if t == 0:
                    dve.wait_ge(*step_done.at(2 * NCH))
                    dve.tensor_copy(carry[:], G[:, NCH])
                for part in range(2):
                    dve.wait_ge(*y_psum.at(part + 1))
                    qs = slice(PH2 * part, PH2 * (part + 1))
                    dve.tensor_tensor(Yt[:, qs, :], bank[4 + part][:].rearrange("k (q t) -> k q t", t=P), w["Y2t"][:, qs, :], ALU.add).then_inc(*y_sum.by())

            @block.scalar
            def _(act):
                if sample:
                    for b in range(DEC_BATCH):
                        act.wait_ge(*s_psum.at(b + 1))
                        act.copy(St[:, b], bank[6 + b % 2].rearrange("k (q v) -> k q v", v=N)).then_inc(*s_done.by())
                for part in range(2):
                    act.wait_ge(*y_tok.at(part + 1))
                    act.copy(w["y"][:, part * HALF:(part + 1) * HALF], bank[part][:]).then_inc(*y_tok_done.by())
                for b in finals:
                    for part in range(2):
                        n = 2 * b + part
                        act.wait_ge(*fin_psum.at(n + 1))
                        act.copy(natural[:, b, 8 * part:8 * part + 8, :].rearrange("v h k -> v (h k)"), bank[2 + n % 2][0:N, :]).then_inc(*fin_done.by())
        core.end_stage()


def wkv_states_and_outputs(core, io, buf, w, t):
    with ExitStack() as ctx:
        if t == 2:
            w["start"] = ctx.enter_context(core.nc.sbuf_tensor("wkv_start", [P, NCH, H // 2, N], F32))
        wkv_states(core, io, buf, w, t)
    wkv_outputs(core, io, buf, w, t)


def load_rows(core, io, gated):
    rows_back = core.sig("rows_back")
    with core.nc.Block() as block:
        @block.sync
        def _(sp):
            for t in range(TILES):
                sp.dma_start(core.x_tok[:, t, :], row_tile(io["x_prompt"], io["x_sample"], t)).then_inc(*rows_back.by(16))
            sp.dma_start(gated[:], core.spill["g"].rearrange("t p d -> p t d")).then_inc(*rows_back.by(16))
            sp.wait_ge(*rows_back.at(16 * (TILES + 1)))
    core.end_stage()


def wkv_outputs(core, io, buf, w, t):
    nc = core.nc
    y, gate = w["y"], buf["g"][:]
    heads = lambda x: x.rearrange("p (h n) -> p h n", n=N)
    wide = lambda x: x[:].unsqueeze(2).broadcast_to([P, H, N])
    with ExitStack() as ctx:
        def sb(name, shape, dt=F32):
            return ctx.enter_context(nc.sbuf_tensor(f"{name}_{t}", shape, dt))

        sq, mean, var, rstd = sb("sq", [P, D]), sb("mean", [P, H]), sb("var", [P, H]), sb("rstd", [P, H])
        lnx_g, lnx_b = sb("lnx_g", [P, D]), sb("lnx_b", [P, D])
        gated, gated_out = core.sig("gated"), core.sig("gated_out")
        lnx_in, var_done, rstd_done, dve_steps = core.sig("vectors_in"), core.sig("var_done"), core.sig("rstd_done"), core.sig("dve_steps")
        with nc.Block() as block:
            @block.sync
            def _(sp):
                sp.dma_start(lnx_g[:], io["rwkv_lnx_g"].broadcast_to([P, D])).then_inc(*lnx_in.by(16))
                sp.dma_start(lnx_b[:], io["rwkv_lnx_b"].broadcast_to([P, D])).then_inc(*lnx_in.by(16))
                sp.wait_ge(*gated.at(1))
                sp.dma_start(core.spill["g"][t], gate).then_inc(*gated_out.by(16))
                sp.wait_ge(*gated_out.at(16))
                sp.wait_ge(*core.sig("fin_out").at(0))

            @block.scalar
            def _(act):
                act.wait_ge(*var_done.at(1))
                act.activation(rstd[:], var[:], ACT.Sqrt).then_inc(*rstd_done.by())

            @block.vector
            def _(dve):
                own = in_order(dve, dve_steps)
                own(dve.tensor_reduce(mean[:], heads(y[:]), AX.X, ALU.add))
                own(dve.tensor_scalar(mean[:], mean[:], 1.0 / N, None, ALU.mult))
                own(dve.tensor_tensor(heads(y[:]), heads(y[:]), wide(mean), ALU.subtract))
                own(dve.tensor_tensor(sq[:], y[:], y[:], ALU.mult))
                own(dve.tensor_reduce(var[:], heads(sq[:]), AX.X, ALU.add))
                own(dve.tensor_scalar(var[:], var[:], 1.0 / N, GN_EPS, ALU.mult, ALU.add))
                own(dve.reciprocal(var[:], var[:]))
                dve.sem_inc(*var_done.by())
                dve.wait_ge(*lnx_in.at(32))
                dve.wait_ge(*rstd_done.at(1))
                own(dve.tensor_tensor(heads(y[:]), heads(y[:]), wide(rstd), ALU.mult))
                own(dve.tensor_tensor(y[:], y[:], lnx_g[:], ALU.mult))
                own(dve.tensor_tensor(y[:], y[:], lnx_b[:], ALU.add))
                own(dve.tensor_tensor(y[:], y[:], w["bonus"][:], ALU.add))
                dve.tensor_tensor(gate, y[:], gate, ALU.mult).then_inc(*gated.by())
        core.end_stage()


def to_features(core, src, dst, name):
    nc = core.nc
    with ExitStack() as ctx:
        bank = [ctx.enter_context(nc.psum_tensor(f"tf{i}_{name}", [P, TOK], F32)) for i in range(4)]
        tf_psum, tf_act, tf_dve = core.sig("rows_psum"), core.sig("copied_act"), core.sig("copied_dve")
        with nc.Block() as block:
            @block.tensor
            def _(pe):
                for k in range(KD):
                    if k >= 4:
                        pe.wait_ge(*(tf_act, tf_dve)[k % 2].at((k - 4) // 2 + 1))
                    for t in range(TILES):
                        mm = pe.transpose(bank[k % 4][:, t * P:(t + 1) * P], src[:, t, k * P:(k + 1) * P], core.const("ident"))
                    mm.then_inc(*tf_psum.by())

            @block.scalar
            def _(act):
                for k in range(0, KD, 2):
                    act.wait_ge(*tf_psum.at(k + 1))
                    act.copy(dst[:, k, :], bank[k % 4][:]).then_inc(*tf_act.by())

            @block.vector
            def _(dve):
                for k in range(1, KD, 2):
                    dve.wait_ge(*tf_psum.at(k + 1))
                    dve.tensor_copy(dst[:, k, :], bank[k % 4][:]).then_inc(*tf_dve.by())
        core.end_stage()


def layer_norm_steps(core, dve, own, res, out, g, b, stats, mv, rstd, n):
    for half in range(2):
        ins = dve.bn_stats(stats[:, half, :], res[:, half * HALF:(half + 1) * HALF])
    own(ins)
    own(dve.bn_aggr(mv[:], stats[:].rearrange("p a s -> p (a s)")))
    own(dve.tensor_scalar(mv[:, 1:2], mv[:, 1:2], LN_EPS, None, ALU.add))
    own(dve.reciprocal(mv[:, 1:2], mv[:, 1:2]))
    dve.sem_inc(*core.sig("ln_var").by())
    dve.wait_ge(*core.sig("ln_rstd").at(n))
    own(dve.tensor_scalar(res, res, mv[:, 0:1], rstd[:], ALU.subtract, ALU.mult))
    own(dve.tensor_tensor(res, res, g, ALU.mult))
    own(dve.tensor_tensor(out, res, b, ALU.add))


def layer_norm_roots(core, act, mv, rstd, tiles=range(TILES)):
    for t in tiles:
        act.wait_ge(*core.sig("ln_var").at(t + 1))
        act.activation(rstd[:], mv[:, 1:2], ACT.Sqrt).then_inc(*core.sig("ln_rstd").by())


def project_and_norm(core, io, actT, weight, layer, name):
    nc = core.nc
    with ExitStack() as ctx:
        def sb(name_, shape, dt=F32):
            return ctx.enter_context(nc.sbuf_tensor(f"{name_}_{name}", shape, dt))

        wt = sb("pn_w", [P, KD, D])
        g, b = sb("pn_g", [P, D]), sb("pn_b", [P, D])
        res = sb("pn_res", [P, 2, D])
        stats, mv, rstd = sb("pn_stats", [P, 2, 6]), sb("pn_mv", [P, 2]), sb("pn_rstd", [P, 1])
        acc = ctx.enter_context(nc.psum_tensor(f"pn_acc_{name}", [P, TILES, D], F32))
        pn_w = [core.sig(f"loaded{k}") for k in range(KD)]
        pn_vec, pn_psum, dve_steps = core.sig("vectors_in"), core.sig("rows_psum"), core.sig("dve_steps")
        core.sig("ln_var"), core.sig("ln_rstd")
        with nc.Block() as block:
            @block.sync
            def _(sp):
                for k in range(KD):
                    sp.dma_start(wt[:, k, :], weight[k * P:(k + 1) * P, :]).then_inc(*pn_w[k].by(16))
                sp.dma_start(g[:], io["ln_mix_g"][layer:layer + 1, :].broadcast_to([P, D])).then_inc(*pn_vec.by(16))
                sp.dma_start(b[:], io["ln_mix_b"][layer:layer + 1, :].broadcast_to([P, D])).then_inc(*pn_vec.by(16))

            @block.tensor
            def _(pe):
                for t in range(TILES):
                    for k in range(KD):
                        if t == 0:
                            pe.wait_ge(*pn_w[k].at(16))
                        for h in range(2):
                            mm = pe.matmul(acc[:, t, h * HALF:(h + 1) * HALF], actT[:, k, t * P:(t + 1) * P],
                                           wt[:, k, h * HALF:(h + 1) * HALF], start=(k == 0), stop=(k == KD - 1))
                    mm.then_inc(*pn_psum.by())

            @block.scalar
            def _(act):
                layer_norm_roots(core, act, mv, rstd)

            @block.vector
            def _(dve):
                own = in_order(dve, dve_steps)
                dve.wait_ge(*pn_vec.at(32))
                for t in range(TILES):
                    dve.wait_ge(*pn_psum.at(t + 1))
                    x = core.x_tok[:, t, :]
                    own(dve.scalar_tensor_tensor(res[:, t % 2], x, ALPHA, acc[:, t, :], ALU.mult, ALU.add))
                    layer_norm_steps(core, dve, own, res[:, t % 2], x, g[:], b[:], stats, mv, rstd, t + 1)
        core.end_stage()


class KeyScores:

    HC = 2 * PH
    PAIR = 2 * P

    def __init__(self, core, io, ctx, xT, scores, layer, tiles, ring):
        def sb(name, shape, dt=F32):
            return ctx.enter_context(core.nc.sbuf_tensor(f"{name}_{layer}_{tiles[0]}", shape, dt))

        self.core, self.io, self.xT, self.scores, self.layer, self.tiles, self.ring = core, io, xT, scores, layer, tiles, ring
        self.rows = slice(tiles[0] * P, (tiles[-1] + 1) * P)
        self.width = len(tiles) * P
        self.wq = sb("wq", [P, ring, KD, self.PAIR])
        self.keys, self.keysT = sb("keys", [P, 2, P]), sb("keysT", [P, 2, P])
        self.qT = sb("qT", [P, self.HC, self.width])
        self.bank = [ctx.enter_context(core.nc.psum_tensor(f"pbank{i}_{layer}_{tiles[0]}", [P, HALF], F32)) for i in range(6)]
        self.wq_in = [core.sig(f"loaded{i}") for i in range(ring)]
        self.keys_in, self.keys_psum, self.keys_done = core.sig(f"loaded{ring}"), core.sig("keysT_psum"), core.sig("keys_done")
        self.q_psum, self.q_done = core.sig("rows_psum"), core.sig("rows_copied")
        self.s_psum, self.s_done = core.sig("s_psum"), core.sig("ps_done")

    def loads(self, sp):
        sp.dma_start(self.keys[:], self.io["peer_sub_keys"][self.layer].rearrange("c k d -> k c d")).then_inc(*self.keys_in.by(16))
        for i in range(PH):
            if i >= self.ring:
                sp.wait_ge(*self.q_psum.at(2 * (i - self.ring) + 2))
            sp.dma_start(self.wq[:, i % self.ring], by_chunk(self.io["peer_w_query"][self.layer][:, i * self.PAIR:(i + 1) * self.PAIR])).then_inc(*self.wq_in[i % self.ring].by(16))

    def products(self, pe):
        pe.wait_ge(*self.keys_in.at(16))
        for c in range(2):
            mm = pe.transpose(self.bank[5][:, c * P:(c + 1) * P], self.keys[:, c, :], self.core.const("ident"))
        mm.then_inc(*self.keys_psum.by())
        for m in range(self.HC):
            if m % 2 == 0:
                pe.wait_ge(*self.wq_in[m // 2 % self.ring].at(16 * (m // 2 // self.ring + 1)))
            if m >= 3:
                pe.wait_ge(*self.q_done.at(m - 2))
            for k in range(KD):
                mm = pe.matmul(self.bank[m % 3][:, 0:self.width], self.wq[:, m // 2 % self.ring, k, (m % 2) * P:(m % 2 + 1) * P],
                               self.xT[:, k, self.rows], start=(k == 0), stop=(k == KD - 1))
            mm.then_inc(*self.q_psum.by())
        pe.wait_ge(*self.keys_done.at(1))
        pe.wait_ge(*self.q_done.at(self.HC))
        n = 0
        for t in range(len(self.tiles)):
            for q in range(self.HC // 4):
                if n >= 3:
                    pe.wait_ge(*self.s_done.at(n - 2))
                for m in range(4 * q, 4 * q + 4):
                    mm = pe.matmul(self.bank[3 + n % 3][:, (m % 4) * P:(m % 4 + 1) * P], self.qT[:, m, t * P:(t + 1) * P], self.keysT[:, m % 2, :])
                mm.then_inc(*self.s_psum.by())
                n += 1

    def copies(self, act):
        act.wait_ge(*self.keys_psum.at(1))
        act.copy(self.keysT[:].rearrange("p c k -> p (c k)"), self.bank[5][:, 0:2 * P]).then_inc(*self.keys_done.by())
        for m in range(self.HC):
            act.wait_ge(*self.q_psum.at(m + 1))
            act.copy(self.qT[:, m, :], self.bank[m % 3][:, 0:self.width]).then_inc(*self.q_done.by())
        for n in range(len(self.tiles) * self.HC // 4):
            act.wait_ge(*self.s_psum.at(n + 1))
            act.copy(self.scores[:, self.tiles[n // 4], 4 * (n % 4):4 * (n % 4) + 4, :].rearrange("p m k -> p (m k)"), self.bank[3 + n % 3][:]).then_inc(*self.s_done.by())


def first_scores(core, io, xT, scores, layer):
    with ExitStack() as ctx:
        part = KeyScores(core, io, ctx, xT, scores, layer, (0,), 4)
        with core.nc.Block() as block:
            @block.sync
            def _(sp):
                part.loads(sp)

            @block.tensor
            def _(pe):
                part.products(pe)

            @block.scalar
            def _(act):
                part.copies(act)
        core.end_stage()


def top16(dve, own, passed, values, places, source):
    dve.sem_inc(*passed.by())
    for n in range(len(source)):
        ins = dve.max(values[n][:, 0:8], source[n])
    own(ins)
    dve.sem_inc(*passed.by())
    for n in range(len(source)):
        dve.max_index(places[n][:, 0:8], values[n][:, 0:8], source[n])
    for n in range(len(source)):
        ins = dve.match_replace(source[n], values[n][:, 0:8], source[n], -3.0e38)
    own(ins)
    dve.sem_inc(*passed.by())
    for n in range(len(source)):
        ins = dve.max(values[n][:, 8:16], source[n])
    own(ins)
    dve.sem_inc(*passed.by())
    for n in range(len(source)):
        ins = dve.max_index(places[n][:, 8:16], values[n][:, 8:16], source[n])
    own(ins)


def peer_experts(core, io, xT, scores, layer):
    nc = core.nc
    RING = 8
    TURN = 2 * RING
    TURNS = SLOTS // TURN
    HC = 2 * PH
    TOPK_STEPS = 25
    WHOLE, SHARE = 3, 4
    PE_TILE = WHOLE * TURN + (TURNS - WHOLE) * (TURN - SHARE)
    DVE_TILE = (TURNS - WHOLE) * SHARE

    def by_dve(kind, j):
        return kind == "shared" and j % 4 == 3

    def pe_upto(t, s, kind, j):
        if kind == "whole":
            return t * PE_TILE + s * TURN + j + 1
        return t * PE_TILE + s * (TURN - SHARE) + WHOLE * SHARE + j + 1 - (j + 1) // 4

    def dve_upto(t, s, kind, j):
        return t * DVE_TILE + s * SHARE - WHOLE * SHARE + (j + 1) // 4

    u_rows, v_rows = (io[n].rearrange("l e d -> (l e) d") for n in ("peer_u", "peer_v"))
    with ExitStack() as ctx:
        def sb(name, shape, dt=F32):
            return ctx.enter_context(nc.sbuf_tensor(f"{name}_{layer}", shape, dt))

        u_ring, v_ring = sb("u_ring", [P, RING, D]), sb("v_ring", [P, RING, D])
        u_at, v_at = sb("u_at", [P, TURN], U32), sb("v_at", [P, TURN], U32)
        expert = sb("expert", [P, TILES * SLOTS], U32)
        gate, act_in, mix = sb("gate", [P, SLOTS]), sb("act_in", [P, SLOTS]), sb("mix", [P, TILES * SLOTS])
        work = sb("work", [P, HC, PK])
        row = sb("row", [P, D])
        best, best_at = sb("best", [P, HC, PTOP]), sb("best_at", [P, HC, PTOP], U32)
        best_at_f = sb("best_at_f", [P, HC, PTOP])
        cand = sb("cand", [P, PH, PTOP * PTOP])
        top, top_at = sb("top", [P, PH, PTOP]), sb("top_at", [P, PH, PTOP], U32)
        digit, digit_f = sb("digit", [P, 2, SLOTS], U32), sb("digit_f", [P, 2, SLOTS])
        hot = cand[:].rearrange("p h (k j) -> p (h k) j", j=PTOP)
        found = sb("found", [P, 2, SLOTS])
        norm = sb("norm", [P, PH])
        dots = sb("dots", [P, TURN])
        dve_mix, dve_acc = sb("dve_mix", [P, TURN]), sb("dve_acc", [P, D])
        mix_now = sb("mix_now", [P, TURN])
        DIAGS = 4
        diag = sb("diag", [P, DIAGS, P])
        zero = sb("zero", [P, P])
        ffn = scores[:].rearrange("p t m k -> p t (m k)")[:, :, 0:D]
        ffn_dve = scores[:].rearrange("p t m k -> p t (m k)")[:, :, D:]
        ln_g, ln_b = sb("ln_g", [P, D]), sb("ln_b", [P, D])
        stats, mv, rstd = sb("pstats", [P, 2, 6]), sb("pmv", [P, 2]), sb("prstd", [P, 1])
        acc = ctx.enter_context(nc.psum_tensor(f"pacc_{layer}", [P, 2, HALF], F32))

        u_in = [core.sig(f"u_in{i}") for i in range(RING)]
        v_in = [core.sig(f"v_in{i}") for i in range(RING)]
        u_used, v_used, at_copied = core.sig("u_used"), core.sig("v_used"), core.sig("at_copied")
        chosen, gate_arg, gate_exp = core.sig("chosen"), core.sig("gate_arg"), core.sig("gate_exp")
        dots_all, gelu_done, mix_done = core.sig("dots_all"), core.sig("gelu_done"), core.sig("mix_done")
        mix_now_done, diag_done = core.sig("mix_now_done"), core.sig("diag_ready")
        zeroed, ffn_psum, ffn_done, ln_in = core.sig("zeroed"), core.sig("ffn_psum"), core.sig("ffn_done"), core.sig("vectors_in")
        dve_steps, pool_turns, passed = core.sig("dve_steps"), core.sig("pool_turns"), core.sig("dve_passed")
        dots_done, act_turns = core.sig("dots_done"), core.sig("act_turns")
        v_used_dve, dve_mix_done = core.sig("v_used_dve"), core.sig("dve_mix_done")
        core.sig("ln_var"), core.sig("ln_rstd")
        others = KeyScores(core, io, ctx, xT, scores, layer, (1, 2), 2)
        scored = others.s_done

        with nc.Block() as block:
            @block.sync
            def _(sp):
                others.loads(sp)
                sp.dma_start(ln_g[:], io["ln_ffn_g"][layer:layer + 1, :].broadcast_to([P, D])).then_inc(*ln_in.by(16))
                sp.dma_start(ln_b[:], io["ln_ffn_b"][layer:layer + 1, :].broadcast_to([P, D])).then_inc(*ln_in.by(16))

            @block.gpsimd
            def _(pool):
                def first_rows(t):
                    with pool.Fori(0, TURNS) as s, turns(s, TURNS, counted=(at_copied, pool_turns, *u_in)):
                        for half in range(2):
                            at = u_at[:, half * RING:(half + 1) * RING]
                            first = t * SLOTS + s * TURN + half * RING
                            pool.wait_ge(*u_used.at(first + 1))
                            pool.sem_inc(*pool_turns.by())
                            pool.tensor_copy(at, expert[:, bass.ds(first, RING)]).then_inc(*at_copied.by())
                            for j in range(RING):
                                pool.wait_ge(*u_used.at(first + j + 1))
                                if j == 0:
                                    pool.wait_ge(*at_copied.at(t * 4 * TURNS + s * 2 + half + 1))
                                pool.sem_inc(*pool_turns.by())
                                pool.indirect_dma_start(u_ring[:, j, :], None, u_rows,
                                                        bass.IndirectOffsetOnAxis(ap=at[:, j:j + 1], axis=0)).then_inc(*u_in[j].by(16))

                def second_rows(t, s, kind, before):
                    def used(j):
                        tt, ss, k, jj = (t, s, kind, j) if j >= 0 else (t, s - 1, before, j + TURN)
                        if j < 0 and isinstance(s, int) and s == 0:
                            tt, ss = t - 1, TURNS - 1
                        if by_dve(k, jj):
                            pool.wait_ge(*v_used_dve.at(dve_upto(tt, ss, k, jj) + RING))
                        else:
                            pool.wait_ge(*v_used.at(pe_upto(tt, ss, k, jj) + RING))

                    for half in range(2):
                        at = v_at[:, half * RING:(half + 1) * RING]
                        first = t * SLOTS + s * TURN + half * RING
                        used(half * RING - RING)
                        if half == 0 and before == "shared":
                            used(-RING - 1)
                        pool.sem_inc(*pool_turns.by())
                        pool.tensor_copy(at, expert[:, bass.ds(first, RING)]).then_inc(*at_copied.by())
                        for j in range(RING):
                            used((half - 1) * RING + j)
                            if j == 0:
                                pool.wait_ge(*at_copied.at(t * 4 * TURNS + 2 * TURNS + s * 2 + half + 1))
                            pool.sem_inc(*pool_turns.by())
                            pool.indirect_dma_start(v_ring[:, j, :], None, v_rows,
                                                    bass.IndirectOffsetOnAxis(ap=at[:, j:j + 1], axis=0)).then_inc(*v_in[j].by(16))

                with pool.Fori(0, TILES) as t, turns(t, TILES, counted=(at_copied, pool_turns, *u_in, *v_in)):
                    pool.wait_ge(*chosen.at(t + 1))
                    pool.sem_inc(*pool_turns.by())
                    first_rows(t)
                    again = (at_copied, pool_turns, *v_in)
                    second_rows(t, 0, "whole", "shared")
                    with pool.Fori(0, WHOLE - 1) as s, turns(s, WHOLE - 1, counted=again):
                        second_rows(t, s + 1, "whole", "whole")
                    second_rows(t, WHOLE, "shared", "whole")
                    with pool.Fori(0, TURNS - WHOLE - 1) as s, turns(s, TURNS - WHOLE - 1, counted=again):
                        second_rows(t, s + WHOLE + 1, "shared", "shared")

            @block.vector
            def _(dve):
                own = in_order(dve, dve_steps)
                x = core.x_tok
                dve.memset(zero[:], 0.0).then_inc(*zeroed.by())
                dve.sem_inc(*u_used.by(RING))
                heads4 = [P, PH, PTOP, PTOP]
                gate_h = gate[:].rearrange("p (h k) -> p h k", k=PTOP)

                def choose(t):
                    dve.tensor_copy(work[:].rearrange("p m k -> p (m k)"), scores[:, bass.ds(t, 1)].rearrange("p o m k -> p (o m k)"))
                    own(dve.tensor_copy(row[:], x[:, bass.ds(t, 1)].rearrange("p o d -> p (o d)")))
                    top16(dve, own, passed, [best[:, m, :] for m in range(HC)], [best_at[:, m, :] for m in range(HC)], [work[:, m, :] for m in range(HC)])
                    two = best[:].rearrange("p (h c) k -> p h c k", c=2)
                    dve.tensor_copy(best_at_f[:], best_at[:])
                    own(dve.tensor_tensor(cand[:].rearrange("p h (i j) -> p h i j", j=PTOP), two[:, :, 0, :].unsqueeze(3).broadcast_to(heads4),
                                          two[:, :, 1, :].unsqueeze(2).broadcast_to(heads4), ALU.add))
                    top16(dve, own, passed, [top[:, h, :] for h in range(PH)], [top_at[:, h, :] for h in range(PH)], [cand[:, h, :] for h in range(PH)])
                    own(dve.tensor_tensor(gate_h, top[:], top[:, :, 0:1].broadcast_to([P, PH, PTOP]), ALU.subtract))
                    dve.sem_inc(*gate_arg.by())
                    flat = top_at[:].rearrange("p h k -> p (h k)")
                    dve.tensor_scalar(digit[:, 0, :], flat, 4, None, ALU.logical_shift_right)
                    own(dve.tensor_scalar(digit[:, 1, :], flat, 15, None, ALU.bitwise_and))
                    own(dve.tensor_copy(digit_f[:], digit[:]))
                    two_at = best_at_f[:].rearrange("p (h c) k -> p h c k", c=2)
                    hot4 = hot.rearrange("p (h k) j -> p h k j", k=PTOP)
                    for c in range(2):
                        own(dve.tensor_tensor(hot, core.const("iota").unsqueeze(1).broadcast_to([P, SLOTS, PTOP]),
                                              digit_f[:, c, :].unsqueeze(2).broadcast_to([P, SLOTS, PTOP]), ALU.is_equal))
                        own(dve.tensor_tensor(hot4, hot4, two_at[:, :, c, :].unsqueeze(2).broadcast_to(heads4), ALU.mult))
                        own(dve.tensor_reduce(found[:, c, :], hot, AX.X, ALU.add))
                    own(dve.tensor_scalar(found[:, 0, :], found[:, 0, :], float(PK), float(layer * EXPERTS), ALU.mult, ALU.add))
                    own(dve.tensor_tensor(expert[:, bass.ds(t * SLOTS, SLOTS)], found[:, 0, :], found[:, 1, :], ALU.add))
                    dve.sem_inc(*chosen.by())

                def dot_products(t):
                    with dve.Fori(0, TURNS) as s, turns(s, TURNS, counted=(u_used, dots_done)):
                        for j in range(TURN):
                            dve.wait_ge(*u_in[j % RING].at(16 * (t * 2 * TURNS + s * 2 + j // RING + 1)))
                            dve.tensor_tensor_reduce(u_ring[:, j % RING, :], u_ring[:, j % RING, :], row[:], 1.0, 0.0,
                                                     ALU.mult, ALU.add, dots[:, j:j + 1]).then_inc(*u_used.by())
                        dve.wait_ge(*u_used.at(t * SLOTS + s * TURN + TURN + RING))
                        dve.tensor_copy(act_in[:, bass.ds(s * TURN, TURN)], dots[:]).then_inc(*dots_done.by())
                        dve.wait_ge(*dots_done.at(t * TURNS + s + 1))
                    dve.wait_ge(*scored.at(2 * HC // 4))
                    dve.sem_inc(*dots_all.by())
                    dve.wait_ge(*gate_exp.at(t + 1))
                    own(dve.tensor_reduce(norm[:], gate_h, AX.X, ALU.add))
                    own(dve.reciprocal(norm[:], norm[:]))
                    own(dve.tensor_tensor(gate_h, gate_h, norm[:].unsqueeze(2).broadcast_to([P, PH, PTOP]), ALU.mult))
                    dve.wait_ge(*gelu_done.at(t + 1))
                    own(dve.tensor_tensor(mix[:, bass.ds(t * SLOTS, SLOTS)], gate[:], act_in[:], ALU.mult))
                    dve.sem_inc(*mix_done.by())
                def mix_share(t):
                    own(dve.memset(dve_acc[:], 0.0))
                    dve.sem_inc(*passed.by())
                    with dve.Fori(0, TURNS - WHOLE) as i, turns(i, TURNS - WHOLE, counted=(v_used_dve, dve_mix_done, passed)):
                        s = i + WHOLE
                        dve.tensor_copy(dve_mix[:], mix[:, bass.ds(t * SLOTS + s * TURN, TURN)]).then_inc(*dve_mix_done.by())
                        dve.wait_ge(*dve_mix_done.at(t * (TURNS - WHOLE) + i + 1))
                        for j in range(3, TURN, 4):
                            dve.wait_ge(*v_in[j % RING].at(16 * (t * 2 * TURNS + s * 2 + j // RING + 1)))
                            dve.wait_ge(*v_used_dve.at(dve_upto(t, s, "shared", j) - 1 + RING))
                            dve.sem_inc(*passed.by())
                            dve.scalar_tensor_tensor(dve_acc[:], v_ring[:, j % RING, :], dve_mix[:, j:j + 1], dve_acc[:], ALU.mult, ALU.add).then_inc(*v_used_dve.by())
                        dve.wait_ge(*v_used_dve.at(dve_upto(t, s, "shared", TURN - 1) + RING))
                        dve.sem_inc(*passed.by())
                    own(dve.tensor_copy(ffn_dve[:, bass.ds(t, 1)].rearrange("p o d -> p (o d)"), dve_acc[:]))
                    dve.sem_inc(*passed.by())

                dve.sem_inc(*v_used_dve.by(RING))
                choose(0)
                dot_products(0)
                with dve.Fori(0, TILES - 1) as i, turns(i, TILES - 1, own=dve_steps, per=TOPK_STEPS + 2,
                                                        counted=(chosen, gate_arg, dots_all, mix_done, u_used, dots_done, passed, v_used_dve, dve_mix_done)):
                    choose(i + 1)
                    mix_share(i)
                    dot_products(i + 1)

                def norm_rows(t):
                    dve.wait_ge(*ffn_done.at(t + 2))
                    own(dve.scalar_tensor_tensor(ffn[:, t, :], x[:, t, :], ALPHA, ffn[:, t, :], ALU.mult, ALU.add))
                    own(dve.tensor_tensor(ffn[:, t, :], ffn[:, t, :], ffn_dve[:, t, :], ALU.add))
                    layer_norm_steps(core, dve, own, ffn[:, t, :], x[:, t, :], ln_g[:], ln_b[:], stats, mv, rstd, t + 1)

                dve.wait_ge(*ln_in.at(32))
                for t in range(TILES - 1):
                    norm_rows(t)
                mix_share(TILES - 1)
                norm_rows(TILES - 1)

            @block.scalar
            def _(act):
                others.copies(act)
                act.sem_inc(*ffn_done.by())

                def weights(t):
                    act.wait_ge(*gate_arg.at(t + 1))
                    act.activation(gate[:], gate[:], ACT.Exp).then_inc(*gate_exp.by())
                    act.wait_ge(*dots_all.at(t + 1))
                    act.activation(act_in[:], act_in[:], ACT.Gelu).then_inc(*gelu_done.by())
                    act.wait_ge(*mix_done.at(t + 1))
                    act.sem_inc(*act_turns.by())

                def diagonals(t, s, kind):
                    act.copy(mix_now[:], mix[:, bass.ds(t * SLOTS + s * TURN, TURN)]).then_inc(*mix_now_done.by())
                    mine = [j for j in range(TURN) if not by_dve(kind, j)]
                    for n, j in enumerate(mine):
                        if j == 0:
                            act.wait_ge(*mix_now_done.at(t * TURNS + s + 1))
                        act.wait_ge(*v_used.at(pe_upto(t, s, kind, j) + RING - DIAGS))
                        act.activation(diag[:, n % DIAGS, :], core.const("ident"), ACT.Copy, scale=mix_now[:, j:j + 1]).then_inc(*diag_done.by())
                    act.wait_ge(*diag_done.at(pe_upto(t, s, kind, mine[-1])))
                    act.sem_inc(*act_turns.by())

                def shared_turns(t):
                    with act.Fori(0, TURNS - WHOLE) as i, turns(i, TURNS - WHOLE, counted=(mix_now_done, diag_done, act_turns)):
                        diagonals(t, i + WHOLE, "shared")
                    act.wait_ge(*ffn_psum.at(t + 1))
                    act.sem_inc(*act_turns.by())
                    act.copy(ffn[:, bass.ds(t, 1)].rearrange("p o d -> p (o d)"), acc[:].rearrange("p a d -> p (a d)")).then_inc(*ffn_done.by())

                with act.Fori(0, TILES - 1) as t, turns(t, TILES - 1, counted=(gate_exp, gelu_done, mix_now_done, diag_done, act_turns, ffn_done)):
                    weights(t)
                    with act.Fori(0, WHOLE) as s, turns(s, WHOLE, counted=(mix_now_done, diag_done, act_turns)):
                        diagonals(t, s, "whole")
                    shared_turns(t)
                weights(TILES - 1)
                assert WHOLE >= TILES - 1
                for s in range(WHOLE):
                    diagonals(TILES - 1, s, "whole")
                    if s < TILES - 1:
                        layer_norm_roots(core, act, mv, rstd, (s,))
                shared_turns(TILES - 1)
                layer_norm_roots(core, act, mv, rstd, (TILES - 1,))

            @block.tensor
            def _(pe):
                others.products(pe)
                finite = core.constants[:, 0:HALF]
                pe.wait_ge(*zeroed.at(1))
                pe.sem_inc(*v_used.by(RING))
                with pe.Fori(0, TILES) as t, turns(t, TILES, counted=(v_used, ffn_psum)):
                    pe.wait_ge(*mix_done.at(t + 1))
                    pe.wait_ge(*ffn_done.at(t + 1))
                    for half in range(2):
                        pe.matmul(acc[:, half, :], zero[:], finite, start=True, stop=False)
                    for start, count, kind in ((0, WHOLE, "whole"), (WHOLE, TURNS - WHOLE, "shared")):
                        with pe.Fori(0, count) as i, turns(i, count, counted=(v_used,)):
                            s = i + start
                            for n, j in enumerate(j for j in range(TURN) if not by_dve(kind, j)):
                                pe.wait_ge(*v_in[j % RING].at(16 * (t * 2 * TURNS + s * 2 + j // RING + 1)))
                                pe.wait_ge(*diag_done.at(pe_upto(t, s, kind, j)))
                                pe.matmul(acc[:, 0, :], diag[:, n % DIAGS, :], v_ring[:, j % RING, 0:HALF], start=False, stop=False)
                                pe.matmul(acc[:, 1, :], diag[:, n % DIAGS, :], v_ring[:, j % RING, HALF:], start=False, stop=False).then_inc(*v_used.by())
                    for half in range(2):
                        mm = pe.matmul(acc[:, half, :], zero[:], finite, start=False, stop=True)
                    mm.then_inc(*ffn_psum.by())
        core.end_stage()


def attention_projections(core, io, xT, out):
    nc = core.nc
    weights = [("k", io["w_kv"][:, 0:D]), ("v", io["w_kv"][:, D:]), ("q", io["diff_w_q"][0])]
    with ExitStack() as ctx:
        RING = 12
        ring = ctx.enter_context(nc.sbuf_tensor("aw_ring", [P, RING, D], F32))
        rot = ctx.enter_context(nc.sbuf_tensor("rot", [P, 4, TILES, 2 * DH, ROT // 2], F32))
        acc = ctx.enter_context(nc.psum_tensor("aacc", [P, 6, HALF], F32))
        aw_in = [core.sig(f"loaded{i}") for i in range(RING)]
        aw_used, a_full, a_free = core.sig("w_used"), core.sig("acc_full"), core.sig("acc_free_act")
        rotated, kv_out, dve_steps = core.sig("rotated"), core.sig("kv_out"), core.sig("dve_steps")

        with nc.Block() as block:
            @block.sync
            def _(sp):
                for n in range(3 * KD):
                    if n >= RING:
                        sp.wait_ge(*aw_used.at(n - RING + 1))
                    sp.dma_start(ring[:, n % RING, :], weights[n // KD][1][n % KD * P:(n % KD + 1) * P, :]).then_inc(*aw_in[n % RING].by(16))

            @block.gpsimd
            def _(pool):
                pool.wait_ge(*a_free.at(12))
                for n, wait in (("v", None), ("k", rotated)):
                    if wait:
                        pool.wait_ge(*wait.at(1))
                    tail = "h c d -> (b s) (h c d)" if n == "k" else "h e -> (b s) (h e)"
                    rows_p, rows_s = (io[f"cache_{n}_{w}"].rearrange("b s " + tail) for w in "ps")
                    pool.dma_start(rows_p.rearrange("(t p) e -> p t e", p=P), out[n][:, 0:2, :]).then_inc(*kv_out.by(16))
                    pool.dma_start(rows_s, out[n][:, 2, :]).then_inc(*kv_out.by(16))
                pool.wait_ge(*kv_out.at(64))

            @block.tensor
            def _(pe):
                for i in range(3):
                    for k in range(KD):
                        n = i * KD + k
                        pe.wait_ge(*aw_in[n % RING].at(16 * (n // RING + 1)))
                        for b in range(6):
                            if k == 0 and i > 0:
                                pe.wait_ge(*a_free.at(6 * (i - 1) + b + 1))
                            t, h = divmod(b, 2)
                            mm = pe.matmul(acc[:, b, :], xT[:, k, t * P:(t + 1) * P], ring[:, n % RING, h * HALF:(h + 1) * HALF],
                                           start=(k == 0), stop=(k == KD - 1))
                            if k == KD - 1:
                                mm.then_inc(*a_full.by())
                        if k < KD - 1:
                            mm.then_inc(*aw_used.by())
                        else:
                            pe.wait_ge(*a_full.at(6 * (i + 1)))
                            pe.sem_inc(*aw_used.by())

            @block.scalar
            def _(act):
                for i, (n, _) in enumerate(weights):
                    for b in range(6):
                        act.wait_ge(*a_full.at(6 * i + b + 1))
                        act.copy(out[n][:, b // 2, (b % 2) * HALF:(b % 2 + 1) * HALF], acc[:, b, :]).then_inc(*a_free.by())

            @block.vector
            def _(dve):
                own = in_order(dve, dve_steps)
                angle = [core.const(n).rearrange("p (t r) -> p t r", t=TILES).unsqueeze(2).broadcast_to([P, TILES, 2 * DH, ROT // 2]) for n in ("cos", "sin")]
                for i, n in ((0, "k"), (2, "q")):
                    dve.wait_ge(*a_free.at(6 * (i + 1)))
                    x = out[n][:].rearrange("p t (g d) -> p t g d", d=DD)
                    x1, x2 = x[:, :, :, 0:ROT // 2], x[:, :, :, ROT // 2:ROT]
                    for j, (src, f) in enumerate(((x1, 0), (x2, 1), (x1, 1), (x2, 0))):
                        ins = dve.tensor_tensor(rot[:, j], src, angle[f], ALU.mult)
                    own(ins)
                    dve.tensor_tensor(x1, rot[:, 0], rot[:, 1], ALU.subtract)
                    own(dve.tensor_tensor(x2, rot[:, 2], rot[:, 3], ALU.add))
                    dve.sem_inc(*rotated.by())
        core.end_stage()


def mixing_weight(core, io, neg_lam):
    nc = core.nc
    with ExitStack() as ctx:
        lp = ctx.enter_context(nc.sbuf_tensor("lam_rows", [P, 2, 2, DD], F32))
        prod = ctx.enter_context(nc.sbuf_tensor("lam_prod", [P, 2, DD], F32))
        dot = ctx.enter_context(nc.sbuf_tensor("lam_dot", [P, 2], F32))
        lam_in, lam_dot, lam_exp, dve_steps = core.sig("vectors_in"), core.sig("lam_dot"), core.sig("lam_exp"), core.sig("dve_steps")
        with nc.Block() as block:
            @block.sync
            def _(sp):
                sp.dma_start(lp[:].rearrange("p a b d -> p (a b d)"), io["diff_lambda"].rearrange("a i d -> a (i d)").broadcast_to([P, 4 * DD])).then_inc(*lam_in.by(16))

            @block.scalar
            def _(act):
                act.wait_ge(*lam_dot.at(1))
                act.activation(dot[:], dot[:], ACT.Exp).then_inc(*lam_exp.by())

            @block.vector
            def _(dve):
                own = in_order(dve, dve_steps)
                dve.wait_ge(*lam_in.at(16))
                own(dve.tensor_tensor(prod[:], lp[:, :, 0, :], lp[:, :, 1, :], ALU.mult))
                own(dve.tensor_reduce(dot[:], prod[:], AX.X, ALU.add))
                dve.sem_inc(*lam_dot.by())
                dve.wait_ge(*lam_exp.at(1))
                own(dve.tensor_tensor(neg_lam[:], dot[:, 1:2], dot[:, 0:1], ALU.subtract))
                own(dve.tensor_scalar(neg_lam[:], neg_lam[:], -LAM_INIT, None, ALU.add))
        core.end_stage()


class Cache:

    def __init__(self, core, io, ctx):
        self.io = io
        self.keys, self.values = (ctx.enter_context(core.nc.sbuf_tensor(f"cache_{n}", [P, places, PAST // P, D], F32)) for n, places in (("k", 2), ("v", 3)))
        self.keys_in, self.values_in = [core.sig(f"loaded{i}") for i in range(2)], [core.sig(f"loaded{2 + i}") for i in range(3)]

    def load_keys(self, sp, b):
        sp.dma_start(self.keys[:, b % 2], self.io["cache_k"][b].rearrange("(j p) h c d -> p j (h c d)", p=P)).then_inc(*self.keys_in[b % 2].by(16))

    def load_values(self, sp, b):
        sp.dma_start(self.values[:, b % 3], self.io["cache_v"][b].rearrange("(j p) h e -> p j (h e)", p=P)).then_inc(*self.values_in[b % 3].by(16))


def prompt_attention(core, cache, qT, kT, v_tok, oT, neg_lam):
    nc = core.nc
    SCALE = DD ** -0.5
    parts = (slice(0, P), slice(P, 3 * P))
    with ExitStack() as ctx:
        def sb(name, shape, dt=F32):
            return ctx.enter_context(nc.sbuf_tensor("pa_" + name, shape, dt))

        s, p = sb("s", [P, 2, 2, TOK]), sb("p", [P, 2, 2, TOK])
        top, low, tot = sb("top", [P, 2, 4]), sb("low", [P, 2, 4]), sb("tot", [P, 2, 4])
        attn, attnT = sb("attn", [P, 2, TOK]), sb("attnT", [P, 2, TOK])
        s_bank = [ctx.enter_context(nc.psum_tensor(f"pa_s{i}", [P, TOK], F32)) for i in range(4)]
        t_bank = [ctx.enter_context(nc.psum_tensor(f"pa_t{i}", [P, TOK], F32)) for i in range(2)]
        o_bank = [ctx.enter_context(nc.psum_tensor(f"pa_o{i}", [P, SEQ], F32)) for i in range(2)]
        sc, sm, top_done, p_done = core.sig("scores_psum"), core.sig("scores_masked"), core.sig("maxima"), core.sig("probs")
        attn_done, at_psum, at_done = core.sig("maps_mixed"), core.sig("mixedT_psum"), core.sig("mixedT")
        o_psum, o_done, dve_steps = core.sig("heads_psum"), core.sig("heads_out"), core.sig("dve_steps")
        with nc.Block() as block:
            @block.sync
            def _(sp):
                for b in range(3):
                    if b < 2:
                        cache.load_keys(sp, b)
                    cache.load_values(sp, b)

            @block.tensor
            def _(pe):
                def scores(h):
                    if h >= 2:
                        pe.wait_ge(*sm.at(2 * (h - 1)))
                    for c in range(2):
                        rows = slice(c * DD, (c + 1) * DD)
                        bank = s_bank[2 * (h % 2) + c]
                        pe.matmul(bank[:, parts[0]], qT[rows, h, 0:P], kT[rows, h, 0:P])
                        pe.matmul(bank[:, parts[1]], qT[rows, h, P:2 * P], kT[rows, h, 0:2 * P]).then_inc(*sc.by())

                scores(0)
                for h in range(DH):
                    if h + 1 < DH:
                        scores(h + 1)
                    pe.wait_ge(*attn_done.at(h + 1))
                    if h >= 2:
                        pe.wait_ge(*at_done.at(h - 1))
                    for i in range(3):
                        mm = pe.transpose(t_bank[h % 2][:, i * P:(i + 1) * P], attn[:, h % 2, i * P:(i + 1) * P], core.const("ident"))
                    mm.then_inc(*at_psum.by())
                    pe.wait_ge(*at_done.at(h + 1))
                    if h >= 2:
                        pe.wait_ge(*o_done.at(h - 1))
                    e = slice(h * P, (h + 1) * P)
                    pe.matmul(o_bank[h % 2][:, 0:P], v_tok[:, 0, e], attnT[:, h % 2, 0:P])
                    pe.matmul(o_bank[h % 2][:, P:], v_tok[:, 0, e], attnT[:, h % 2, P:2 * P], start=True, stop=False)
                    pe.matmul(o_bank[h % 2][:, P:], v_tok[:, 1, e], attnT[:, h % 2, 2 * P:], start=False, stop=True).then_inc(*o_psum.by())

            @block.scalar
            def _(act):
                def flush(h):
                    act.wait_ge(*at_psum.at(h + 1))
                    act.copy(attnT[:, h % 2, :], t_bank[h % 2][:]).then_inc(*at_done.by())
                    act.wait_ge(*o_psum.at(h + 1))
                    act.copy(oT[:, h, 0:SEQ], o_bank[h % 2][:]).then_inc(*o_done.by())

                for h in range(DH):
                    act.wait_ge(*top_done.at(h + 1))
                    if h >= 2:
                        act.wait_ge(*attn_done.at(h - 1))
                    for c in range(2):
                        for i in range(2):
                            j = 2 * c + i
                            act.activation(p[:, h % 2, c, parts[i]], s[:, h % 2, c, parts[i]], ACT.Exp, bias=low[:, h % 2, j:j + 1],
                                           scale=SCALE, accum_out=tot[:, h % 2, j:j + 1]).then_inc(*p_done.by())
                    if h >= 1:
                        flush(h - 1)
                flush(DH - 1)

            @block.vector
            def _(dve):
                own = in_order(dve, dve_steps)

                def combine(h):
                    dve.wait_ge(*p_done.at(4 * (h + 1)))
                    own(dve.reciprocal(tot[:, h % 2, :], tot[:, h % 2, :]))
                    own(dve.tensor_scalar(tot[:, h % 2, 2:4], tot[:, h % 2, 2:4], neg_lam[:, 0:1], None, ALU.mult))
                    if h >= 2:
                        dve.wait_ge(*at_psum.at(h - 1))
                    for i in range(2):
                        dve.tensor_scalar(attn[:, h % 2, parts[i]], p[:, h % 2, 1, parts[i]], tot[:, h % 2, 2 + i:3 + i], None, ALU.mult)
                    own(dve.tensor_copy(top[:, h % 2, 0:1], top[:, h % 2, 0:1]))
                    for i in range(2):
                        ins = dve.scalar_tensor_tensor(attn[:, h % 2, parts[i]], p[:, h % 2, 0, parts[i]], tot[:, h % 2, i:i + 1],
                                                       attn[:, h % 2, parts[i]], ALU.mult, ALU.add)
                    own(ins)
                    dve.sem_inc(*attn_done.by())

                for h in range(DH):
                    if h >= 2:
                        dve.wait_ge(*p_done.at(4 * (h - 1)))
                    for c in range(2):
                        dve.wait_ge(*sc.at(2 * h + c + 1))
                        dve.tensor_tensor(s[:, h % 2, c, :], s_bank[2 * (h % 2) + c][:], core.const("causal"), ALU.add).then_inc(*sm.by())
                    dve.wait_ge(*sm.at(2 * h + 2))
                    for c in range(2):
                        for i in range(2):
                            ins = dve.tensor_reduce(top[:, h % 2, 2 * c + i:2 * c + i + 1], s[:, h % 2, c, parts[i]], AX.X, ALU.max)
                    own(ins)
                    own(dve.tensor_scalar(low[:, h % 2, :], top[:, h % 2, :], -SCALE, None, ALU.mult))
                    dve.sem_inc(*top_done.by())
                    if h >= 1:
                        combine(h - 1)
                combine(DH - 1)
        core.end_stage()


def sample_attention(core, cache, qT, kT, v_tok, oT, neg_lam):
    nc = core.nc
    SCALE = DD ** -0.5
    KT = PAST // P
    GROUPS, PER = 2, 4
    HR = 2 * DEC_SEQ
    assert PER * HR == P
    ident = core.const("ident")
    with ExitStack() as ctx:
        def sb(name, shape, dt=F32):
            return ctx.enter_context(nc.sbuf_tensor("sa_" + name, shape, dt))

        kc, vc, kc_in, vc_in = cache.keys, cache.values, cache.keys_in, cache.values_in
        kcT = sb("kcT", [P, DH, PAST])
        q_maps = sb("q_maps", [P, DEC_BATCH, DH, HR])
        p = sb("p", [P, GROUPS, PAST])
        p_new = sb("p_new", [P, GROUPS, DEC_BATCH, P])
        pT = sb("pT", [P, GROUPS, KT + 1, P])
        top, low, tot = sb("top", [P, 2, GROUPS]), sb("low", [P, GROUPS]), sb("tot", [P, 2, GROUPS])
        row_w, map_w = sb("row_w", [P, GROUPS]), sb("map_w", [P, 1])
        o_rows = sb("o_rows", [P, GROUPS, P])
        bank = [ctx.enter_context(nc.psum_tensor(f"sa_b{i}", [P, HALF], F32)) for i in range(8)]
        s_bank, new_bank, pT_bank, pT_new_bank, o_bank, oT_bank = bank[2:4], bank[4], bank[5:7], bank[7], bank[5], bank[6]
        zeros, q_done = core.sig("zeros"), core.sig("q_maps")
        kt_psum, kt_act, kt_dve = core.sig("keysT_psum"), core.sig("copied_act"), core.sig("copied_dve")
        sc, low_done, p_done = core.sig("scores_psum"), core.sig("maxima"), core.sig("probs")
        pT_psum, pT_act, pT_dve = core.sig("probsT_psum"), core.sig("probsT_act"), core.sig("probsT_dve")
        o_psum, o_scaled, oT_psum, o_done = (core.sig(n) for n in ("rows_psum", "rows_copied", "heads_psum", "heads_out"))
        dve_steps = core.sig("dve_steps")

        with nc.Block() as block:
            @block.sync
            def _(sp):
                for b in range(2, DEC_BATCH):
                    sp.wait_ge(*kt_psum.at(DH * (b - 1)))
                    cache.load_keys(sp, b)
                    if b >= 3:
                        sp.wait_ge(*o_psum.at(b - 2))
                        cache.load_values(sp, b)

            @block.gpsimd
            def _(pool):
                pool.memset(q_maps[:], 0.0).then_inc(*zeros.by())
                pool.memset(p_new[:], 0.0).then_inc(*zeros.by())

            @block.tensor
            def _(pe):
                def key_transposes(b):
                    pe.wait_ge(*kc_in[b % 2].at(16 * (b // 2)))
                    for h in range(DH):
                        n = b * DH + h
                        if n >= 2:
                            pe.wait_ge(*(kt_act if n % 2 == 0 else kt_dve).at(n // 2))
                        for j in range(KT):
                            mm = pe.transpose(bank[n % 2][:, j * P:(j + 1) * P], kc[:, b % 2, j, h * P:(h + 1) * P], ident)
                        mm.then_inc(*kt_psum.by())

                def scores(b, between):
                    pe.wait_ge(*kt_act.at(DH * (b + 1) // 2))
                    pe.wait_ge(*kt_dve.at(DH * (b + 1) // 2))
                    if b > 0:
                        pe.wait_ge(*p_done.at(4 * b))
                    for h in range(DH):
                        g, rows = h // PER, slice(h % PER * HR, (h % PER + 1) * HR)
                        mm = pe.matmul(new_bank[rows, g * DEC_SEQ:(g + 1) * DEC_SEQ], q_maps[:, b, h, :], kT[:, h, SEQ + b * DEC_SEQ:SEQ + (b + 1) * DEC_SEQ],
                                       tile_position=(0, h % PER * HR))
                    mm.then_inc(*sc.by())
                    for h in range(DH):
                        g, rows = h // PER, slice(h % PER * HR, (h % PER + 1) * HR)
                        mm = pe.matmul(s_bank[g][rows, :], q_maps[:, b, h, :], kcT[:, h, :], tile_position=(0, h % PER * HR))
                        if h % PER == PER - 1:
                            mm.then_inc(*sc.by())
                        if h == PER - 1 and between is not None:
                            mix_maps(between)

                def turn_probs(b):
                    pe.wait_ge(*p_done.at(4 * (b + 1)))
                    if b > 0:
                        pe.wait_ge(*o_scaled.at(b))
                        pe.wait_ge(*o_done.at(b))
                    for g in range(GROUPS):
                        for j in range(KT):
                            pe.transpose(pT_bank[g][:, j * P:(j + 1) * P], p[:, g, j * P:(j + 1) * P], ident)
                        mm = pe.transpose(pT_new_bank[:, g * P:(g + 1) * P], p_new[:, g, b, :], ident)
                        mm.then_inc(*pT_psum.by())

                def values(b):
                    pe.wait_ge(*pT_act.at(2 * (b + 1)))
                    pe.wait_ge(*pT_dve.at(b + 1))
                    pe.wait_ge(*vc_in[b % 3].at(16 * (b // 3)))
                    for h in range(DH):
                        g, rows, e = h // PER, slice(h % PER * HR, (h % PER + 1) * HR), slice(h * P, (h + 1) * P)
                        for j in range(KT + 1):
                            v = vc[:, b % 3, j, e] if j < KT else v_tok[:, 2, e]
                            mm = pe.matmul(o_bank[rows, g * P:(g + 1) * P], pT[:, g, j, rows], v, start=(j == 0), stop=(j == KT),
                                           tile_position=(0, h % PER * HR))
                    mm.then_inc(*o_psum.by())

                def mix_maps(b):
                    pe.wait_ge(*o_scaled.at(b + 1))
                    for g in range(GROUPS):
                        mm = pe.matmul(oT_bank[:, g * DD:(g + 1) * DD], o_rows[:, g, :], core.const("sum_maps"))
                    mm.then_inc(*oT_psum.by())

                key_transposes(0)
                pe.wait_ge(*q_done.at(1))
                for b in range(DEC_BATCH):
                    scores(b, b - 2 if b >= 2 else None)
                    if b > 0:
                        turn_probs(b - 1)
                    if b + 1 < DEC_BATCH:
                        key_transposes(b + 1)
                    if b > 0:
                        values(b - 1)
                last = DEC_BATCH - 1
                mix_maps(last - 1)
                turn_probs(last)
                values(last)
                mix_maps(last)

            @block.scalar
            def _(act):
                def keys(b):
                    for n in range(b * DH, (b + 1) * DH, 2):
                        act.wait_ge(*kt_psum.at(n + 1))
                        if b > 0:
                            act.wait_ge(*sc.at(3 * b))
                        act.copy(kcT[:, n % DH, :], bank[0][:]).then_inc(*kt_act.by())

                def probs_turned(b):
                    act.wait_ge(*pT_psum.at(2 * b + 2))
                    if b > 0:
                        act.wait_ge(*o_psum.at(b))
                    act.copy(pT[:, 0, 0:KT, :].rearrange("p j r -> p (j r)"), pT_bank[0][:]).then_inc(*pT_act.by())
                    act.copy(pT[:, :, KT, :], pT_new_bank[:, 0:2 * P].rearrange("p (g r) -> p g r", g=GROUPS)).then_inc(*pT_act.by())

                keys(0)
                act.wait_ge(*zeros.at(2))
                for b in range(DEC_BATCH):
                    if b > 0:
                        probs_turned(b - 1)
                    if b + 1 < DEC_BATCH:
                        keys(b + 1)
                    act.wait_ge(*low_done.at(b + 1))
                    if b > 0:
                        act.wait_ge(*pT_psum.at(2 * b))
                    for g in range(GROUPS):
                        act.activation(p[:, g, :], s_bank[g][:], ACT.Exp, bias=low[:, g:g + 1], scale=SCALE,
                                       accum_out=tot[:, 0, g:g + 1]).then_inc(*p_done.by())
                        act.activation(p_new[:, g, b, b * DEC_SEQ:(b + 1) * DEC_SEQ], new_bank[:, g * DEC_SEQ:(g + 1) * DEC_SEQ], ACT.Exp,
                                       bias=low[:, g:g + 1], scale=SCALE, accum_out=tot[:, 1, g:g + 1]).then_inc(*p_done.by())
                probs_turned(DEC_BATCH - 1)

            @block.vector
            def _(dve):
                own = in_order(dve, dve_steps)

                def keys(b):
                    for n in range(b * DH + 1, (b + 1) * DH, 2):
                        dve.wait_ge(*kt_psum.at(n + 1))
                        if b > 0:
                            dve.wait_ge(*sc.at(3 * b))
                        dve.tensor_copy(kcT[:, n % DH, :], bank[1][:]).then_inc(*kt_dve.by())

                def probs_turned(b):
                    dve.wait_ge(*pT_psum.at(2 * b + 2))
                    if b > 0:
                        dve.wait_ge(*o_psum.at(b))
                    dve.tensor_copy(pT[:, 1, 0:KT, :].rearrange("p j r -> p (j r)"), pT_bank[1][:]).then_inc(*pT_dve.by())

                def scale_rows(b):
                    dve.wait_ge(*o_psum.at(b + 1))
                    if b > 0:
                        dve.wait_ge(*oT_psum.at(b))
                    for g in range(GROUPS):
                        ins = dve.tensor_scalar(o_rows[:, g, :], o_bank[:, g * P:(g + 1) * P], row_w[:, g:g + 1], None, ALU.mult)
                    own(ins)
                    dve.sem_inc(*o_scaled.by())

                def row_weights(b):
                    dve.wait_ge(*p_done.at(4 * (b + 1)))
                    own(dve.tensor_tensor(row_w[:], tot[:, 0, :], tot[:, 1, :], ALU.add))
                    own(dve.reciprocal(row_w[:], row_w[:]))
                    own(dve.tensor_scalar(row_w[:], row_w[:], map_w[:, 0:1], None, ALU.mult))

                def copy_out(b):
                    dve.wait_ge(*oT_psum.at(b + 1))
                    dve.tensor_copy(oT[:, :, SEQ + b * DEC_SEQ:SEQ + (b + 1) * DEC_SEQ],
                                    oT_bank[:, 0:P].rearrange("p (h q) -> p h q", h=DH)).then_inc(*o_done.by())

                own(dve.scalar_tensor_tensor(map_w[:], core.const("map1"), neg_lam[:, 0:1], core.const("map0"), ALU.mult, ALU.add))
                dve.wait_ge(*zeros.at(1))
                for c in range(2):
                    rows = slice(c * DD, (c + 1) * DD)
                    for h in range(DH):
                        ins = dve.tensor_copy(q_maps[rows, :, h, c * DEC_SEQ:(c + 1) * DEC_SEQ],
                                               qT[rows, h, SEQ:TOK].rearrange("p (b s) -> p b s", s=DEC_SEQ))
                ins.then_inc(*q_done.by())
                keys(0)
                for b in range(DEC_BATCH):
                    dve.wait_ge(*sc.at(3 * b + 1))
                    dve.tensor_reduce(top[:, 1, :], new_bank[:, 0:GROUPS * DEC_SEQ].rearrange("p (g k) -> p g k", g=GROUPS), AX.X, ALU.max)
                    dve.wait_ge(*sc.at(3 * b + 2))
                    dve.tensor_reduce(top[:, 0, 0:1], s_bank[0][:], AX.X, ALU.max)
                    if b >= 2:
                        copy_out(b - 2)
                    dve.wait_ge(*sc.at(3 * b + 3))
                    if b > 0:
                        probs_turned(b - 1)
                    if b + 1 < DEC_BATCH:
                        keys(b + 1)
                    own(dve.tensor_reduce(top[:, 0, 1:2], s_bank[1][:], AX.X, ALU.max))
                    own(dve.tensor_tensor(low[:], top[:, 0, :], top[:, 1, :], ALU.max))
                    own(dve.tensor_scalar(low[:], low[:], -SCALE, None, ALU.mult))
                    dve.sem_inc(*low_done.by())
                    if b > 0:
                        scale_rows(b - 1)
                    row_weights(b)
                last = DEC_BATCH - 1
                copy_out(last - 1)
                probs_turned(last)
                scale_rows(last)
                copy_out(last)
        core.end_stage()


def head_norm(core, io, oT):
    nc = core.nc
    flat = oT[:].rearrange("p h t -> p (h t)")
    BLOCKS = DH * TOK // P
    COLS = DH * TOK // HALF
    PER = HALF // P
    with ExitStack() as ctx:
        def sb(name, shape, dt=F32):
            return ctx.enter_context(nc.sbuf_tensor("hn_" + name, shape, dt))

        sq, diag = sb("sq", [P, DH * TOK]), sb("diag", [P, BLOCKS, P])
        root, ones, gain = sb("root", [P, BLOCKS]), sb("ones", [P, P]), sb("gain", [P, 1])
        sums = ctx.enter_context(nc.psum_tensor("hn_sums", [P, HALF], F32))
        bank = [ctx.enter_context(nc.psum_tensor(f"hn_b{i}", [P, HALF], F32)) for i in range(COLS)]
        hn_in, hn_sq, hn_sum, hn_inv, hn_root = (core.sig(n) for n in ("vectors_in", "squares", "rows_psum", "inverses", "rows_copied"))
        hn_diag, hn_wide, dve_steps = core.sig("diag_done"), core.sig("heads_psum"), core.sig("dve_steps")
        with nc.Block() as block:
            @block.sync
            def _(sp):
                sp.dma_start(gain[:], io["diff_subln_g"].rearrange("a (p e) -> (a p) e", e=1)).then_inc(*hn_in.by(16))

            @block.tensor
            def _(pe):
                for n in range(BLOCKS):
                    if n % PER == 0:
                        pe.wait_ge(*hn_sq.at(n // PER + 1))
                    mm = pe.matmul(sums[:, n:n + 1], sq[:, n * P:(n + 1) * P], ones[:, 0:1])
                mm.then_inc(*hn_sum.by())
                for n in range(BLOCKS):
                    if n % PER == 0:
                        pe.wait_ge(*hn_diag.at(n // PER + 1))
                    mm = pe.matmul(bank[n // PER][:, n % PER * P:(n % PER + 1) * P], ones[:], diag[:, n, :])
                    if n % PER == PER - 1:
                        mm.then_inc(*hn_wide.by())

            @block.scalar
            def _(act):
                act.wait_ge(*hn_inv.at(1))
                act.activation(root[:], root[:], ACT.Sqrt).then_inc(*hn_root.by())

            @block.vector
            def _(dve):
                own = in_order(dve, dve_steps)
                own(dve.memset(ones[:], 1.0))
                for i in range(COLS):
                    cols = slice(i * HALF, (i + 1) * HALF)
                    dve.tensor_tensor(sq[:, cols], flat[:, cols], flat[:, cols], ALU.mult).then_inc(*hn_sq.by())
                dve.wait_ge(*hn_in.at(16))
                own(dve.tensor_scalar(gain[:], gain[:], 1.0 - LAM_INIT, None, ALU.mult))
                dve.wait_ge(*hn_sum.at(1))
                own(dve.tensor_scalar(root[:], sums[:, 0:BLOCKS], 1.0 / P, SUBLN_EPS, ALU.mult, ALU.add))
                own(dve.reciprocal(root[:], root[:]))
                dve.sem_inc(*hn_inv.by())
                dve.wait_ge(*hn_root.at(1))
                for n in range(BLOCKS):
                    ins = dve.tensor_scalar(diag[:, n, :], core.const("ident"), root[:, n:n + 1], None, ALU.mult)
                    if n % PER == PER - 1:
                        ins.then_inc(*hn_diag.by())
                for i in range(COLS):
                    cols = slice(i * HALF, (i + 1) * HALF)
                    dve.wait_ge(*hn_wide.at(i + 1))
                    own(dve.scalar_tensor_tensor(flat[:, cols], flat[:, cols], gain[:, 0:1], bank[i][:], ALU.mult, ALU.mult))
        core.end_stage()


def attention(core, io):
    nc = core.nc
    with ExitStack() as ctx:
        def sb(name, shape, dt=F32):
            return ctx.enter_context(nc.sbuf_tensor("at_" + name, shape, dt))

        oT, qT, kT = (sb(n, [P, DH, TOK]) for n in ("oT", "qT", "kT"))
        v_tok, neg_lam = sb("v", [P, TILES, D]), sb("neg_lam", [P, 1])
        mixing_weight(core, io, neg_lam)
        with ExitStack() as proj:
            tok = {n: proj.enter_context(nc.sbuf_tensor("at_tok_" + n, [P, TILES, D], F32)) for n in "kq"}
            tok["v"] = v_tok
            xT = proj.enter_context(nc.sbuf_tensor("at_xT", [P, KD, TOK], F32))
            to_features(core, core.x_tok, xT, "at_x")
            attention_projections(core, io, xT, tok)
            to_features(core, tok["k"], kT, "at_k")
            to_features(core, tok["q"], qT, "at_q")
        with ExitStack() as cached:
            cache = Cache(core, io, cached)
            prompt_attention(core, cache, qT, kT, v_tok, oT, neg_lam)
            sample_attention(core, cache, qT, kT, v_tok, oT, neg_lam)
        head_norm(core, io, oT)
        project_and_norm(core, io, oT, io["diff_w_o"][0], 1, "attention")


def store_rows(core, io):
    y_out = core.sig("y_out")
    with core.nc.Block() as block:
        @block.sync
        def _(sp):
            for t in range(TILES):
                sp.dma_start(row_tile(io["y_prompt"], io["y_sample"], t), core.x_tok[:, t, :]).then_inc(*y_out.by(16))
            sp.wait_ge(*y_out.at(16 * TILES))
    core.end_stage()


INS = ["x_prompt", "x_sample", "state_wkv", "state_shift", "cache_k", "cache_v",
       "rwkv_mu", "rwkv_w_rkv", "rwkv_w0", "rwkv_w1", "rwkv_w2", "rwkv_a0", "rwkv_a1", "rwkv_a2",
       "rwkv_g1", "rwkv_g2", "rwkv_k_k", "rwkv_k_a", "rwkv_r_k", "rwkv_lnx_g", "rwkv_lnx_b", "rwkv_w_out",
       "w_kv", "diff_w_q", "diff_lambda", "diff_subln_g", "diff_w_o",
       "ln_mix_g", "ln_mix_b", "ln_ffn_g", "ln_ffn_b",
       "peer_w_query", "peer_sub_keys", "peer_u", "peer_v"]
OUTS = {"y_prompt": (1, SEQ, D), "y_sample": (DEC_BATCH, DEC_SEQ, D),
        "wkv_p": (1, 1, H, N, N), "shift_p": (1, 1, 1, D),
        "cache_k_p": (1, SEQ, DH, 2, DD), "cache_v_p": (1, SEQ, DH, 2 * DD),
        "wkv_s": (1, DEC_BATCH, H, N, N), "shift_s": (1, DEC_BATCH, 1, D),
        "cache_k_s": (DEC_BATCH, DEC_SEQ, DH, 2, DD), "cache_v_s": (DEC_BATCH, DEC_SEQ, DH, 2 * DD)}


def program(nc, io, stages=99):
    with ExitStack() as ctx:
        core = Core(nc, ctx)
        core.where, width = constant_layout()
        core.constants = ctx.enter_context(nc.sbuf_tensor("constants_sb", [P, width], F32))
        core.spill = {n: nc.dram_tensor(f"spill_{n}", [TILES, P, D], F32, kind="Internal").ap() for n in "rkvwag"}
        with ExitStack() as proj:
            buf = {n: proj.enter_context(nc.sbuf_tensor(f"buf_{n}", [P, TILES, D], F32)) for n in "rkvzag"}
            rwkv_projections(core, io, buf)
        if stages == 1:
            return
        with ExitStack() as wkv:
            w = {"carry": wkv.enter_context(nc.sbuf_tensor("carry", [P, H // 2, N], F32))}
            for t in range(TILES):
                with ExitStack() as per_tile:
                    def sb(name, shape):
                        return per_tile.enter_context(nc.sbuf_tensor(f"wkv_{name}_{t}", shape, F32))

                    tile = {n: sb(n, [P, D]) for n in "rkvzag"}
                    for n, shape in {"bonus": [P, D], "y": [P, D], "Y2t": [P, H // 2, P], "Q1t": [P, H // 2, P]}.items():
                        w[n] = sb(n, shape)
                    w["natural"] = per_tile.enter_context(nc.sbuf_tensor(f"wkv_natural_{t}", [N, DEC_BATCH if t == 2 else 1, H, N], F32))
                    with ExitStack() as ops:
                        names = ["B", "B_end", "K_end", "e_end"]
                        w["G"], w["Ft"] = sb("G", [P, NCH + 1, H // 2, N]), None
                        for n in names:
                            w[n] = ops.enter_context(nc.sbuf_tensor(f"wkv_{n}_{t}", [P, D], F32))
                        wkv_operands(core, io, tile, w, t)
                        w["Ft"] = ops.enter_context(nc.sbuf_tensor(f"wkv_Ft_{t}", [P, NCH, H // 2, N], F32))
                        wkv_chunks(core, tile, w, t)
                        wkv_states_and_outputs(core, io, tile, w, t)
        if stages == 2:
            return
        core.x_tok = ctx.enter_context(nc.sbuf_tensor("x_tok", [P, TILES, D], F32))
        with ExitStack() as rwkv:
            gated = rwkv.enter_context(nc.sbuf_tensor("gated_wkv", [P, TILES, D], F32))
            mixT = rwkv.enter_context(nc.sbuf_tensor("mixT", [P, KD, TOK], F32))
            load_rows(core, io, gated)
            to_features(core, gated, mixT, "rwkv")
            project_and_norm(core, io, mixT, io["rwkv_w_out"][0], 0, "rwkv")
        if stages == 3:
            return
        peer(core, io, 0)
        if stages == 4:
            return
        attention(core, io)
        if stages == 5:
            return
        peer(core, io, 1)
        store_rows(core, io)


def peer(core, io, layer):
    with ExitStack() as ctx:
        scores = ctx.enter_context(core.nc.sbuf_tensor(f"scores_{layer}", [P, TILES, 2 * PH, PK], F32))
        xT = ctx.enter_context(core.nc.sbuf_tensor(f"peer_xT_{layer}", [P, KD, TOK], F32))
        to_features(core, core.x_tok, xT, f"peer{layer}")
        first_scores(core, io, xT, scores, layer)
        peer_experts(core, io, xT, scores, layer)


def kernel(**inputs):
    import concourse.bacc as bacc
    from concourse.bass_utils import run_bass_kernel_spmd

    nc = bacc.Bacc("TRN2", target_bir_lowering=False, num_devices=1)
    arrays, io = {}, {}
    for name in INS:
        a = np.ascontiguousarray(inputs[name])
        arrays[f"in_{name}"] = a
        io[name] = nc.dram_tensor(f"in_{name}", a.shape, F32, kind="ExternalInput").ap()
    c = shape_constants()
    arrays["in_constants"] = c
    io["constants"] = nc.dram_tensor("in_constants", c.shape, F32, kind="ExternalInput").ap()
    for name, shape in OUTS.items():
        io[name] = nc.dram_tensor(f"out_{name}", shape, F32, kind="ExternalOutput").ap()
    program(nc, io)
    r = run_bass_kernel_spmd(nc, [arrays], core_ids=[0])
    return tuple(r.results[0][f"out_{name}"] for name in OUTS)
```
